# Optimizing a Trainium2 kernel written in Bass

```python
import jax, jax.numpy as jnp
from jax import lax
import numpy as np

D_MODEL = 1024
BATCH = 1
SEQ = 512
DEPTH = 2

N_MIXERS = 2
N_POOL_LAYERS = (DEPTH + 1) // 2
N_SGU_LAYERS = DEPTH // 2
POOL_WINDOWS = (2, 4, 8, 16)
POOL_GROUPS = 4
POOL_WIDTH = D_MODEL
POOL_GROUP_DIM = POOL_WIDTH // POOL_GROUPS
SGU_CHUNK = 128
SGU_HEADS = 4
SGU_WIDTH = 2 * D_MODEL
SGU_HEAD_DIM = SGU_WIDTH // SGU_HEADS
N_EXPERTS = 64
TOP_K = 8
N_GROUPS = 8
TOPK_GROUPS = 4
EXPERT_DIM = D_MODEL // 4
SHARED_DIM = EXPERT_DIM
ROUTED_SCALE = 2.5
EXPERT_BLOCK = 128
DEEPNORM_ALPHA = (2 * DEPTH) ** 0.25
DEEPNORM_BETA = (8 * DEPTH) ** -0.25
LN_EPS = 1e-5

kernel_name = "hybrid_pool_sgu_moe_deepnorm"

def layer_norm(x, g, b):
    xf = x.astype(jnp.float32)
    mu = jnp.mean(xf, axis=-1, keepdims=True)
    xc = xf - mu
    var = jnp.mean(jnp.square(xc), axis=-1, keepdims=True)
    y = xc * lax.rsqrt(var + LN_EPS) * g.astype(jnp.float32) + b.astype(jnp.float32)
    return y.astype(x.dtype)

def pool_mixer(x, w_in, w_grp, scale, w_out):
    bsz, s, _ = x.shape
    z = (x @ w_in).astype(jnp.float32).reshape(bsz, s, POOL_GROUPS, POOL_GROUP_DIM)
    cs = jnp.cumsum(z, axis=1)
    t = jnp.arange(1, s + 1, dtype=jnp.float32)
    pooled = []
    for g, w in enumerate(POOL_WINDOWS):
        c = cs[:, :, g]
        prev = jnp.pad(c[:, : s - w], ((0, 0), (w, 0), (0, 0)))
        mean = (c - prev) / jnp.minimum(t, float(w))[None, :, None]
        pooled.append(mean - z[:, :, g])
    pooled = jnp.stack(pooled, axis=2)
    y = jnp.einsum('bsgc,gcd->bsgd', pooled, w_grp.astype(jnp.float32))
    y = y.reshape(bsz, s, POOL_WIDTH) * scale.astype(jnp.float32)
    return y.astype(x.dtype) @ w_out

def sgu_mixer(x, w_in, b_in, ln_g, ln_b, w_s, b_s, w_out):
    bsz, s, _ = x.shape
    h = jax.nn.gelu(x @ w_in + b_in)
    u, v = h[..., :SGU_WIDTH], h[..., SGU_WIDTH:]
    v = layer_norm(v, ln_g, ln_b)
    v = v.reshape(bsz, s // SGU_CHUNK, SGU_CHUNK, SGU_HEADS, SGU_HEAD_DIM)
    causal = jnp.tril(jnp.ones((SGU_CHUNK, SGU_CHUNK), dtype=w_s.dtype))
    ws = w_s * causal[None]
    sv = jnp.einsum('hij,bnjhc->bnihc', ws, v) + b_s.T[:, :, None]
    gated = u * sv.reshape(bsz, s, SGU_WIDTH)
    return gated @ w_out

def moe(x, w_router, router_bias, w_gate, w_up, w_down, sh_gate, sh_up, sh_down):
    bsz, s, d = x.shape
    n_tok = bsz * s
    xf = x.reshape(n_tok, d)
    scores = jax.nn.sigmoid((xf @ w_router).astype(jnp.float32))
    biased = scores + router_bias.astype(jnp.float32)
    grouped = biased.reshape(n_tok, N_GROUPS, N_EXPERTS // N_GROUPS)
    group_score = lax.top_k(grouped, 2)[0].sum(-1)
    _, top_groups = lax.top_k(group_score, TOPK_GROUPS)
    group_mask = jax.nn.one_hot(top_groups, N_GROUPS, dtype=jnp.float32).sum(1) > 0
    expert_mask = jnp.repeat(group_mask, N_EXPERTS // N_GROUPS, axis=1)
    masked = jnp.where(expert_mask, biased, -jnp.inf)
    _, idx = lax.top_k(masked, TOP_K)
    gate = jnp.take_along_axis(scores, idx, axis=1)
    gate = gate / jnp.sum(gate, axis=-1, keepdims=True) * ROUTED_SCALE

    n_assign = n_tok * TOP_K
    flat_e = idx.reshape(n_assign)
    flat_tok = jnp.repeat(jnp.arange(n_tok, dtype=jnp.int32), TOP_K)
    order = jnp.argsort(flat_e)
    sorted_e = flat_e[order]
    counts = jnp.bincount(flat_e, length=N_EXPERTS)
    starts = jnp.cumsum(counts) - counts
    padded = (counts + EXPERT_BLOCK - 1) // EXPERT_BLOCK * EXPERT_BLOCK
    padded_end = jnp.cumsum(padded)
    padded_start = padded_end - padded
    dest_sorted = (padded_start[sorted_e] + jnp.arange(n_assign, dtype=jnp.int32) - starts[sorted_e]).astype(jnp.int32)
    n_rows = n_assign + N_EXPERTS * EXPERT_BLOCK
    n_blocks = n_rows // EXPERT_BLOCK
    row_tok = jnp.zeros((n_rows,), jnp.int32).at[dest_sorted].set(flat_tok[order])
    block_start = jnp.arange(n_blocks, dtype=jnp.int32) * EXPERT_BLOCK
    block_e = jnp.minimum(jnp.searchsorted(padded_end, block_start, side='right'), N_EXPERTS - 1)

    def expert_block(args):
        tok, e = args
        xb = xf[tok]
        hb = jax.nn.silu(xb @ w_gate[e]) * (xb @ w_up[e])
        return hb @ w_down[e]

    rows = lax.map(expert_block, (row_tok.reshape(n_blocks, EXPERT_BLOCK), block_e))
    rows = rows.reshape(n_rows, d)
    dest = jnp.zeros((n_assign,), jnp.int32).at[order].set(dest_sorted)
    picked = rows[dest].reshape(n_tok, TOP_K, d).astype(jnp.float32)
    routed = jnp.einsum('tkd,tk->td', picked, gate)
    shared = (jax.nn.silu(xf @ sh_gate) * (xf @ sh_up)) @ sh_down
    return (routed.astype(x.dtype) + shared).reshape(bsz, s, d)

def setup_inputs(seed: int = 0) -> dict:
    key = jax.random.key(seed)
    keys = iter(jax.random.split(key, 32))

    def nrm(shape, scale):
        return jax.random.normal(next(keys), shape, jnp.float32) * scale

    beta = DEEPNORM_BETA
    return {
        "x": nrm((BATCH, SEQ, D_MODEL), 1.0),
        "pool_w_in": nrm((N_POOL_LAYERS, D_MODEL, POOL_WIDTH), D_MODEL ** -0.5),
        "pool_w_grp": nrm((N_POOL_LAYERS, POOL_GROUPS, POOL_GROUP_DIM, POOL_GROUP_DIM), POOL_GROUP_DIM ** -0.5),
        "pool_scale": 1.0 + nrm((N_POOL_LAYERS, POOL_WIDTH), 0.1),
        "pool_w_out": nrm((N_POOL_LAYERS, POOL_WIDTH, D_MODEL), beta * POOL_WIDTH ** -0.5),
        "sgu_w_in": nrm((N_SGU_LAYERS, D_MODEL, 2 * SGU_WIDTH), D_MODEL ** -0.5),
        "sgu_b_in": nrm((N_SGU_LAYERS, 2 * SGU_WIDTH), 0.02),
        "sgu_ln_g": 1.0 + nrm((N_SGU_LAYERS, SGU_WIDTH), 0.1),
        "sgu_ln_b": nrm((N_SGU_LAYERS, SGU_WIDTH), 0.02),
        "sgu_w_s": nrm((N_SGU_LAYERS, SGU_HEADS, SGU_CHUNK, SGU_CHUNK), SGU_CHUNK ** -0.5),
        "sgu_b_s": 1.0 + nrm((N_SGU_LAYERS, SGU_HEADS, SGU_CHUNK), 0.1),
        "sgu_w_out": nrm((N_SGU_LAYERS, SGU_WIDTH, D_MODEL), beta * SGU_WIDTH ** -0.5),
        "ln_mix_g": 1.0 + nrm((DEPTH, D_MODEL), 0.1),
        "ln_mix_b": nrm((DEPTH, D_MODEL), 0.02),
        "moe_w_router": nrm((DEPTH, D_MODEL, N_EXPERTS), D_MODEL ** -0.5),
        "moe_router_bias": nrm((DEPTH, N_EXPERTS), 0.01),
        "moe_w_gate": nrm((DEPTH, N_EXPERTS, D_MODEL, EXPERT_DIM), D_MODEL ** -0.5),
        "moe_w_up": nrm((DEPTH, N_EXPERTS, D_MODEL, EXPERT_DIM), D_MODEL ** -0.5),
        "moe_w_down": nrm((DEPTH, N_EXPERTS, EXPERT_DIM, D_MODEL), beta * EXPERT_DIM ** -0.5),
        "moe_sh_gate": nrm((DEPTH, D_MODEL, SHARED_DIM), D_MODEL ** -0.5),
        "moe_sh_up": nrm((DEPTH, D_MODEL, SHARED_DIM), D_MODEL ** -0.5),
        "moe_sh_down": nrm((DEPTH, SHARED_DIM, D_MODEL), beta * SHARED_DIM ** -0.5),
        "ln_ffn_g": 1.0 + nrm((DEPTH, D_MODEL), 0.1),
        "ln_ffn_b": nrm((DEPTH, D_MODEL), 0.02),
    }

def reference(x, pool_w_in, pool_w_grp, pool_scale, pool_w_out, sgu_w_in, sgu_b_in, sgu_ln_g, sgu_ln_b, sgu_w_s, sgu_b_s, sgu_w_out, ln_mix_g, ln_mix_b, moe_w_router, moe_router_bias, moe_w_gate, moe_w_up, moe_w_down, moe_sh_gate, moe_sh_up, moe_sh_down, ln_ffn_g, ln_ffn_b):
    for i in range(DEPTH):
        j = i // N_MIXERS
        if i % N_MIXERS == 0:
            mix = pool_mixer(x, pool_w_in[j], pool_w_grp[j], pool_scale[j], pool_w_out[j])
        else:
            mix = sgu_mixer(x, sgu_w_in[j], sgu_b_in[j], sgu_ln_g[j], sgu_ln_b[j], sgu_w_s[j], sgu_b_s[j], sgu_w_out[j])
        x = layer_norm(DEEPNORM_ALPHA * x + mix, ln_mix_g[i], ln_mix_b[i])
        ffn = moe(x, moe_w_router[i], moe_router_bias[i], moe_w_gate[i], moe_w_up[i], moe_w_down[i], moe_sh_gate[i], moe_sh_up[i], moe_sh_down[i])
        x = layer_norm(DEEPNORM_ALPHA * x + ffn, ln_ffn_g[i], ln_ffn_b[i])
    return x


_drawn_inputs = setup_inputs


def setup_inputs(seed=0):
    import zlib

    import numpy as np

    out = dict(_drawn_inputs(seed))
    spreads = {}
    factors = {'sgu_b_in': 3.479, 'sgu_ln_b': 4.292}
    for name, (base, spread) in spreads.items():
        noise = np.random.default_rng([zlib.crc32(name.encode()), seed]).standard_normal(out[name].shape)
        drawn = base * np.exp(spread * noise) if base else spread * noise
        out[name] = __import__('jax').numpy.asarray(drawn.astype(out[name].dtype))
    for name, factor in factors.items():
        out[name] = (out[name] * factor).astype(out[name].dtype)
    return out
```

```python
from contextlib import ExitStack

import concourse.bass as bass
from concourse import mybir

ALU = mybir.AluOpType
ACT = mybir.ActivationFunctionType
AX = mybir.AxisListType
F32 = mybir.dt.float32
U32 = mybir.dt.uint32
I32 = mybir.dt.int32

P = 128
BANK = 512
CAP = 112
RING = 12
WAYS = 4
LATE = 8192
LN_EPS = 1e-5
ROUTED_SCALE = 2.5
WINDOWS = (2, 4, 8, 16)


def count(i, r, div=1, mul=1):
    return i * (mul // div) + mul * (r // div)


def wait(eng, sem, value):
    if isinstance(value, int) and value <= 0:
        return
    eng.wait_ge(sem, value)


def hybrid_trunk(nc, x, pool_w_in, pool_w_grp, pool_scale, pool_w_out, sgu_w_in, sgu_b_in, sgu_ln_g, sgu_ln_b,
                 sgu_w_s, sgu_b_s, sgu_w_out, ln_mix_g, ln_mix_b, moe_w_router, moe_router_bias, moe_w_gate,
                 moe_w_up, moe_w_down, moe_sh_gate, moe_sh_up, moe_sh_down, ln_ffn_g, ln_ffn_b, out):
    _, S, D = x.shape
    DEPTH, E, _, F = moe_w_gate.shape
    T = S // P
    K = D // P
    J = F // P
    TOP = 8
    NG = 8
    EG = E // NG
    TOPG = 4
    SW = sgu_w_in.shape[2] // 2
    KS = SW // P
    HEADS = sgu_w_s.shape[1]
    ALPHA = (2 * DEPTH) ** 0.25
    HALF = D // 2
    PASSES = -(-S // CAP)
    assert D == 1024 and S == 512 and F == 256 and E == 64 and SW == 2048 and RING == 3 * WAYS
    UNIT = 2 * D
    MIX_UNITS = (4 + 1 + 4 + 3, 8 + 8 + 8 + 3)
    MIX_BASE = (0, MIX_UNITS[0] + 3 * E)
    MOE_BASE = (MIX_UNITS[0], MIX_BASE[1] + MIX_UNITS[1])

    x1_dram = [nc.dram_tensor(f"mixed_rows_{l}", [S, D], F32, kind="Internal").ap() for l in range(DEPTH)]
    picked_dram = [nc.dram_tensor(f"picked_rows_{l}", [S * TOP, D], F32, kind="Internal").ap() for l in range(DEPTH)]

    with ExitStack() as ctx:
        def sb(name, shape, dt=F32):
            return ctx.enter_context(nc.sbuf_tensor(name, shape, dt))

        def sem(name):
            return ctx.enter_context(nc.semaphore(name))

        ps = [ctx.enter_context(nc.psum_tensor(f"ps{i}", [P, BANK], F32)) for i in range(8)]

        ring = sb("ring", [P, RING, UNIT])
        x_tok = sb("x_tok", [P, T, D])
        xT = sb("xT", [P, K, S])
        ident = sb("ident", [P, P])
        before = sb("before", [P, P])
        ones = sb("ones", [P, P])
        lower = sb("lower", [P, NG, NG])
        tok_id = sb("tok_id", [P, T])
        tok_row = sb("tok_row", [P, T])
        wr = sb("wr", [P, DEPTH, K, E])
        rb = sb("rb", [P, DEPTH, E])
        scale_col = sb("scale_col", [P, K])
        sgu_cols = sb("sgu_cols", [P, 3, KS])
        idx = [sb(f"idx{i}", [P, 2], U32) for i in range(4)]
        gate_col = [sb(f"gate_col{i}", [P, 1]) for i in range(4)]
        eps = sb("eps", [P, 1])
        stats = sb("stats", [P, T, 4, 6])
        mv = sb("mv", [P, T, 2])
        std = sb("std", [P, T])
        rstd = sb("rstd", [P, T])
        counts_i = sb("counts_i", [P, E], I32)
        most_i = sb("most_i", [P, 1], I32)

        WORK = 18432
        work = sb("work", [P, WORK])

        def area(at, *dims):
            n = 1
            for d in dims:
                n *= d
            assert at + n <= WORK
            v = work[:, at:at + n]
            if len(dims) == 2:
                v = v.rearrange("p (a b) -> p a b", a=dims[0])
            if len(dims) == 3:
                v = v.rearrange("p (a b c) -> p a b c", a=dims[0], b=dims[1])
            return v, at + n

        gain_shift, end = area(0, 2, D)
        ZP = 16 + S
        z_pad, at = area(end, 2, ZP)
        win_a, at = area(at, ZP)
        win_b, at = area(at, ZP)
        pooled, at = area(at, K, S)
        pool_yT, at = area(at, K, S)
        edge, at = area(at, len(WINDOWS), 16)
        v_tok, at = area(0, T, SW)
        gT, at = area(at, KS, S)
        v_bias, at = area(at, 2, 256)
        wsT, at = area(at, HEADS, P)
        ws_sum, at = area(at, HEADS, P)
        bs_row, at = area(at, HEADS, P)
        ws_raw, _ = area(T * SW, HEADS, P)
        xg, at = area(end, 2, D)
        xgT, at = area(at, 2, K, CAP)
        sil, at = area(at, 2, J * CAP)
        hT, at = area(at, 2, J, CAP)
        y_sb, at = area(at, 2, D)
        onehot, at = area(at, 2, T, CAP)
        slot_no, at = area(at, CAP)
        table, at = area(at, T, E * 3)
        posm, at = area(at, T, E)
        sh_sil, at = area(at, J, S)
        sh_hT, at = area(at, J, S)
        rows, end_rows = area(at, 4, D)
        scores, r_at = area(at, T, E)
        biased, r_at = area(r_at, T, E)
        top2, r_at = area(r_at, T * NG, 8)
        gscore, r_at = area(r_at, T, NG)
        g_gt, r_at = area(r_at, T, NG, NG)
        g_eq, r_at = area(r_at, T, NG, NG)
        g_rank, r_at = area(r_at, T, NG)
        g_sel, r_at = area(r_at, T, NG)
        g_pen, r_at = area(r_at, T, NG)
        masked, r_at = area(r_at, T, E)
        top8, r_at = area(r_at, T, 8)
        taken, r_at = area(r_at, T, E)
        chosen, r_at = area(r_at, T, E)
        cum_a, r_at = area(r_at, T, E)
        cum_b, r_at = area(r_at, T, E)
        gsum, r_at = area(r_at, T)
        grec, r_at = area(r_at, T)
        most, r_at = area(r_at, 1)
        assert r_at <= end_rows

        landed = [sem(f"landed{i}") for i in range(RING)]
        consts = sem("consts")
        const_step = sem("const_step")
        small = sem("small")
        x_in = sem("x_in")
        gain_in = sem("gain_in")
        dve_step = sem("dve_step")
        act_step = sem("act_step")
        out_stored = sem("out_stored")
        carrier = sem("carrier")
        z_ps, z_sb, pooled_ok, grp_ps, grp_sb = map(sem, ("z_ps", "z_sb", "pooled_ok", "grp_ps", "grp_sb"))
        bias_in = [sem("bias_in0"), sem("bias_in1")]
        v_ps, v_add, v_sb, v_var, v_std, v_ok = map(sem, ("v_ps", "v_add", "v_sb", "v_var", "v_std", "v_ok"))
        ws_in, ws_cut, ws_ps, ws_ok, wsum_ps, wsum_ok = map(sem, ("ws_in", "ws_cut", "ws_ps", "ws_ok", "wsum_ps", "wsum_ok"))
        u_ps, u_sb, sp_ps, gated_ok = map(sem, ("u_ps", "u_sb", "sp_ps", "gated_ok"))

        names = ("mix_ps mix_res "
                 "x1_stored table_ok shg_ps sh_sil_ok sh_h_ok shy_ps base_ok "
                 "onehot_ok idx_ps idx_ok gath0 gath1 t_ps xgt_a xgt_b h_ps silu_ok h_ok y_ps ya yb scat0 scat1 "
                 "rows0 rows1 rows2 rows3 rows_used "
                 "o_w o_onehot o_idx_ps o_idx o_gath o_gathered o_t o_xgt_a o_xgt_b o_h o_silu o_hok o_y o_ya o_yb o_scat o_scattered o_done").split()
        L = [{n: sem(f"{n}_{l}") for n in names} for l in range(DEPTH)]
        logit_ps, score_ok, chosen_ok, pos_ps, slots_ok, zeroed = map(
            sem, ("logit_ps", "score_ok", "chosen_ok", "pos_ps", "slots_ok", "zeroed"))
        norm_var, norm_std, norm_done = map(sem, ("norm_var", "norm_std", "norm_done"))
        x_turned, xT_a, xT_b = map(sem, ("x_turned", "xT_a", "xT_b"))

        def landed_count(n):
            return 16 * (n // RING + 1)

        def expert_unit(l, i, r, k):
            n = MOE_BASE[l] + 3 * r + k
            return n % RING, i * 4 + landed_count(n)

        def gate_up_view(place):
            return ring[:, place, :].rearrange("p (c f) -> p c f", c=K)

        def down_view(place):
            return ring[:, place, :].rearrange("p (j d) -> p j d", j=J)

        block = ctx.enter_context(nc.Block())

        @block.sync
        def _(sp):
            for t in range(T):
                sp.dma_start(x_tok[:, t, :], x[0, t * P:(t + 1) * P, :]).then_inc(x_in, 16)

            def mixer_sources(l):
                if l == 0:
                    for u in range(4):
                        yield "w", pool_w_in[0][:, u * 256:(u + 1) * 256].rearrange("(p c) f -> p c f", c=K)
                    yield "w", pool_w_grp[0].rearrange("g (k p) d -> p (g k) d", p=P)
                    for u in range(4):
                        yield "r", pool_w_out[0][u * 256:(u + 1) * 256, :].rearrange("(k p) d -> p k d", p=P)
                else:
                    for u in list(range(8, 16)) + list(range(8)):
                        yield "w", sgu_w_in[0][:, u * 256:(u + 1) * 256].rearrange("(p c) f -> p c f", c=K)
                    for u in range(8):
                        yield "r", sgu_w_out[0][u * 256:(u + 1) * 256, :].rearrange("(k p) d -> p k d", p=P)
                yield "w", moe_sh_gate[l].rearrange("(p c) f -> p c f", c=K)
                yield "w", moe_sh_up[l].rearrange("(p c) f -> p c f", c=K)
                yield "r", moe_sh_down[l].rearrange("(p j) d -> p j d", j=J)

            def wait_mixer_unit(l, m):
                s, u = L[l], m
                if l == 0:
                    if u < 4:
                        return sp.wait_ge(z_ps, 2 * u + 2)
                    if u < 5:
                        return sp.wait_ge(grp_ps, K)
                else:
                    if u < 8:
                        return sp.wait_ge(v_ps, T * (u + 1))
                    if u < 16:
                        return sp.wait_ge(u_ps, 2 * (u - 8) + 2)
                u -= MIX_UNITS[l] - 3
                if u < 0:
                    sp.wait_ge(s["mix_ps"], 2 * T)
                elif u < 2:
                    sp.wait_ge(s["shg_ps"], u + 1)
                else:
                    sp.wait_ge(s["shy_ps"], 2 * T)

            def load_expert(l, i, r):
                e = i + r
                for k, w in enumerate((moe_w_gate, moe_w_up, moe_w_down)):
                    place, _ = expert_unit(l, 0, r, k)
                    src = w[l, bass.ds(e, 1)].rearrange("o (p c) f -> p (o c f)", p=P)
                    sp.dma_start(ring[:, place, :], src).then_inc(landed[place], 16)

            for l in range(DEPTH):
                s = L[l]
                for m, (kind, src) in enumerate(mixer_sources(l)):
                    n = MIX_BASE[l] + m
                    if m >= RING:
                        wait_mixer_unit(l, m - RING)
                    elif l > 0:
                        last = E - WAYS + m // 3
                        sp.wait_ge(L[l - 1]["h_ps"], last + 1)
                        sp.wait_ge(L[l - 1]["y_ps"], last + 1)
                    place = n % RING
                    dst = ring[:, place, :].rearrange("p (c f) -> p c f", c=K if kind == "w" else 2)
                    sp.dma_start(dst, src).then_inc(landed[place], 16)
                for r in range(WAYS):
                    for k in range(3):
                        wait_mixer_unit(l, MIX_UNITS[l] - RING + 3 * r + k)
                    load_expert(l, 0, r)
                with sp.Fori(1, E // WAYS) as body:
                    i = body * WAYS
                    for r in range(WAYS):
                        sp.wait_ge(s["h_ps"], count(i, r) - WAYS + 1)
                        sp.wait_ge(s["y_ps"], count(i, r) - WAYS + 1)
                        load_expert(l, i, r)
                sp.wait_ge(s["table_ok"], 2)
                n_most = sp.value_load(most_i[0:1, 0:1], min_val=0, max_val=S)
                with sp.If(n_most > CAP):
                    sp.wait_ge(s["y_ps"], E)
                    with sp.Fori(0, E) as e:
                        n_e = sp.value_load(counts_i[0:1, bass.ds(e, 1)], min_val=0, max_val=S)
                        with sp.If(n_e > CAP):
                            for k, w in enumerate((moe_w_gate, moe_w_up, moe_w_down)):
                                src = w[l, bass.ds(e, 1)].rearrange("o (p c) f -> p (o c f)", p=P)
                                sp.dma_start(ring[:, k, :], src).then_inc(s["o_w"], 16)
                            sp.wait_ge(s["o_y"], e * (PASSES - 1) + (PASSES - 1))
                            sp.sem_inc(carrier, 1)
                        with sp.Else():
                            sp.sem_inc(s["o_w"], 48)
                            sp.nop()
                        sp.nop()
                with sp.Else():
                    sp.nop()
            for t in range(T):
                sp.wait_ge(norm_done, (2 * DEPTH - 1) * T + t + 1)
                sp.dma_start(out[0, t * P:(t + 1) * P, :], x_tok[:, t, :]).then_inc(out_stored, 16)
            sp.wait_ge(out_stored, 16 * T)

        @block.gpsimd
        def _(pool):
            gp = nc.gpsimd
            gp.memset(ident[:, :], 0.0).then_inc(const_step, 1)
            gp.memset(before[:, :], 1.0).then_inc(const_step, 1)
            gp.memset(lower[:, :, :], 1.0).then_inc(const_step, 1)
            gp.memset(ones[:, :], 1.0).then_inc(consts, 1)
            gp.memset(eps[:, :], LN_EPS).then_inc(consts, 1)
            gp.memset(z_pad[:, :, 0:16], 0.0).then_inc(consts, 1)
            gp.memset(win_a[:, 0:16], 0.0).then_inc(consts, 1)
            gp.memset(win_b[:, 0:16], 0.0).then_inc(consts, 1)
            pool.wait_ge(const_step, 3)
            gp.affine_select(out=ident[:, :], in_=ident[:, :], compare_op=ALU.not_equal, fill=1.0, base=0,
                             pattern=[[-1, P]], channel_multiplier=1).then_inc(consts, 1)
            gp.affine_select(out=before[:, :], in_=before[:, :], compare_op=ALU.is_gt, fill=0.0, base=0,
                             pattern=[[1, P]], channel_multiplier=-1).then_inc(consts, 1)
            gp.affine_select(out=lower[:, :, :], in_=lower[:, :, :], compare_op=ALU.is_gt, fill=0.0, base=0,
                             pattern=[[1, NG], [-1, NG]], channel_multiplier=0).then_inc(consts, 1)
            gp.iota(tok_id[:, :], pattern=[[P, T]], base=-LATE, channel_multiplier=1,
                    allow_small_or_imprecise_dtypes=True).then_inc(consts, 1)
            gp.iota(tok_row[:, :], pattern=[[P * TOP, T]], base=-LATE, channel_multiplier=TOP,
                    allow_small_or_imprecise_dtypes=True).then_inc(consts, 1)
            gp.iota(edge, pattern=[[0, len(WINDOWS)], [1, 16]], base=1, channel_multiplier=0,
                    allow_small_or_imprecise_dtypes=True).then_inc(consts, 1)

            passed = pool.alloc_register("passed")
            last_token = pool.to_reg(S - 1)
            last_row = pool.to_reg(S * TOP - 1)

            def load_gain_shift(g, b):
                pool.dma_start(gain_shift[:, 0, :], g.partition_broadcast(P)).then_inc(gain_in, 16)
                pool.dma_start(gain_shift[:, 1, :], b.partition_broadcast(P)).then_inc(gain_in, 16)

            def gather(s, i, r):
                e = count(i, r)
                pool.wait_ge(s["idx_ok"], e * 2 + 2)
                wait(pool, s["t_ps"], e - 1)
                b = r % 2
                pool.sem_inc(carrier, 1)
                pool.indirect_dma_start(
                    out=xg[0:CAP, b, :], out_offset=None, in_=x1_dram[l][:, :],
                    in_offset=bass.IndirectOffsetOnAxis(ap=idx[r % 4][0:CAP, 0:1], axis=0),
                    bounds_check=last_token, oob_is_err=False).then_inc((s["gath0"], s["gath1"])[b], 16)

            def scatter(s, i, r):
                e = count(i, r)
                pool.wait_ge(s["ya"], e + 1)
                pool.wait_ge(s["yb"], e + 1)
                b = r % 2
                pool.sem_inc(carrier, 1)
                pool.indirect_dma_start(
                    out=picked_dram[l][:, :],
                    out_offset=bass.IndirectOffsetOnAxis(ap=idx[r % 4][0:CAP, 1:2], axis=0),
                    in_=y_sb[0:CAP, b, :], in_offset=None,
                    bounds_check=last_row, oob_is_err=False).then_inc((s["scat0"], s["scat1"])[b], 16)

            for l in range(DEPTH):
                s = L[l]
                if l == 0:
                    load_gain_shift(ln_mix_g[0], ln_mix_b[0])
                else:
                    pool.wait_ge(norm_done, (2 * l - 1) * T + T)
                    pool.dma_start(ws_raw, sgu_w_s[0].rearrange("h i j -> i h j")).then_inc(ws_in, 16)
                    pool.dma_start(bs_row.rearrange("p h i -> p (h i)"),
                                   sgu_b_s[0].rearrange("h i -> (h i)").partition_broadcast(P)).then_inc(ws_in, 16)
                    for u in range(8):
                        if u >= 2:
                            pool.wait_ge(v_add, T * (u - 1))
                        pool.dma_start(v_bias[:, u % 2, :], sgu_b_in[0, SW + u * 256:SW + (u + 1) * 256]
                                       .partition_broadcast(P)).then_inc(bias_in[u % 2], 16)
                        if u == 1:
                            pool.wait_ge(ws_in, 32)
                            gp.affine_select(out=ws_raw, in_=ws_raw, compare_op=ALU.is_ge, fill=0.0, base=0,
                                             pattern=[[0, HEADS], [-1, P]], channel_multiplier=1).then_inc(ws_cut, 1)
                    pool.wait_ge(sp_ps, KS)
                    load_gain_shift(ln_mix_g[l], ln_mix_b[l])
                for t in range(T):
                    pool.wait_ge(norm_done, 2 * l * T + t + 1)
                    pool.dma_start(x1_dram[l][t * P:(t + 1) * P, :], x_tok[:, t, :]).then_inc(s["x1_stored"], 16)
                load_gain_shift(ln_ffn_g[l], ln_ffn_b[l])
                gp.memset(xg[:, :, :], 0.0).then_inc(zeroed, 1)
                gp.iota(slot_no, pattern=[[1, CAP]], base=0, channel_multiplier=0,
                        allow_small_or_imprecise_dtypes=True).then_inc(slots_ok, 1)
                pool.wait_ge(zeroed, l + 1)
                pool.wait_ge(s["x1_stored"], 16 * T)
                for i in range(-3, WAYS):
                    gather(s, 0, i + 3)
                    if i >= 0:
                        scatter(s, 0, i)
                with pool.Fori(1, E // WAYS - 1) as body:
                    i = body * WAYS
                    for r in range(WAYS):
                        gather(s, i, r + 3)
                        scatter(s, i, r)
                for i in range(E - WAYS, E):
                    if i + 3 < E:
                        gather(s, 0, i + 3)
                    scatter(s, 0, i)
                n_most = pool.value_load(most_i[0:1, 0:1], min_val=0, max_val=S)
                with pool.If(n_most > CAP):
                    pool.wait_ge(s["scat0"], 8 * E)
                    pool.wait_ge(s["scat1"], 8 * E)
                    pool.reg_mov(passed, 0)
                    with pool.Fori(0, E) as e:
                        n_e = pool.value_load(counts_i[0:1, bass.ds(e, 1)], min_val=0, max_val=S)
                        with pool.If(n_e > CAP):
                            for p in range(PASSES - 1):
                                q = e * (PASSES - 1) + p
                                pool.wait_ge(s["o_idx"], q * 2 + 2)
                                pool.sem_inc(carrier, 1)
                                pool.indirect_dma_start(
                                    out=xg[0:CAP, 0, :], out_offset=None, in_=x1_dram[l][:, :],
                                    in_offset=bass.IndirectOffsetOnAxis(ap=idx[0][0:CAP, 0:1], axis=0),
                                    bounds_check=last_token, oob_is_err=False).then_inc(s["o_gath"], 16)
                                pool.reg_add(passed, passed, 16)
                                pool.wait_ge(s["o_gath"], pool.snap(passed))
                                pool.sem_inc(s["o_gathered"], 1)
                                pool.wait_ge(s["o_ya"], q + 1)
                                pool.wait_ge(s["o_yb"], q + 1)
                                pool.sem_inc(carrier, 1)
                                pool.indirect_dma_start(
                                    out=picked_dram[l][:, :],
                                    out_offset=bass.IndirectOffsetOnAxis(ap=idx[0][0:CAP, 1:2], axis=0),
                                    in_=y_sb[0:CAP, 0, :], in_offset=None,
                                    bounds_check=last_row, oob_is_err=False).then_inc(s["o_scat"], 16)
                                pool.wait_ge(s["o_scat"], pool.snap(passed))
                                pool.sem_inc(s["o_scattered"], 1)
                        with pool.Else():
                            pool.sem_inc(s["o_gathered"], PASSES - 1)
                            pool.sem_inc(s["o_scattered"], PASSES - 1)
                        pool.nop()
                with pool.Else():
                    pool.nop()
                pool.sem_inc(s["o_done"], 1)

        @block.scalar
        def _(act):
            sc = nc.scalar
            chain = [0]

            def link(ins):
                chain[0] += 1
                ins.then_inc(act_step, 1)
                act.wait_ge(act_step, chain[0])

            with nc.allow_non_contiguous_dma(reason="per-channel columns, a few hundred numbers"):
                act.dma_start(scale_col[:, :], pool_scale[0].rearrange("(k p) -> p k", p=P)).then_inc(small, 16)
                act.dma_start(sgu_cols[:, 0, :], sgu_b_in[0, 0:SW].rearrange("(k p) -> p k", p=P)).then_inc(small, 16)
                act.dma_start(sgu_cols[:, 1, :], sgu_ln_g[0].rearrange("(k p) -> p k", p=P)).then_inc(small, 16)
                act.dma_start(sgu_cols[:, 2, :], sgu_ln_b[0].rearrange("(k p) -> p k", p=P)).then_inc(small, 16)
            act.dma_start(rb[:, :, :].rearrange("p l e -> p (l e)"),
                          moe_router_bias.rearrange("l e -> (l e)").partition_broadcast(P)).then_inc(small, 16)
            for l in range(DEPTH):
                act.dma_start(wr[:, l, :, :], moe_w_router[l].rearrange("(p c) e -> p c e", c=K)).then_inc(small, 16)
            SMALL_ALL = 16 * (5 + DEPTH)

            def turn(q):
                for t in range(T):
                    act.wait_ge(x_turned, q * T + t + 1)
                    sc.activation(xT[:, 0:4, t * P:(t + 1) * P],
                                  ps[4 + 2 * (t % 2)][:, :].rearrange("p (c n) -> p c n", c=4), ACT.Copy).then_inc(xT_a, 1)

            def norm(q, tiles=range(T)):
                for t in tiles:
                    act.wait_ge(norm_var, q * T + t + 1)
                    if q == 0 and t == 0:
                        act.wait_ge(consts, 11)
                    sc.activation(std[:, t:t + 1], mv[:, t, 1:2], ACT.Sqrt, bias=eps[:, 0:1]).then_inc(norm_std, 1)

            def silu(s, i, r):
                e = count(i, r)
                act.wait_ge(s["h_ps"], e + 1)
                wait(act, s["h_ok"], e - 1)
                sc.activation(sil[:, r % 2, :], ps[r % 2][:, 0:J * CAP], ACT.Silu).then_inc(s["silu_ok"], 1)

            def xgt_half(s, i, r):
                e = count(i, r)
                act.wait_ge(s["t_ps"], e + 1)
                wait(act, s["h_ps"], e - 1)
                sc.activation(xgT[:, r % 2, 0:4, :], ps[4][:, 0:4 * CAP].rearrange("p (c n) -> p c n", c=4),
                              ACT.Copy).then_inc(s["xgt_a"], 1)

            def y_half(s, i, r):
                e = count(i, r)
                act.wait_ge(s["y_ps"], e + 1)
                act.wait_ge(s["idx_ok"], e * 2 + 2)
                wait(act, (s["scat0"], s["scat1"])[r % 2], count(i, r, 2, 16))
                sc.activation(y_sb[0:CAP, r % 2, 0:HALF], ps[2][0:CAP, :], ACT.Copy,
                              scale=gate_col[r % 4][0:CAP, 0:1]).then_inc(s["ya"], 1)

            for l in range(DEPTH):
                s = L[l]
                turn(2 * l)
                if l == 0:
                    for j in range(K):
                        act.wait_ge(z_ps, j + 1)
                        if j == 0:
                            act.wait_ge(small, SMALL_ALL)
                        if j >= 2:
                            act.wait_ge(pooled_ok, j - 1)
                        sc.activation(z_pad[:, j % 2, 16:], ps[j % 4][:, :], ACT.Copy).then_inc(z_sb, 1)
                        if j % 2 == 1 and j >= 3:
                            for jd in (j - 3, j - 2):
                                act.wait_ge(grp_ps, jd + 1)
                                sc.activation(pool_yT[:, jd, :], ps[4 + jd % 2][:, :], ACT.Copy,
                                              scale=scale_col[:, jd:jd + 1]).then_inc(grp_sb, 1)
                    for jd in (K - 2, K - 1):
                        act.wait_ge(grp_ps, jd + 1)
                        sc.activation(pool_yT[:, jd, :], ps[4 + jd % 2][:, :], ACT.Copy,
                                      scale=scale_col[:, jd:jd + 1]).then_inc(grp_sb, 1)
                else:
                    act.wait_ge(ws_ps, 1)
                    sc.activation(wsT[:, :, :], ps[6][:, :].rearrange("p (h n) -> p h n", h=HEADS), ACT.Copy).then_inc(ws_ok, 1)
                    act.wait_ge(wsum_ps, 1)
                    sc.activation(ws_sum[:, :, :], ps[7][:, :].rearrange("p (h n) -> p h n", h=HEADS), ACT.Copy).then_inc(wsum_ok, 1)
                    for u in range(8):
                        for t in range(T):
                            act.wait_ge(v_add, u * T + t + 1)
                            blk = v_tok[:, t, u * 256:(u + 1) * 256]
                            sc.activation(blk, blk, ACT.Gelu_apprx_tanh).then_inc(v_sb, 1)
                    for j in range(KS):
                        if j == 1:
                            for t in range(T):
                                act.wait_ge(v_var, t + 1)
                                sc.activation(std[:, t:t + 1], mv[:, t, 1:2], ACT.Sqrt, bias=eps[:, 0:1]).then_inc(v_std, 1)
                        act.wait_ge(u_ps, j + 1)
                        if j == 0:
                            act.wait_ge(ws_ps, 1)
                        sc.activation(gT[:, j, :], ps[4 + j % 2][:, :], ACT.Gelu_apprx_tanh,
                                      bias=sgu_cols[:, 0, j:j + 1]).then_inc(u_sb, 1)
                norm(2 * l)
                turn(2 * l + 1)
                act.wait_ge(logit_ps, l + 1)
                sc.activation(scores.rearrange("p t e -> p (t e)"), ps[6][:, 0:T * E], ACT.Sigmoid).then_inc(score_ok, 1)
                act.wait_ge(s["shg_ps"], 1)
                for j in range(J):
                    sc.activation(sh_sil[:, j, :], ps[j][:, :], ACT.Silu).then_inc(s["sh_sil_ok"], 1)
                for i in range(-3, WAYS):
                    if i >= -1:
                        silu(s, 0, i + 1)
                    if i >= -2:
                        xgt_half(s, 0, i + 2)
                    if i >= 0:
                        y_half(s, 0, i)
                with act.Fori(1, E // WAYS - 1) as body:
                    i = body * WAYS
                    for r in range(WAYS):
                        silu(s, i, r + 1)
                        xgt_half(s, i, r + 2)
                        y_half(s, i, r)
                for i in range(E - WAYS, E):
                    if i + 1 < E:
                        silu(s, 0, i + 1)
                    if i + 2 < E:
                        xgt_half(s, 0, i + 2)
                    y_half(s, 0, i)
                n_most = act.value_load(most_i[0:1, 0:1], min_val=0, max_val=S)
                with act.If(n_most > CAP):
                    with act.Fori(0, E) as e:
                        n_e = act.value_load(counts_i[0:1, bass.ds(e, 1)], min_val=0, max_val=S)
                        with act.If(n_e > CAP):
                            for p in range(PASSES - 1):
                                q = e * (PASSES - 1) + p
                                act.wait_ge(s["o_t"], q + 1)
                                sc.activation(xgT[:, 0, 0:4, :], ps[4][:, 0:4 * CAP].rearrange("p (c n) -> p c n", c=4),
                                              ACT.Copy).then_inc(s["o_xgt_a"], 1)
                                act.wait_ge(s["o_h"], q + 1)
                                sc.activation(sil[:, 0, :], ps[0][:, 0:J * CAP], ACT.Silu).then_inc(s["o_silu"], 1)
                                act.wait_ge(s["o_y"], q + 1)
                                sc.activation(y_sb[0:CAP, 0, 0:HALF], ps[2][0:CAP, :], ACT.Copy,
                                              scale=gate_col[0][0:CAP, 0:1]).then_inc(s["o_ya"], 1)
                        with act.Else():
                            act.sem_inc(s["o_xgt_a"], PASSES - 1)
                            act.sem_inc(s["o_silu"], PASSES - 1)
                            act.sem_inc(s["o_ya"], PASSES - 1)
                        act.nop()
                with act.Else():
                    act.nop()
                act.wait_ge(s["scat0"], 8 * E)
                act.wait_ge(s["scat1"], 8 * E)
                act.wait_ge(s["o_done"], 1)
                picks = picked_dram[l].rearrange("(t p k) d -> t k p d", t=T, k=TOP)
                for n in range(T * TOP):
                    if n >= 4:
                        act.wait_ge(s["rows_used"], n - 3)
                    act.dma_start(rows[:, n % 4, :], picks[n // TOP, n % TOP]).then_inc(
                        (s["rows0"], s["rows1"], s["rows2"], s["rows3"])[n % 4], 16)
                    if n % TOP == 3 and n > TOP:
                        norm(2 * l + 1, [n // TOP - 1])
                norm(2 * l + 1, [T - 1])

        @block.vector
        def _(dve):
            ve = nc.vector
            chain = [0]

            def link(ins):
                chain[0] += 1
                ins.then_inc(dve_step, 1)
                dve.wait_ge(dve_step, chain[0])

            def turn(q):
                for t in range(T):
                    dve.wait_ge(x_turned, q * T + t + 1)
                    ve.tensor_copy(xT[:, 4:8, t * P:(t + 1) * P],
                                   ps[5 + 2 * (t % 2)][:, :].rearrange("p (c n) -> p c n", c=4)).then_inc(xT_b, 1)

            def norm_stats(q, t):
                for h in range(2):
                    link(ve.bn_stats(stats[:, t, h, :], x_tok[:, t, h * HALF:(h + 1) * HALF]))
                ve.bn_aggr(mv[:, t, :], stats[:, t, 0:2, :].rearrange("p a b -> p (a b)")).then_inc(norm_var, 1)

            def norm_apply(q, t):
                dve.wait_ge(norm_std, q * T + t + 1)
                link(ve.reciprocal(rstd[:, t:t + 1], std[:, t:t + 1]))
                xt = x_tok[:, t, :]
                link(ve.tensor_scalar(xt, xt, mv[:, t, 0:1], rstd[:, t:t + 1], ALU.subtract, ALU.mult))
                if t == 0:
                    dve.wait_ge(gain_in, 32 * (q + 1))
                link(ve.tensor_tensor(xt, xt, gain_shift[:, 0, :], ALU.mult))
                ve.tensor_tensor(xt, xt, gain_shift[:, 1, :], ALU.add).then_inc(norm_done, 1)

            def onehot_of(s, i, r):
                e = count(i, r)
                wait(dve, s["idx_ps"], e - 1)
                ve.tensor_tensor(onehot[:, r % 2, :, :], slot_no.unsqueeze(1).to_broadcast([P, T, CAP]),
                                 posm[:, :, bass.ds(e, 1)].to_broadcast([P, T, CAP]), ALU.is_equal).then_inc(s["onehot_ok"], 1)

            def indices(s, i, r):
                e = count(i, r)
                dve.wait_ge(s["idx_ps"], e + 1)
                wait(dve, (s["scat0"], s["scat1"])[r % 2], count(i, r, 2, 16) - 16)
                wait(dve, s["ya"], e - 3)
                wait(dve, s["yb"], e - 3)
                ve.tensor_scalar(idx[r % 4][0:CAP, :], ps[6][0:CAP, 0:2], float(LATE), None, ALU.add).then_inc(s["idx_ok"], 1)
                ve.tensor_copy(gate_col[r % 4][0:CAP, :], ps[6][0:CAP, 2:3]).then_inc(s["idx_ok"], 1)

            def product(s, i, r):
                e = count(i, r)
                dve.wait_ge(s["silu_ok"], e + 1)
                wait(dve, s["y_ps"], e - 1)
                ve.tensor_tensor(hT[:, r % 2, :, :].rearrange("p j n -> p (j n)"), sil[:, r % 2, :],
                                 ps[r % 2][:, J * CAP:2 * J * CAP], ALU.mult).then_inc(s["h_ok"], 1)

            def xgt_half(s, i, r):
                e = count(i, r)
                dve.wait_ge(s["t_ps"], e + 1)
                wait(dve, s["h_ps"], e - 1)
                ve.tensor_copy(xgT[:, r % 2, 4:8, :],
                               ps[5][:, 0:4 * CAP].rearrange("p (c n) -> p c n", c=4)).then_inc(s["xgt_b"], 1)

            def y_half(s, i, r):
                e = count(i, r)
                dve.wait_ge(s["y_ps"], e + 1)
                wait(dve, (s["scat0"], s["scat1"])[r % 2], count(i, r, 2, 16))
                ve.tensor_scalar(y_sb[0:CAP, r % 2, HALF:D], ps[3][0:CAP, :], gate_col[r % 4][0:CAP, 0:1], None,
                                 ALU.mult).then_inc(s["yb"], 1)

            def route(l):
                s = L[l]
                dve.wait_ge(score_ok, l + 1)
                link(ve.tensor_tensor(biased, scores, rb[:, l, :].unsqueeze(1).to_broadcast([P, T, E]), ALU.add))
                for t in range(T):
                    for g in range(NG):
                        m = ve.max(top2[:, t * NG + g, :], biased[:, t, g * EG:(g + 1) * EG])
                link(m)
                link(ve.tensor_tensor(gscore.rearrange("p t g -> p (t g)"), top2[:, :, 0], top2[:, :, 1], ALU.add))
                other = gscore.unsqueeze(2).to_broadcast([P, T, NG, NG])
                own = gscore.unsqueeze(3).to_broadcast([P, T, NG, NG])
                ve.tensor_tensor(g_gt, other, own, ALU.is_gt)
                link(ve.tensor_tensor(g_eq, other, own, ALU.is_equal))
                link(ve.tensor_tensor(g_eq, g_eq, lower[:, :, :].unsqueeze(1).to_broadcast([P, T, NG, NG]), ALU.mult))
                link(ve.tensor_tensor(g_gt, g_gt, g_eq, ALU.add))
                link(ve.tensor_reduce(g_rank, g_gt, axis=AX.X, op=ALU.add))
                link(ve.tensor_scalar(g_sel, g_rank, TOPG - 0.5, None, ALU.is_lt))
                link(ve.tensor_scalar(g_pen, g_sel, -1.0, 1e30, ALU.add, ALU.mult))
                by_group = masked.rearrange("p t (g k) -> p t g k", g=NG)
                link(ve.tensor_tensor(by_group, biased.rearrange("p t (g k) -> p t g k", g=NG),
                                      g_sel.unsqueeze(3).to_broadcast([P, T, NG, EG]), ALU.mult))
                link(ve.tensor_tensor(by_group, by_group, g_pen.unsqueeze(3).to_broadcast([P, T, NG, EG]), ALU.add))
                for t in range(T):
                    m = ve.max(top8[:, t, :], masked[:, t, :])
                link(m)
                for t in range(T):
                    m = ve.match_replace(taken[:, t, :], top8[:, t, :], masked[:, t, :], -3e38)
                link(m)
                link(ve.tensor_tensor(chosen, taken, masked, ALU.not_equal))
                link(ve.tensor_tensor(scores, scores, chosen, ALU.mult))
                link(ve.tensor_reduce(gsum, scores, axis=AX.X, op=ALU.add))
                link(ve.reciprocal(grec, gsum))
                link(ve.tensor_scalar(grec, grec, ROUTED_SCALE, None, ALU.mult))
                columns = table.rearrange("p t (e k) -> p t e k", k=3)
                link(ve.tensor_tensor(columns[:, :, :, 2], scores, grec.unsqueeze(2).to_broadcast([P, T, E]), ALU.mult))
                m = ve.tensor_copy(columns[:, :, :, 0], tok_id[:, :].unsqueeze(2).to_broadcast([P, T, E]))
                m.then_inc(chosen_ok, 1)
                src, step = chosen, 1
                spare = [cum_a, cum_b]
                while step < E:
                    dst = spare[0]
                    ve.tensor_copy(dst[:, :, 0:step], src[:, :, 0:step])
                    link(ve.tensor_tensor(dst[:, :, step:], src[:, :, step:], src[:, :, 0:E - step], ALU.add))
                    src, step = dst, 2 * step
                    spare.reverse()
                dst = spare[0]
                link(ve.tensor_tensor(dst, src, chosen, ALU.subtract))
                link(ve.tensor_tensor(columns[:, :, :, 1], dst, tok_row[:, :].unsqueeze(2).to_broadcast([P, T, E]), ALU.add))

            def place_tokens(l):
                s = L[l]
                dve.wait_ge(pos_ps, l + 1)
                flat = posm.rearrange("p t e -> p (t e)")
                link(ve.scalar_tensor_tensor(out=flat, in0=ps[6][:, 0:T * E], scalar=1.0,
                                             in1=chosen.rearrange("p t e -> p (t e)"), op0=ALU.add, op1=ALU.mult))
                link(ve.tensor_scalar(flat, flat, -1.0, None, ALU.add))
                link(ve.reduce_max(most, ps[6][:, T * E:(T + 1) * E], axis=AX.X))
                ve.tensor_copy(most_i[:, :], most).then_inc(s["table_ok"], 1)
                ve.tensor_copy(counts_i[:, :], ps[6][:, T * E:(T + 1) * E]).then_inc(s["table_ok"], 1)

            dve.wait_ge(consts, 11)
            link(ve.reciprocal(edge, edge))
            for g, w in enumerate(WINDOWS):
                m = ve.tensor_scalar(edge[:, g, :], edge[:, g, :], 1.0 / w, float(w), ALU.max, ALU.mult)
            link(m)

            for l in range(DEPTH):
                s = L[l]
                turn(2 * l)
                if l == 0:
                    for j in range(K):
                        g = j // 2
                        dve.wait_ge(z_sb, j + 1)
                        z = z_pad[:, j % 2, :]
                        a, spare = z, [win_a, win_b]
                        for n in range(g + 1):
                            step, b = 1 << n, spare[n % 2]
                            link(ve.tensor_tensor(b[:, 16:], a[:, 16:], a[:, 16 - step:ZP - step], ALU.add))
                            a = b
                        link(ve.tensor_tensor(a[:, 16:32], a[:, 16:32], edge[:, g, :], ALU.mult))
                        m = ve.scalar_tensor_tensor(out=pooled[:, j, :], in0=a[:, 16:], scalar=1.0 / WINDOWS[g],
                                                    in1=z[:, 16:], op0=ALU.mult, op1=ALU.subtract)
                        m.then_inc(pooled_ok, 1)
                        dve.wait_ge(pooled_ok, j + 1)
                else:
                    for u in range(8):
                        dve.wait_ge(bias_in[u % 2], 16 * (u // 2 + 1))
                        for t in range(T):
                            dve.wait_ge(v_ps, u * T + t + 1)
                            ve.tensor_tensor(v_tok[:, t, u * 256:(u + 1) * 256], ps[t][:, 0:256], v_bias[:, u % 2, :],
                                             ALU.add).then_inc(v_add, 1)
                    for t in range(T):
                        dve.wait_ge(v_sb, 7 * T + t + 1)
                        for h in range(4):
                            link(ve.bn_stats(stats[:, t, h, :], v_tok[:, t, h * 512:(h + 1) * 512]))
                        ve.bn_aggr(mv[:, t, :], stats[:, t, :, :].rearrange("p a b -> p (a b)")).then_inc(v_var, 1)
                    for t in range(T):
                        dve.wait_ge(v_std, t + 1)
                        link(ve.reciprocal(rstd[:, t:t + 1], std[:, t:t + 1]))
                        ve.tensor_scalar(v_tok[:, t, :], v_tok[:, t, :], mv[:, t, 0:1], rstd[:, t:t + 1],
                                         ALU.subtract, ALU.mult).then_inc(v_ok, 1)
                    dve.wait_ge(wsum_ok, 1)
                    for j in range(KS):
                        h = j * HEADS // KS
                        tail = v_bias[:, j % 2, 0:P]
                        link(ve.scalar_tensor_tensor(out=tail, in0=ws_sum[:, h, :], scalar=sgu_cols[:, 2, j:j + 1],
                                                     in1=bs_row[:, h, :], op0=ALU.mult, op1=ALU.add))
                        dve.wait_ge(sp_ps, j + 1)
                        bank = ps[6 + j % 2][:, :].rearrange("p (t n) -> p t n", t=T)
                        link(ve.scalar_tensor_tensor(out=bank, in0=bank, scalar=sgu_cols[:, 1, j:j + 1],
                                                     in1=tail.unsqueeze(1).to_broadcast([P, T, P]),
                                                     op0=ALU.mult, op1=ALU.add))
                        dve.wait_ge(u_sb, j + 1)
                        m = ve.tensor_tensor(gT[:, j, :], gT[:, j, :], ps[6 + j % 2][:, :], ALU.mult)
                        m.then_inc(gated_ok, 1)
                        dve.wait_ge(gated_ok, j + 1)
                for t in range(T):
                    for h in range(2):
                        dve.wait_ge(s["mix_ps"], 2 * t + h + 1)
                        xt = x_tok[:, t, h * HALF:(h + 1) * HALF]
                        m = ve.scalar_tensor_tensor(out=xt, in0=xt, scalar=ALPHA, in1=ps[2 * (t % 2) + h][:, :],
                                                    op0=ALU.mult, op1=ALU.add)
                        m.then_inc(s["mix_res"], 1)
                    dve.wait_ge(s["mix_res"], 2 * t + 2)
                    norm_stats(2 * l, t)
                    if t > 0:
                        norm_apply(2 * l, t - 1)
                norm_apply(2 * l, T - 1)
                turn(2 * l + 1)
                route(l)
                for j in range(J):
                    dve.wait_ge(s["shg_ps"], 2)
                    dve.wait_ge(s["sh_sil_ok"], j + 1)
                    ve.tensor_tensor(sh_hT[:, j, :], sh_sil[:, j, :], ps[2 + j][:, :], ALU.mult).then_inc(s["sh_h_ok"], 1)
                place_tokens(l)
                dve.wait_ge(slots_ok, l + 1)
                dve.wait_ge(s["x1_stored"], 16 * T)
                for t in range(T):
                    for h in range(2):
                        dve.wait_ge(s["shy_ps"], 2 * t + h + 1)
                        xt = x_tok[:, t, h * HALF:(h + 1) * HALF]
                        m = ve.scalar_tensor_tensor(out=xt, in0=xt, scalar=ALPHA, in1=ps[2 * (t % 2) + h][:, :],
                                                    op0=ALU.mult, op1=ALU.add)
                        m.then_inc(s["base_ok"], 1)
                for i in range(-3, WAYS):
                    onehot_of(s, 0, i + 3)
                    indices(s, 0, i + 3)
                    if i >= -1:
                        product(s, 0, i + 1)
                    if i >= -2:
                        xgt_half(s, 0, i + 2)
                    if i >= 0:
                        y_half(s, 0, i)
                with dve.Fori(1, E // WAYS - 1) as body:
                    i = body * WAYS
                    for r in range(WAYS):
                        onehot_of(s, i, r + 3)
                        indices(s, i, r + 3)
                        product(s, i, r + 1)
                        xgt_half(s, i, r + 2)
                        y_half(s, i, r)
                for i in range(E - WAYS, E):
                    if i + 3 < E:
                        onehot_of(s, 0, i + 3)
                        indices(s, 0, i + 3)
                    if i + 1 < E:
                        product(s, 0, i + 1)
                    if i + 2 < E:
                        xgt_half(s, 0, i + 2)
                    y_half(s, 0, i)
                n_most = dve.value_load(most_i[0:1, 0:1], min_val=0, max_val=S)
                with dve.If(n_most > CAP):
                    dve.wait_ge(s["scat0"], 8 * E)
                    dve.wait_ge(s["scat1"], 8 * E)
                    dve.wait_ge(s["ya"], E)
                    with dve.Fori(0, E) as e:
                        n_e = dve.value_load(counts_i[0:1, bass.ds(e, 1)], min_val=0, max_val=S)
                        with dve.If(n_e > CAP):
                            for p in range(PASSES - 1):
                                q = e * (PASSES - 1) + p
                                ve.scalar_tensor_tensor(
                                    out=onehot[:, 0, :, :], in0=posm[:, :, bass.ds(e, 1)].to_broadcast([P, T, CAP]),
                                    scalar=-float((p + 1) * CAP),
                                    in1=slot_no.unsqueeze(1).to_broadcast([P, T, CAP]),
                                    op0=ALU.add, op1=ALU.is_equal).then_inc(s["o_onehot"], 1)
                                dve.wait_ge(s["o_idx_ps"], q + 1)
                                ve.tensor_scalar(idx[0][0:CAP, :], ps[6][0:CAP, 0:2], float(LATE), None,
                                                 ALU.add).then_inc(s["o_idx"], 1)
                                ve.tensor_copy(gate_col[0][0:CAP, :], ps[6][0:CAP, 2:3]).then_inc(s["o_idx"], 1)
                                dve.wait_ge(s["o_t"], q + 1)
                                ve.tensor_copy(xgT[:, 0, 4:8, :],
                                               ps[5][:, 0:4 * CAP].rearrange("p (c n) -> p c n", c=4)).then_inc(s["o_xgt_b"], 1)
                                dve.wait_ge(s["o_silu"], q + 1)
                                ve.tensor_tensor(hT[:, 0, :, :].rearrange("p j n -> p (j n)"), sil[:, 0, :],
                                                 ps[0][:, J * CAP:2 * J * CAP], ALU.mult).then_inc(s["o_hok"], 1)
                                dve.wait_ge(s["o_y"], q + 1)
                                dve.wait_ge(s["o_idx"], q * 2 + 2)
                                ve.tensor_scalar(y_sb[0:CAP, 0, HALF:D], ps[3][0:CAP, :], gate_col[0][0:CAP, 0:1],
                                                 None, ALU.mult).then_inc(s["o_yb"], 1)
                                dve.wait_ge(s["o_scattered"], q + 1)
                                dve.sem_inc(carrier, 1)
                        with dve.Else():
                            dve.sem_inc(s["o_onehot"], PASSES - 1)
                            dve.sem_inc(s["o_idx"], 2 * (PASSES - 1))
                            dve.sem_inc(s["o_xgt_b"], PASSES - 1)
                            dve.sem_inc(s["o_hok"], PASSES - 1)
                            dve.sem_inc(s["o_yb"], PASSES - 1)
                        dve.nop()
                with dve.Else():
                    dve.nop()
                dve.wait_ge(s["base_ok"], 2 * T)
                for t in range(T):
                    for k in range(TOP):
                        n = t * TOP + k
                        dve.wait_ge((s["rows0"], s["rows1"], s["rows2"], s["rows3"])[n % 4], 16 * (n // 4 + 1))
                        ve.tensor_tensor(x_tok[:, t, :], x_tok[:, t, :], rows[:, n % 4, :], ALU.add).then_inc(s["rows_used"], 1)
                        dve.wait_ge(s["rows_used"], n + 1)
                    norm_stats(2 * l + 1, t)
                    norm_apply(2 * l + 1, t)

        @block.tensor
        def _(pe):
            te = nc.tensor

            def turn(q):
                for t in range(T):
                    if q > 0:
                        pe.wait_ge(norm_done, (q - 1) * T + t + 1)
                    if t >= 2:
                        pe.wait_ge(xT_a, q * T + t - 1)
                        pe.wait_ge(xT_b, q * T + t - 1)
                    for c in range(K):
                        m = te.transpose(ps[4 + 2 * (t % 2) + c // 4][:, (c % 4) * P:(c % 4 + 1) * P],
                                         x_tok[:, t, bass.ds(c, P, step=K)], ident[:, :])
                    m.then_inc(x_turned, 1)
                pe.wait_ge(xT_a, q * T + T)
                pe.wait_ge(xT_b, q * T + T)

            def mixer_unit(l, m):
                n = MIX_BASE[l] + m
                pe.wait_ge(landed[n % RING], landed_count(n))
                return n % RING

            def token_list(s, i, r):
                e = count(i, r)
                pe.wait_ge(s["onehot_ok"], e + 1)
                wait(pe, s["idx_ok"], e * 2)
                for t in range(T):
                    m = te.matmul(ps[6][0:CAP, 0:3], onehot[:, r % 2, t, :], table[:, t, bass.ds(e * 3, 3)],
                                  start=(t == 0), stop=(t == T - 1))
                m.then_inc(s["idx_ps"], 1)

            def turn_rows(s, i, r):
                e = count(i, r)
                pe.wait_ge((s["gath0"], s["gath1"])[r % 2], count(i, r, 2, 16) + 16)
                wait(pe, s["xgt_a"], e)
                wait(pe, s["xgt_b"], e)
                for c in range(K):
                    m = te.transpose(ps[4 + c // 4][:, (c % 4) * CAP:(c % 4 + 1) * CAP],
                                     xg[0:CAP, r % 2, bass.ds(c, P, step=K)], ident[0:CAP, 0:CAP])
                m.then_inc(s["t_ps"], 1)

            def gate_up(s, i, r):
                e = count(i, r)
                pe.wait_ge(s["xgt_a"], e + 1)
                pe.wait_ge(s["xgt_b"], e + 1)
                wait(pe, s["h_ok"], e - 1)
                for k in range(2):
                    place, there = expert_unit(l, i, r, k)
                    pe.wait_ge(landed[place], there)
                    w = gate_up_view(place)
                    for j in range(J):
                        for c in range(K):
                            m = te.matmul(ps[r % 2][:, (k * J + j) * CAP:(k * J + j + 1) * CAP],
                                          w[:, c, bass.ds(j, P, step=J)], xgT[:, r % 2, c, :],
                                          start=(c == 0), stop=(c == K - 1))
                m.then_inc(s["h_ps"], 1)

            def down(s, i, r):
                e = count(i, r)
                place, there = expert_unit(l, i, r, 2)
                pe.wait_ge(landed[place], there)
                pe.wait_ge(s["h_ok"], e + 1)
                wait(pe, s["ya"], e)
                wait(pe, s["yb"], e)
                w = down_view(place)
                for h in range(2):
                    for j in range(J):
                        m = te.matmul(ps[2 + h][0:CAP, :], hT[:, r % 2, j, :], w[:, j, h * HALF:(h + 1) * HALF],
                                      start=(j == 0), stop=(j == J - 1))
                m.then_inc(s["y_ps"], 1)

            pe.wait_ge(consts, 11)
            for l in range(DEPTH):
                s = L[l]
                if l == 0:
                    pe.wait_ge(x_in, 16 * T)
                    turn(0)

                    def group_product(g):
                        place = MIX_BASE[0] + 4
                        if g == 0:
                            mixer_unit(0, 4)
                        w = ring[:, place, :].rearrange("p (g k d) -> p g k d", g=4, k=2)
                        pe.wait_ge(pooled_ok, 2 * g + 2)
                        for jd in range(2):
                            if 2 * g + jd >= 2:
                                pe.wait_ge(grp_sb, 2 * g + jd - 1)
                            for k in range(2):
                                m = te.matmul(ps[4 + jd][:, :], w[:, g, k, jd * P:(jd + 1) * P], pooled[:, 2 * g + k, :],
                                              start=(k == 0), stop=(k == 1))
                            m.then_inc(grp_ps, 1)

                    for j in range(K):
                        if j % 2 == 0:
                            place = mixer_unit(0, j // 2)
                        if j >= 4:
                            pe.wait_ge(z_sb, j - 3)
                        w = gate_up_view(place)
                        for c in range(K):
                            m = te.matmul(ps[j % 4][:, :], w[:, c, (j % 2) * P:(j % 2 + 1) * P], xT[:, c, :],
                                          start=(c == 0), stop=(c == K - 1))
                        m.then_inc(z_ps, 1)
                        if j % 2 == 1 and j >= 3:
                            group_product((j - 3) // 2)
                    group_product(3)
                    pe.wait_ge(z_sb, K)
                    pe.wait_ge(grp_sb, K)
                    mid, n_out, first = pool_yT, 4, 5
                else:
                    turn(2)
                    pe.wait_ge(ws_cut, 1)
                    for h in range(HEADS):
                        m = te.transpose(ps[6][:, h * P:(h + 1) * P], ws_raw[:, h, :], ident[:, :])
                    m.then_inc(ws_ps, 1)
                    pe.wait_ge(ws_ok, 1)
                    te.matmul(ps[7][:, :], ones[:, :], wsT[:, :, :].rearrange("p h n -> p (h n)"),
                              start=True, stop=True).then_inc(wsum_ps, 1)
                    for u in range(8):
                        w = gate_up_view(mixer_unit(1, u))
                        for t in range(T):
                            if u >= 1:
                                pe.wait_ge(v_add, (u - 1) * T + t + 1)
                            for c in range(K):
                                m = te.matmul(ps[t][:, 0:256], xT[:, c, t * P:(t + 1) * P], w[:, c, :],
                                              start=(c == 0), stop=(c == K - 1))
                            m.then_inc(v_ps, 1)

                    def spatial(j):
                        h = j * HEADS // KS
                        if j == 0:
                            pe.wait_ge(v_ok, T)
                            pe.wait_ge(wsum_ok, 1)
                        if j >= 2:
                            pe.wait_ge(gated_ok, j - 1)
                        for t in range(T):
                            m = te.matmul(ps[6 + j % 2][:, t * P:(t + 1) * P], v_tok[:, t, j * P:(j + 1) * P],
                                          wsT[:, h, :], start=True, stop=True)
                        m.then_inc(sp_ps, 1)

                    LAG = 4
                    for j in range(KS):
                        if j % 2 == 0:
                            w = gate_up_view(mixer_unit(1, 8 + j // 2))
                        if j >= 2:
                            pe.wait_ge(u_sb, j - 1)
                        for c in range(K):
                            m = te.matmul(ps[4 + j % 2][:, :], w[:, c, (j % 2) * P:(j % 2 + 1) * P], xT[:, c, :],
                                          start=(c == 0), stop=(c == K - 1))
                        m.then_inc(u_ps, 1)
                        if j >= LAG:
                            spatial(j - LAG)
                    for j in range(KS - LAG, KS):
                        spatial(j)
                    pe.wait_ge(gated_ok, KS)
                    mid, n_out, first = gT, 8, 16
                places = [mixer_unit(l, first + u) for u in range(n_out)]
                for t in range(T):
                    for h in range(2):
                        n = 2 * t + h
                        if n >= 4:
                            pe.wait_ge(s["mix_res"], n - 3)
                        for k in range(2 * n_out):
                            w = down_view(places[k // 2])
                            m = te.matmul(ps[2 * (t % 2) + h][:, :], mid[:, k, t * P:(t + 1) * P],
                                          w[:, k % 2, h * HALF:(h + 1) * HALF], start=(k == 0), stop=(k == 2 * n_out - 1))
                        m.then_inc(s["mix_ps"], 1)
                turn(2 * l + 1)
                if l == 0:
                    pe.wait_ge(small, 16 * (5 + DEPTH))
                for t in range(T):
                    for c in range(K):
                        m = te.matmul(ps[6][:, t * E:(t + 1) * E], xT[:, c, t * P:(t + 1) * P], wr[:, l, c, :],
                                      start=(c == 0), stop=(c == K - 1))
                m.then_inc(logit_ps, 1)
                pe.wait_ge(s["mix_res"], 2 * T)
                for k in range(2):
                    w = gate_up_view(mixer_unit(l, first + n_out + k))
                    for j in range(J):
                        for c in range(K):
                            m = te.matmul(ps[2 * k + j][:, :], w[:, c, bass.ds(j, P, step=J)], xT[:, c, :],
                                          start=(c == 0), stop=(c == K - 1))
                    m.then_inc(s["shg_ps"], 1)
                pe.wait_ge(score_ok, l + 1)
                pe.wait_ge(chosen_ok, l + 1)
                for t in range(T):
                    for b in range(t + 1):
                        te.matmul(ps[6][:, t * E:(t + 1) * E], before[:, :] if b == t else ones[:, :], chosen[:, b, :],
                                  start=(b == 0), stop=(b == t))
                for b in range(T):
                    m = te.matmul(ps[6][:, T * E:(T + 1) * E], ones[:, :], chosen[:, b, :], start=(b == 0), stop=(b == T - 1))
                m.then_inc(pos_ps, 1)
                w = down_view(mixer_unit(l, first + n_out + 2))
                pe.wait_ge(s["sh_h_ok"], J)
                for t in range(T):
                    for h in range(2):
                        n = 2 * t + h
                        if n >= 4:
                            pe.wait_ge(s["base_ok"], n - 3)
                        for j in range(J):
                            m = te.matmul(ps[2 * (t % 2) + h][:, :], sh_hT[:, j, t * P:(t + 1) * P],
                                          w[:, j, h * HALF:(h + 1) * HALF], start=(j == 0), stop=(j == J - 1))
                        m.then_inc(s["shy_ps"], 1)
                pe.wait_ge(s["table_ok"], 2)
                pe.wait_ge(s["base_ok"], 2 * T)
                for i in range(-3, WAYS):
                    if i >= -1:
                        gate_up(s, 0, i + 1)
                    token_list(s, 0, i + 3)
                    if i >= -2:
                        turn_rows(s, 0, i + 2)
                    if i >= 0:
                        down(s, 0, i)
                with pe.Fori(1, E // WAYS - 1) as body:
                    i = body * WAYS
                    for r in range(WAYS):
                        gate_up(s, i, r + 1)
                        token_list(s, i, r + 3)
                        turn_rows(s, i, r + 2)
                        down(s, i, r)
                for i in range(E - WAYS, E):
                    if i + 1 < E:
                        gate_up(s, 0, i + 1)
                    if i + 3 < E:
                        token_list(s, 0, i + 3)
                    if i + 2 < E:
                        turn_rows(s, 0, i + 2)
                    down(s, 0, i)
                n_most = pe.value_load(most_i[0:1, 0:1], min_val=0, max_val=S)
                with pe.If(n_most > CAP):
                    with pe.Fori(0, E) as e:
                        n_e = pe.value_load(counts_i[0:1, bass.ds(e, 1)], min_val=0, max_val=S)
                        with pe.If(n_e > CAP):
                            pe.wait_ge(s["o_w"], e * 48 + 48)
                            for p in range(PASSES - 1):
                                q = e * (PASSES - 1) + p
                                pe.wait_ge(s["o_onehot"], q + 1)
                                for t in range(T):
                                    m = te.matmul(ps[6][0:CAP, 0:3], onehot[:, 0, t, :], table[:, t, bass.ds(e * 3, 3)],
                                                  start=(t == 0), stop=(t == T - 1))
                                m.then_inc(s["o_idx_ps"], 1)
                                pe.wait_ge(s["o_gathered"], q + 1)
                                for c in range(K):
                                    m = te.transpose(ps[4 + c // 4][:, (c % 4) * CAP:(c % 4 + 1) * CAP],
                                                     xg[0:CAP, 0, bass.ds(c, P, step=K)], ident[0:CAP, 0:CAP])
                                m.then_inc(s["o_t"], 1)
                                pe.wait_ge(s["o_xgt_a"], q + 1)
                                pe.wait_ge(s["o_xgt_b"], q + 1)
                                for k in range(2):
                                    w = gate_up_view(k)
                                    for j in range(J):
                                        for c in range(K):
                                            m = te.matmul(ps[0][:, (k * J + j) * CAP:(k * J + j + 1) * CAP],
                                                          w[:, c, bass.ds(j, P, step=J)], xgT[:, 0, c, :],
                                                          start=(c == 0), stop=(c == K - 1))
                                m.then_inc(s["o_h"], 1)
                                pe.wait_ge(s["o_hok"], q + 1)
                                for h in range(2):
                                    for j in range(J):
                                        m = te.matmul(ps[2 + h][0:CAP, :], hT[:, 0, j, :],
                                                      down_view(2)[:, j, h * HALF:(h + 1) * HALF],
                                                      start=(j == 0), stop=(j == J - 1))
                                m.then_inc(s["o_y"], 1)
                                pe.wait_ge(s["o_ya"], q + 1)
                                pe.wait_ge(s["o_yb"], q + 1)
                        with pe.Else():
                            pe.sem_inc(s["o_idx_ps"], PASSES - 1)
                            pe.sem_inc(s["o_t"], PASSES - 1)
                            pe.sem_inc(s["o_h"], PASSES - 1)
                            pe.sem_inc(s["o_y"], PASSES - 1)
                        pe.nop()
                with pe.Else():
                    pe.nop()


_INS = ["x", "pool_w_in", "pool_w_grp", "pool_scale", "pool_w_out", "sgu_w_in", "sgu_b_in", "sgu_ln_g", "sgu_ln_b",
        "sgu_w_s", "sgu_b_s", "sgu_w_out", "ln_mix_g", "ln_mix_b", "moe_w_router", "moe_router_bias", "moe_w_gate",
        "moe_w_up", "moe_w_down", "moe_sh_gate", "moe_sh_up", "moe_sh_down", "ln_ffn_g", "ln_ffn_b"]


def kernel(**inputs):
    import numpy as _np
    import concourse.bacc as _bacc
    from concourse import mybir as _mybir
    from concourse.bass_utils import run_bass_kernel_spmd as _run

    nc = _bacc.Bacc("TRN2", target_bir_lowering=False, num_devices=1)
    arrays, args = {}, []
    for name in _INS:
        a = _np.ascontiguousarray(inputs[name])
        arrays[f"in_{name}_dram"] = a
        args.append(nc.dram_tensor(f"in_{name}_dram", a.shape, _mybir.dt.from_np(a.dtype), kind="ExternalInput").ap())
    args.append(nc.dram_tensor("out_0_dram", tuple(inputs["x"].shape), _mybir.dt.float32, kind="ExternalOutput").ap())
    hybrid_trunk(nc, *args)
    r = _run(nc, [arrays], core_ids=[0])
    return r.results[0]["out_0_dram"]
```

```python
from contextlib import ExitStack

import concourse.bass as bass
from concourse import mybir

ALU = mybir.AluOpType
ACT = mybir.ActivationFunctionType
AX = mybir.AxisListType
F32 = mybir.dt.float32
U32 = mybir.dt.uint32
I32 = mybir.dt.int32

P = 128
BANK = 512
CAP = 112
RING = 12
AHEAD = 5
ROWS = 4
WAYS = 4
LATE = 8192
LN_EPS = 1e-5
ROUTED_SCALE = 2.5
WINDOWS = (2, 4, 8, 16)


def count(i, r, div=1, mul=1):
    return i * (mul // div) + mul * (r // div)


def wait(eng, sem, value):
    if isinstance(value, int) and value <= 0:
        return
    eng.wait_ge(sem, value)


def hybrid_trunk(nc, x, pool_w_in, pool_w_grp, pool_scale, pool_w_out, sgu_w_in, sgu_b_in, sgu_ln_g, sgu_ln_b,
                 sgu_w_s, sgu_b_s, sgu_w_out, ln_mix_g, ln_mix_b, moe_w_router, moe_router_bias, moe_w_gate,
                 moe_w_up, moe_w_down, moe_sh_gate, moe_sh_up, moe_sh_down, ln_ffn_g, ln_ffn_b, out):
    _, S, D = x.shape
    DEPTH, E, _, F = moe_w_gate.shape
    T = S // P
    K = D // P
    J = F // P
    TOP = 8
    NG = 8
    EG = E // NG
    TOPG = 4
    SW = sgu_w_in.shape[2] // 2
    KS = SW // P
    HEADS = sgu_w_s.shape[1]
    ALPHA = (2 * DEPTH) ** 0.25
    HALF = D // 2
    PASSES = -(-S // CAP)
    assert D == 1024 and S == 512 and F == 256 and E == 64 and SW == 2048 and RING == 3 * WAYS
    UNIT = 2 * D
    LAST_BODY = (E - AHEAD) // WAYS
    MIX_UNITS = (4 + 1 + 4 + 3, 8 + 8 + 8 + 3)
    MIX_BASE = (0, MIX_UNITS[0] + 3 * E)
    MOE_BASE = (MIX_UNITS[0], MIX_BASE[1] + MIX_UNITS[1])

    x1_dram = [nc.dram_tensor(f"mixed_rows_{l}", [S, D], F32, kind="Internal").ap() for l in range(DEPTH)]
    picked_dram = [nc.dram_tensor(f"picked_rows_{l}", [S * TOP, D], F32, kind="Internal").ap() for l in range(DEPTH)]

    with ExitStack() as ctx:
        def sb(name, shape, dt=F32):
            return ctx.enter_context(nc.sbuf_tensor(name, shape, dt))

        def sem(name):
            return ctx.enter_context(nc.semaphore(name))

        ps = [ctx.enter_context(nc.psum_tensor(f"ps{i}", [P, BANK], F32)) for i in range(8)]

        ring = sb("ring", [P, RING, UNIT])
        x_tok = sb("x_tok", [P, T, D])
        xT = sb("xT", [P, K, S])
        ident = sb("ident", [P, P])
        before = sb("before", [P, P])
        ones = sb("ones", [P, P])
        lower = sb("lower", [P, NG, NG])
        tok_id = sb("tok_id", [P, T])
        tok_row = sb("tok_row", [P, T])
        wr = sb("wr", [P, DEPTH, K, E])
        rb = sb("rb", [P, DEPTH, E])
        scale_col = sb("scale_col", [P, K])
        sgu_cols = sb("sgu_cols", [P, 3, KS])
        token_idx = [sb(f"token_idx{i}", [P, 1], U32) for i in range(WAYS)]
        row_idx = [sb(f"row_idx{i}", [P, 1], U32) for i in range(WAYS)]
        eps = sb("eps", [P, 1])
        stats = sb("stats", [P, T, 4, 6])
        mv = sb("mv", [P, T, 2])
        std = sb("std", [P, T])
        rstd = sb("rstd", [P, T])
        counts_i = sb("counts_i", [P, E], I32)
        most_i = sb("most_i", [P, 1], I32)

        WORK = 18432
        work = sb("work", [P, WORK])

        def area(at, *dims):
            n = 1
            for d in dims:
                n *= d
            assert at + n <= WORK
            v = work[:, at:at + n]
            if len(dims) == 2:
                v = v.rearrange("p (a b) -> p a b", a=dims[0])
            if len(dims) == 3:
                v = v.rearrange("p (a b c) -> p a b c", a=dims[0], b=dims[1])
            return v, at + n

        gain_shift, end = area(0, 2, D)
        ZP = 16 + S
        z_pad, at = area(end, 2, ZP)
        win_a, at = area(at, ZP)
        win_b, at = area(at, ZP)
        pooled, at = area(at, K, S)
        pool_yT, at = area(at, K, S)
        edge, at = area(at, len(WINDOWS), 16)
        v_tok, at = area(0, T, SW)
        gT, at = area(at, KS, S)
        v_bias, at = area(at, 2, 256)
        wsT, at = area(at, HEADS, P)
        ws_sum, at = area(at, HEADS, P)
        bs_row, at = area(at, HEADS, P)
        ws_raw, _ = area(T * SW, HEADS, P)
        xg, at = area(end, WAYS, D)
        xgT, at = area(at, 2, K, CAP)
        sil, at = area(at, 2, J * CAP)
        hT, at = area(at, 2, J, CAP)
        y_at = at
        y_sb, at = area(at, WAYS, D)
        onehot, at = area(at, 2, T, CAP)
        slot_no, at = area(at, CAP)
        table, at = area(at, T, E * 3)
        posm, at = area(at, T, E)
        sh_sil, at = area(at, J, S)
        sh_hT, at = area(at, J, S)
        slots, at = area(at, E * 3)
        assert 2 * WAYS >= 2 * ROWS
        rows = [v[:, 2 * n:2 * n + 2, :].rearrange("p k d -> p (k d)") for v in (xg, y_sb) for n in range(WAYS // 2)]
        end_rows = y_at + WAYS * D
        scores, r_at = area(y_at, T, E)
        biased, r_at = area(r_at, T, E)
        top2, r_at = area(r_at, T * NG, 8)
        gscore, r_at = area(r_at, T, NG)
        g_gt, r_at = area(r_at, T, NG, NG)
        g_eq, r_at = area(r_at, T, NG, NG)
        g_rank, r_at = area(r_at, T, NG)
        g_sel, r_at = area(r_at, T, NG)
        g_pen, r_at = area(r_at, T, NG)
        masked, r_at = area(r_at, T, E)
        top8, r_at = area(r_at, T, 8)
        taken, r_at = area(r_at, T, E)
        chosen, r_at = area(r_at, T, E)
        cum_a, r_at = area(r_at, T, E)
        cum_b, r_at = area(r_at, T, E)
        gsum, r_at = area(r_at, T)
        grec, r_at = area(r_at, T)
        most, r_at = area(r_at, 1)
        assert r_at <= end_rows

        landed = [sem(f"landed{i}") for i in range(RING)]
        consts = sem("consts")
        const_step = sem("const_step")
        small = sem("small")
        rows_used = sem("rows_used")
        x_in = sem("x_in")
        gain_in = sem("gain_in")
        dve_step = sem("dve_step")
        act_step = sem("act_step")
        out_stored = sem("out_stored")
        carrier = sem("carrier")
        z_ps, z_sb, pooled_ok, grp_ps, grp_sb = map(sem, ("z_ps", "z_sb", "pooled_ok", "grp_ps", "grp_sb"))
        bias_in = [sem("bias_in0"), sem("bias_in1")]
        v_ps, v_add, v_sb, v_var, v_std, v_ok = map(sem, ("v_ps", "v_add", "v_sb", "v_var", "v_std", "v_ok"))
        ws_in, ws_cut, ws_ps, ws_ok, wsum_ps, wsum_ok = map(sem, ("ws_in", "ws_cut", "ws_ps", "ws_ok", "wsum_ps", "wsum_ok"))
        u_ps, u_sb, sp_ps, gated_ok = map(sem, ("u_ps", "u_sb", "sp_ps", "gated_ok"))

        names = ("mix_ps mix_res "
                 "x1_stored table_ok shg_ps sh_sil_ok sh_h_ok shy_ps base_ok "
                 "o_w o_onehot o_idx_ps o_idx o_gath o_gathered o_t o_xgt_a o_xgt_b o_h o_silu o_hok o_y o_ya o_yb o_scat o_scattered o_done").split()
        L = [{n: sem(f"{n}_{l}") for n in names} for l in range(DEPTH)]
        onehot_ok, idx_ps, idx_ok, t_ps, xgt_a, xgt_b, h_ps, silu_ok, h_ok, y_ps, ya, yb = map(
            sem, ("onehot_ok", "idx_ps", "idx_ok", "t_ps", "xgt_a", "xgt_b", "h_ps", "silu_ok", "h_ok", "y_ps", "ya", "yb"))
        gathered = [sem(f"gathered{i}") for i in range(WAYS)]
        scattered = [sem(f"scattered{i}") for i in range(WAYS)]
        rows_in = [sem(f"rows_in{i}") for i in range(ROWS)]
        logit_ps, score_ok, chosen_ok, pos_ps, slots_ok, zeroed = map(
            sem, ("logit_ps", "score_ok", "chosen_ok", "pos_ps", "slots_ok", "zeroed"))
        norm_var, norm_std, norm_done = map(sem, ("norm_var", "norm_std", "norm_done"))
        x_turned, xT_a, xT_b = map(sem, ("x_turned", "xT_a", "xT_b"))

        def landed_count(n):
            return 16 * (n // RING + 1)

        def expert_unit(l, i, r, k):
            n = MOE_BASE[l] + 3 * r + k
            return n % RING, i * 4 + landed_count(n)

        def nth(l, i, r):
            return count(i, r) + l * E

        def uses(l, i, r):
            return count(i, r, WAYS, 16) + 16 + l * 16 * (E // WAYS)

        def wait_scattered(eng, l):
            for b in range(WAYS):
                eng.wait_ge(scattered[b], 16 * (E // WAYS) * (l + 1))

        def gate_up_view(place):
            return ring[:, place, :].rearrange("p (c f) -> p c f", c=K)

        def down_view(place):
            return ring[:, place, :].rearrange("p (j d) -> p j d", j=J)

        block = ctx.enter_context(nc.Block())

        @block.sync
        def _(sp):
            for t in range(T):
                sp.dma_start(x_tok[:, t, :], x[0, t * P:(t + 1) * P, :]).then_inc(x_in, 16)

            def mixer_sources(l):
                if l == 0:
                    for u in range(4):
                        yield "w", pool_w_in[0][:, u * 256:(u + 1) * 256].rearrange("(p c) f -> p c f", c=K)
                    yield "w", pool_w_grp[0].rearrange("g (k p) d -> p (g k) d", p=P)
                    for u in range(4):
                        yield "r", pool_w_out[0][u * 256:(u + 1) * 256, :].rearrange("(k p) d -> p k d", p=P)
                else:
                    for u in list(range(8, 16)) + list(range(8)):
                        yield "w", sgu_w_in[0][:, u * 256:(u + 1) * 256].rearrange("(p c) f -> p c f", c=K)
                    for u in range(8):
                        yield "r", sgu_w_out[0][u * 256:(u + 1) * 256, :].rearrange("(k p) d -> p k d", p=P)
                yield "w", moe_sh_gate[l].rearrange("(p c) f -> p c f", c=K)
                yield "w", moe_sh_up[l].rearrange("(p c) f -> p c f", c=K)
                yield "r", moe_sh_down[l].rearrange("(p j) d -> p j d", j=J)

            def wait_mixer_unit(l, m):
                s, u = L[l], m
                if l == 0:
                    if u < 4:
                        return sp.wait_ge(z_ps, 2 * u + 2)
                    if u < 5:
                        return sp.wait_ge(grp_ps, K)
                else:
                    if u < 8:
                        return sp.wait_ge(v_ps, T * (u + 1))
                    if u < 16:
                        return sp.wait_ge(u_ps, 2 * (u - 8) + 2)
                u -= MIX_UNITS[l] - 3
                if u < 0:
                    sp.wait_ge(s["mix_ps"], 2 * T)
                elif u < 2:
                    sp.wait_ge(s["shg_ps"], u + 1)
                else:
                    sp.wait_ge(s["shy_ps"], 2 * T)

            def load(l, i, r, k, w):
                place, _ = expert_unit(l, 0, r, k)
                src = w[l, bass.ds(count(i, r), 1)].rearrange("o (p c) f -> p (o c f)", p=P)
                sp.dma_start(ring[:, place, :], src).then_inc(landed[place], 16)

            def load_gate_up(l, i, r):
                wait(sp, h_ps, nth(l, i, r) - WAYS + 1)
                load(l, i, r, 0, moe_w_gate)
                load(l, i, r, 1, moe_w_up)

            def load_down(l, i, r):
                wait(sp, y_ps, nth(l, i, r) - WAYS + 1)
                load(l, i, r, 2, moe_w_down)

            def load_rows(l):
                wait_scattered(sp, l)
                sp.wait_ge(L[l]["o_done"], 1)
                picks = picked_dram[l].rearrange("(t p k) d -> t p (k d)", t=T, k=TOP)
                for n in range(T * TOP // 2):
                    g = l * T * TOP // 2 + n
                    wait(sp, rows_used, (g - ROWS + 1 if n >= ROWS else 0))
                    half = n % (TOP // 2)
                    sp.dma_start(rows[n % ROWS], picks[n // (TOP // 2), :, half * 2 * D:(half + 1) * 2 * D]
                                 ).then_inc(rows_in[n % ROWS], 16)

            EARLY = 6
            for l in range(DEPTH):
                s = L[l]
                for m, (kind, src) in enumerate(mixer_sources(l)):
                    n = MIX_BASE[l] + m
                    if l > 0 and m == EARLY:
                        load_rows(l - 1)
                    if m >= RING:
                        wait_mixer_unit(l, m - RING)
                    elif l > 0:
                        sp.wait_ge(y_ps if m % 3 == 2 else h_ps, l * E - WAYS + m // 3 + 1)
                    place = n % RING
                    dst = ring[:, place, :].rearrange("p (c f) -> p c f", c=K if kind == "w" else 2)
                    sp.dma_start(dst, src).then_inc(landed[place], 16)
                for r in range(WAYS):
                    for k, w in enumerate((moe_w_gate, moe_w_up, moe_w_down)):
                        wait_mixer_unit(l, MIX_UNITS[l] - RING + 3 * r + k)
                        load(l, 0, r, k, w)
                load_gate_up(l, 0, WAYS)
                with sp.Fori(1, E // WAYS - 1) as body:
                    i = body * WAYS
                    for r in range(WAYS):
                        load_down(l, i, r)
                        load_gate_up(l, i, r + 1)
                for r in range(E - WAYS, E):
                    load_down(l, 0, r)
                    if r + 1 < E:
                        load_gate_up(l, 0, r + 1)
                sp.wait_ge(s["table_ok"], 2)
                n_most = sp.value_load(most_i[0:1, 0:1], min_val=0, max_val=S)
                with sp.If(n_most > CAP):
                    sp.wait_ge(y_ps, E * (l + 1))
                    with sp.Fori(0, E) as e:
                        n_e = sp.value_load(counts_i[0:1, bass.ds(e, 1)], min_val=0, max_val=S)
                        with sp.If(n_e > CAP):
                            for k, w in enumerate((moe_w_gate, moe_w_up, moe_w_down)):
                                src = w[l, bass.ds(e, 1)].rearrange("o (p c) f -> p (o c f)", p=P)
                                sp.dma_start(ring[:, k, :], src).then_inc(s["o_w"], 16)
                            sp.wait_ge(s["o_y"], e * (PASSES - 1) + (PASSES - 1))
                            sp.sem_inc(carrier, 1)
                        with sp.Else():
                            sp.sem_inc(s["o_w"], 48)
                            sp.nop()
                        sp.nop()
                with sp.Else():
                    sp.nop()
            load_rows(DEPTH - 1)
            for t in range(T):
                sp.wait_ge(norm_done, (2 * DEPTH - 1) * T + t + 1)
                sp.dma_start(out[0, t * P:(t + 1) * P, :], x_tok[:, t, :]).then_inc(out_stored, 16)
            sp.wait_ge(out_stored, 16 * T)

        @block.gpsimd
        def _(pool):
            gp = nc.gpsimd
            gp.memset(ident[:, :], 0.0).then_inc(const_step, 1)
            gp.memset(before[:, :], 1.0).then_inc(const_step, 1)
            gp.memset(lower[:, :, :], 1.0).then_inc(const_step, 1)
            gp.memset(ones[:, :], 1.0).then_inc(consts, 1)
            gp.memset(eps[:, :], LN_EPS).then_inc(consts, 1)
            gp.memset(z_pad[:, :, 0:16], 0.0).then_inc(consts, 1)
            gp.memset(win_a[:, 0:16], 0.0).then_inc(consts, 1)
            gp.memset(win_b[:, 0:16], 0.0).then_inc(consts, 1)
            pool.wait_ge(const_step, 3)
            gp.affine_select(out=ident[:, :], in_=ident[:, :], compare_op=ALU.not_equal, fill=1.0, base=0,
                             pattern=[[-1, P]], channel_multiplier=1).then_inc(consts, 1)
            gp.affine_select(out=before[:, :], in_=before[:, :], compare_op=ALU.is_gt, fill=0.0, base=0,
                             pattern=[[1, P]], channel_multiplier=-1).then_inc(consts, 1)
            gp.affine_select(out=lower[:, :, :], in_=lower[:, :, :], compare_op=ALU.is_gt, fill=0.0, base=0,
                             pattern=[[1, NG], [-1, NG]], channel_multiplier=0).then_inc(consts, 1)
            gp.iota(tok_id[:, :], pattern=[[P, T]], base=-LATE, channel_multiplier=1,
                    allow_small_or_imprecise_dtypes=True).then_inc(consts, 1)
            gp.iota(tok_row[:, :], pattern=[[P * TOP, T]], base=-LATE, channel_multiplier=TOP,
                    allow_small_or_imprecise_dtypes=True).then_inc(consts, 1)
            gp.iota(edge, pattern=[[0, len(WINDOWS)], [1, 16]], base=1, channel_multiplier=0,
                    allow_small_or_imprecise_dtypes=True).then_inc(consts, 1)

            passed = pool.alloc_register("passed")
            last_token = pool.to_reg(S - 1)
            last_row = pool.to_reg(S * TOP - 1)

            def load_gain_shift(g, b):
                pool.dma_start(gain_shift[:, 0, :], g.partition_broadcast(P)).then_inc(gain_in, 16)
                pool.dma_start(gain_shift[:, 1, :], b.partition_broadcast(P)).then_inc(gain_in, 16)

            def gather(l, i, r):
                g, b = nth(l, i, r), r % WAYS
                pool.wait_ge(idx_ok, g + 1)
                wait(pool, t_ps, g - WAYS + 1)
                pool.sem_inc(carrier, 1)
                pool.indirect_dma_start(
                    out=xg[0:CAP, b, :], out_offset=None, in_=x1_dram[l][:, :],
                    in_offset=bass.IndirectOffsetOnAxis(ap=token_idx[b][0:CAP, :], axis=0),
                    bounds_check=last_token, oob_is_err=False).then_inc(gathered[b], 16)

            def scatter(l, i, r):
                g, b = nth(l, i, r), r % WAYS
                pool.wait_ge(ya, g + 1)
                pool.wait_ge(yb, g + 1)
                pool.sem_inc(carrier, 1)
                pool.indirect_dma_start(
                    out=picked_dram[l][:, :],
                    out_offset=bass.IndirectOffsetOnAxis(ap=row_idx[b][0:CAP, :], axis=0),
                    in_=y_sb[0:CAP, b, :], in_offset=None,
                    bounds_check=last_row, oob_is_err=False).then_inc(scattered[b], 16)

            for l in range(DEPTH):
                s = L[l]
                if l == 0:
                    load_gain_shift(ln_mix_g[0], ln_mix_b[0])
                else:
                    pool.wait_ge(norm_done, (2 * l - 1) * T + T)
                    pool.dma_start(ws_raw, sgu_w_s[0].rearrange("h i j -> i h j")).then_inc(ws_in, 16)
                    pool.dma_start(bs_row.rearrange("p h i -> p (h i)"),
                                   sgu_b_s[0].rearrange("h i -> (h i)").partition_broadcast(P)).then_inc(ws_in, 16)
                    for u in range(8):
                        if u >= 2:
                            pool.wait_ge(v_add, T * (u - 1))
                        pool.dma_start(v_bias[:, u % 2, :], sgu_b_in[0, SW + u * 256:SW + (u + 1) * 256]
                                       .partition_broadcast(P)).then_inc(bias_in[u % 2], 16)
                        if u == 1:
                            pool.wait_ge(ws_in, 32)
                            gp.affine_select(out=ws_raw, in_=ws_raw, compare_op=ALU.is_ge, fill=0.0, base=0,
                                             pattern=[[0, HEADS], [-1, P]], channel_multiplier=1).then_inc(ws_cut, 1)
                    pool.wait_ge(sp_ps, KS)
                    load_gain_shift(ln_mix_g[l], ln_mix_b[l])
                for t in range(T):
                    pool.wait_ge(norm_done, 2 * l * T + t + 1)
                    pool.dma_start(x1_dram[l][t * P:(t + 1) * P, :], x_tok[:, t, :]).then_inc(s["x1_stored"], 16)
                load_gain_shift(ln_ffn_g[l], ln_ffn_b[l])
                gp.memset(xg[:, :, :], 0.0).then_inc(zeroed, 1)
                gp.iota(slot_no, pattern=[[1, CAP]], base=0, channel_multiplier=0,
                        allow_small_or_imprecise_dtypes=True).then_inc(slots_ok, 1)
                pool.wait_ge(zeroed, l + 1)
                pool.wait_ge(s["x1_stored"], 16 * T)
                for i in range(-AHEAD, WAYS):
                    gather(l, 0, i + AHEAD)
                    if i >= 0:
                        scatter(l, 0, i)
                with pool.Fori(1, LAST_BODY) as body:
                    i = body * WAYS
                    for r in range(WAYS):
                        gather(l, i, r + AHEAD)
                        scatter(l, i, r)
                for i in range(LAST_BODY * WAYS, E):
                    if i + AHEAD < E:
                        gather(l, 0, i + AHEAD)
                    scatter(l, 0, i)
                n_most = pool.value_load(most_i[0:1, 0:1], min_val=0, max_val=S)
                with pool.If(n_most > CAP):
                    wait_scattered(pool, l)
                    pool.reg_mov(passed, 0)
                    with pool.Fori(0, E) as e:
                        n_e = pool.value_load(counts_i[0:1, bass.ds(e, 1)], min_val=0, max_val=S)
                        with pool.If(n_e > CAP):
                            for p in range(PASSES - 1):
                                q = e * (PASSES - 1) + p
                                pool.wait_ge(s["o_idx"], q + 1)
                                pool.sem_inc(carrier, 1)
                                pool.indirect_dma_start(
                                    out=xg[0:CAP, 0, :], out_offset=None, in_=x1_dram[l][:, :],
                                    in_offset=bass.IndirectOffsetOnAxis(ap=token_idx[0][0:CAP, :], axis=0),
                                    bounds_check=last_token, oob_is_err=False).then_inc(s["o_gath"], 16)
                                pool.reg_add(passed, passed, 16)
                                pool.wait_ge(s["o_gath"], pool.snap(passed))
                                pool.sem_inc(s["o_gathered"], 1)
                                pool.wait_ge(s["o_ya"], q + 1)
                                pool.wait_ge(s["o_yb"], q + 1)
                                pool.sem_inc(carrier, 1)
                                pool.indirect_dma_start(
                                    out=picked_dram[l][:, :],
                                    out_offset=bass.IndirectOffsetOnAxis(ap=row_idx[0][0:CAP, :], axis=0),
                                    in_=y_sb[0:CAP, 0, :], in_offset=None,
                                    bounds_check=last_row, oob_is_err=False).then_inc(s["o_scat"], 16)
                                pool.wait_ge(s["o_scat"], pool.snap(passed))
                                pool.sem_inc(s["o_scattered"], 1)
                        with pool.Else():
                            pool.sem_inc(s["o_gathered"], PASSES - 1)
                            pool.sem_inc(s["o_scattered"], PASSES - 1)
                        pool.nop()
                with pool.Else():
                    pool.nop()
                pool.sem_inc(s["o_done"], 1)

        @block.scalar
        def _(act):
            sc = nc.scalar
            chain = [0]

            def link(ins):
                chain[0] += 1
                ins.then_inc(act_step, 1)
                act.wait_ge(act_step, chain[0])

            with nc.allow_non_contiguous_dma(reason="per-channel columns, a few hundred numbers"):
                act.dma_start(scale_col[:, :], pool_scale[0].rearrange("(k p) -> p k", p=P)).then_inc(small, 16)
                act.dma_start(sgu_cols[:, 0, :], sgu_b_in[0, 0:SW].rearrange("(k p) -> p k", p=P)).then_inc(small, 16)
                act.dma_start(sgu_cols[:, 1, :], sgu_ln_g[0].rearrange("(k p) -> p k", p=P)).then_inc(small, 16)
                act.dma_start(sgu_cols[:, 2, :], sgu_ln_b[0].rearrange("(k p) -> p k", p=P)).then_inc(small, 16)
            act.dma_start(rb[:, :, :].rearrange("p l e -> p (l e)"),
                          moe_router_bias.rearrange("l e -> (l e)").partition_broadcast(P)).then_inc(small, 16)
            for l in range(DEPTH):
                act.dma_start(wr[:, l, :, :], moe_w_router[l].rearrange("(p c) e -> p c e", c=K)).then_inc(small, 16)
            SMALL_ALL = 16 * (5 + DEPTH)

            def turn(q):
                for t in range(T):
                    act.wait_ge(x_turned, q * T + t + 1)
                    sc.activation(xT[:, 0:4, t * P:(t + 1) * P],
                                  ps[4 + 2 * (t % 2)][:, :].rearrange("p (c n) -> p c n", c=4), ACT.Copy).then_inc(xT_a, 1)

            def norm(q):
                for t in range(T):
                    act.wait_ge(norm_var, q * T + t + 1)
                    if q == 0 and t == 0:
                        act.wait_ge(consts, 11)
                    sc.activation(std[:, t:t + 1], mv[:, t, 1:2], ACT.Sqrt, bias=eps[:, 0:1]).then_inc(norm_std, 1)

            def silu(l, i, r):
                g = nth(l, i, r)
                act.wait_ge(h_ps, g + 1)
                wait(act, h_ok, g - 1)
                sc.activation(sil[:, r % 2, :], ps[r % 2][:, 0:J * CAP], ACT.Silu).then_inc(silu_ok, 1)

            def xgt_half(l, i, r):
                g = nth(l, i, r)
                act.wait_ge(t_ps, g + 1)
                wait(act, h_ps, g - 1)
                sc.activation(xgT[:, r % 2, 0:4, :], ps[4][:, 0:4 * CAP].rearrange("p (c n) -> p c n", c=4),
                              ACT.Copy).then_inc(xgt_a, 1)

            def y_half(l, i, r):
                g, b = nth(l, i, r), r % WAYS
                act.wait_ge(y_ps, g + 1)
                act.wait_ge(idx_ok, g + 1)
                wait(act, scattered[b], uses(l, i, r) - 16)
                act.sem_inc(carrier, 1)
                sc.activation(y_sb[0:CAP, b, 0:HALF], ps[2][0:CAP, :], ACT.Copy,
                              scale=slots[0:CAP, bass.ds(count(i, r) * 3 + 2, 1)]).then_inc(ya, 1)

            for l in range(DEPTH):
                s = L[l]
                turn(2 * l)
                if l == 0:
                    for j in range(K):
                        act.wait_ge(z_ps, j + 1)
                        if j == 0:
                            act.wait_ge(small, SMALL_ALL)
                        if j >= 2:
                            act.wait_ge(pooled_ok, j - 1)
                        sc.activation(z_pad[:, j % 2, 16:], ps[j % 4][:, :], ACT.Copy).then_inc(z_sb, 1)
                        if j % 2 == 1 and j >= 3:
                            for jd in (j - 3, j - 2):
                                act.wait_ge(grp_ps, jd + 1)
                                sc.activation(pool_yT[:, jd, :], ps[4 + jd % 2][:, :], ACT.Copy,
                                              scale=scale_col[:, jd:jd + 1]).then_inc(grp_sb, 1)
                    for jd in (K - 2, K - 1):
                        act.wait_ge(grp_ps, jd + 1)
                        sc.activation(pool_yT[:, jd, :], ps[4 + jd % 2][:, :], ACT.Copy,
                                      scale=scale_col[:, jd:jd + 1]).then_inc(grp_sb, 1)
                else:
                    act.wait_ge(ws_ps, 1)
                    sc.activation(wsT[:, :, :], ps[6][:, :].rearrange("p (h n) -> p h n", h=HEADS), ACT.Copy).then_inc(ws_ok, 1)
                    act.wait_ge(wsum_ps, 1)
                    sc.activation(ws_sum[:, :, :], ps[7][:, :].rearrange("p (h n) -> p h n", h=HEADS), ACT.Copy).then_inc(wsum_ok, 1)
                    for u in range(8):
                        for t in range(T):
                            act.wait_ge(v_add, u * T + t + 1)
                            blk = v_tok[:, t, u * 256:(u + 1) * 256]
                            sc.activation(blk, blk, ACT.Gelu_apprx_tanh).then_inc(v_sb, 1)
                    for j in range(KS):
                        if j == 1:
                            for t in range(T):
                                act.wait_ge(v_var, t + 1)
                                sc.activation(std[:, t:t + 1], mv[:, t, 1:2], ACT.Sqrt, bias=eps[:, 0:1]).then_inc(v_std, 1)
                        act.wait_ge(u_ps, j + 1)
                        if j == 0:
                            act.wait_ge(ws_ps, 1)
                        sc.activation(gT[:, j, :], ps[4 + j % 2][:, :], ACT.Gelu_apprx_tanh,
                                      bias=sgu_cols[:, 0, j:j + 1]).then_inc(u_sb, 1)
                norm(2 * l)
                turn(2 * l + 1)
                act.wait_ge(logit_ps, l + 1)
                sc.activation(scores.rearrange("p t e -> p (t e)"), ps[6][:, 0:T * E], ACT.Sigmoid).then_inc(score_ok, 1)
                act.wait_ge(s["shg_ps"], 1)
                for j in range(J):
                    sc.activation(sh_sil[:, j, :], ps[j][:, :], ACT.Silu).then_inc(s["sh_sil_ok"], 1)
                for i in range(-2, WAYS):
                    if i >= -1:
                        silu(l, 0, i + 1)
                    xgt_half(l, 0, i + 2)
                    if i >= 0:
                        y_half(l, 0, i)
                with act.Fori(1, LAST_BODY) as body:
                    i = body * WAYS
                    for r in range(WAYS):
                        silu(l, i, r + 1)
                        xgt_half(l, i, r + 2)
                        y_half(l, i, r)
                for i in range(LAST_BODY * WAYS, E):
                    if i + 1 < E:
                        silu(l, 0, i + 1)
                    if i + 2 < E:
                        xgt_half(l, 0, i + 2)
                    y_half(l, 0, i)
                n_most = act.value_load(most_i[0:1, 0:1], min_val=0, max_val=S)
                with act.If(n_most > CAP):
                    with act.Fori(0, E) as e:
                        n_e = act.value_load(counts_i[0:1, bass.ds(e, 1)], min_val=0, max_val=S)
                        with act.If(n_e > CAP):
                            for p in range(PASSES - 1):
                                q = e * (PASSES - 1) + p
                                act.wait_ge(s["o_t"], q + 1)
                                sc.activation(xgT[:, 0, 0:4, :], ps[4][:, 0:4 * CAP].rearrange("p (c n) -> p c n", c=4),
                                              ACT.Copy).then_inc(s["o_xgt_a"], 1)
                                act.wait_ge(s["o_h"], q + 1)
                                sc.activation(sil[:, 0, :], ps[0][:, 0:J * CAP], ACT.Silu).then_inc(s["o_silu"], 1)
                                act.wait_ge(s["o_y"], q + 1)
                                act.sem_inc(carrier, 1)
                                sc.activation(y_sb[0:CAP, 0, 0:HALF], ps[2][0:CAP, :], ACT.Copy,
                                              scale=slots[0:CAP, bass.ds(e * 3 + 2, 1)]).then_inc(s["o_ya"], 1)
                                act.wait_ge(s["o_ya"], q + 1)
                                act.sem_inc(carrier, 1)
                        with act.Else():
                            act.sem_inc(s["o_xgt_a"], PASSES - 1)
                            act.sem_inc(s["o_silu"], PASSES - 1)
                            act.sem_inc(s["o_ya"], PASSES - 1)
                        act.nop()
                with act.Else():
                    act.nop()
                norm(2 * l + 1)

        @block.vector
        def _(dve):
            ve = nc.vector
            chain = [0]

            def link(ins):
                chain[0] += 1
                ins.then_inc(dve_step, 1)
                dve.wait_ge(dve_step, chain[0])

            def turn(q):
                for t in range(T):
                    dve.wait_ge(x_turned, q * T + t + 1)
                    ve.tensor_copy(xT[:, 4:8, t * P:(t + 1) * P],
                                   ps[5 + 2 * (t % 2)][:, :].rearrange("p (c n) -> p c n", c=4)).then_inc(xT_b, 1)

            def norm_stats(q, t):
                for h in range(2):
                    link(ve.bn_stats(stats[:, t, h, :], x_tok[:, t, h * HALF:(h + 1) * HALF]))
                ve.bn_aggr(mv[:, t, :], stats[:, t, 0:2, :].rearrange("p a b -> p (a b)")).then_inc(norm_var, 1)

            def norm_apply(q, t):
                dve.wait_ge(norm_std, q * T + t + 1)
                link(ve.reciprocal(rstd[:, t:t + 1], std[:, t:t + 1]))
                xt = x_tok[:, t, :]
                link(ve.tensor_scalar(xt, xt, mv[:, t, 0:1], rstd[:, t:t + 1], ALU.subtract, ALU.mult))
                if t == 0:
                    dve.wait_ge(gain_in, 32 * (q + 1))
                link(ve.tensor_tensor(xt, xt, gain_shift[:, 0, :], ALU.mult))
                ve.tensor_tensor(xt, xt, gain_shift[:, 1, :], ALU.add).then_inc(norm_done, 1)

            def onehot_of(l, i, r):
                g = nth(l, i, r)
                wait(dve, idx_ps, g - 1)
                ve.tensor_tensor(onehot[:, r % 2, :, :], slot_no.unsqueeze(1).to_broadcast([P, T, CAP]),
                                 posm[:, :, bass.ds(count(i, r), 1)].to_broadcast([P, T, CAP]), ALU.is_equal
                                 ).then_inc(onehot_ok, 1)

            def indices(l, i, r):
                g = nth(l, i, r)
                dve.wait_ge(idx_ps, g + 1)
                wait(dve, t_ps, g - WAYS + 1)
                ve.tensor_scalar(token_idx[r % WAYS][0:CAP, :], ps[6][0:CAP, 0:1], float(LATE), None, ALU.add)
                ve.tensor_copy(slots[0:CAP, bass.ds(count(i, r) * 3, 3)], ps[6][0:CAP, 0:3]).then_inc(idx_ok, 1)

            def product(l, i, r):
                g = nth(l, i, r)
                dve.wait_ge(silu_ok, g + 1)
                wait(dve, y_ps, g - 1)
                ve.tensor_tensor(hT[:, r % 2, :, :].rearrange("p j n -> p (j n)"), sil[:, r % 2, :],
                                 ps[r % 2][:, J * CAP:2 * J * CAP], ALU.mult).then_inc(h_ok, 1)

            def xgt_half(l, i, r):
                g = nth(l, i, r)
                dve.wait_ge(t_ps, g + 1)
                wait(dve, h_ps, g - 1)
                ve.tensor_copy(xgT[:, r % 2, 4:8, :],
                               ps[5][:, 0:4 * CAP].rearrange("p (c n) -> p c n", c=4)).then_inc(xgt_b, 1)

            def y_half(l, i, r):
                g, e, b = nth(l, i, r), count(i, r), r % WAYS
                dve.wait_ge(idx_ok, g + 1)
                wait(dve, scattered[b], uses(l, i, r) - 16)
                ve.tensor_scalar(row_idx[b][0:CAP, :], slots[0:CAP, bass.ds(e * 3 + 1, 1)], float(LATE), None, ALU.add)
                dve.wait_ge(y_ps, g + 1)
                ve.tensor_scalar(y_sb[0:CAP, b, HALF:D], ps[3][0:CAP, :], slots[0:CAP, bass.ds(e * 3 + 2, 1)], None,
                                 ALU.mult).then_inc(yb, 1)

            def route(l):
                s = L[l]
                dve.wait_ge(score_ok, l + 1)
                link(ve.tensor_tensor(biased, scores, rb[:, l, :].unsqueeze(1).to_broadcast([P, T, E]), ALU.add))
                for t in range(T):
                    for g in range(NG):
                        m = ve.max(top2[:, t * NG + g, :], biased[:, t, g * EG:(g + 1) * EG])
                link(m)
                link(ve.tensor_tensor(gscore.rearrange("p t g -> p (t g)"), top2[:, :, 0], top2[:, :, 1], ALU.add))
                other = gscore.unsqueeze(2).to_broadcast([P, T, NG, NG])
                own = gscore.unsqueeze(3).to_broadcast([P, T, NG, NG])
                ve.tensor_tensor(g_gt, other, own, ALU.is_gt)
                link(ve.tensor_tensor(g_eq, other, own, ALU.is_equal))
                link(ve.tensor_tensor(g_eq, g_eq, lower[:, :, :].unsqueeze(1).to_broadcast([P, T, NG, NG]), ALU.mult))
                link(ve.tensor_tensor(g_gt, g_gt, g_eq, ALU.add))
                link(ve.tensor_reduce(g_rank, g_gt, axis=AX.X, op=ALU.add))
                link(ve.tensor_scalar(g_sel, g_rank, TOPG - 0.5, None, ALU.is_lt))
                link(ve.tensor_scalar(g_pen, g_sel, -1.0, 1e30, ALU.add, ALU.mult))
                by_group = masked.rearrange("p t (g k) -> p t g k", g=NG)
                link(ve.tensor_tensor(by_group, biased.rearrange("p t (g k) -> p t g k", g=NG),
                                      g_sel.unsqueeze(3).to_broadcast([P, T, NG, EG]), ALU.mult))
                link(ve.tensor_tensor(by_group, by_group, g_pen.unsqueeze(3).to_broadcast([P, T, NG, EG]), ALU.add))
                for t in range(T):
                    m = ve.max(top8[:, t, :], masked[:, t, :])
                link(m)
                for t in range(T):
                    m = ve.match_replace(taken[:, t, :], top8[:, t, :], masked[:, t, :], -3e38)
                link(m)
                link(ve.tensor_tensor(chosen, taken, masked, ALU.not_equal))
                link(ve.tensor_tensor(scores, scores, chosen, ALU.mult))
                link(ve.tensor_reduce(gsum, scores, axis=AX.X, op=ALU.add))
                link(ve.reciprocal(grec, gsum))
                link(ve.tensor_scalar(grec, grec, ROUTED_SCALE, None, ALU.mult))
                columns = table.rearrange("p t (e k) -> p t e k", k=3)
                link(ve.tensor_tensor(columns[:, :, :, 2], scores, grec.unsqueeze(2).to_broadcast([P, T, E]), ALU.mult))
                m = ve.tensor_copy(columns[:, :, :, 0], tok_id[:, :].unsqueeze(2).to_broadcast([P, T, E]))
                m.then_inc(chosen_ok, 1)
                src, step = chosen, 1
                spare = [cum_a, cum_b]
                while step < E:
                    dst = spare[0]
                    ve.tensor_copy(dst[:, :, 0:step], src[:, :, 0:step])
                    link(ve.tensor_tensor(dst[:, :, step:], src[:, :, step:], src[:, :, 0:E - step], ALU.add))
                    src, step = dst, 2 * step
                    spare.reverse()
                dst = spare[0]
                link(ve.tensor_tensor(dst, src, chosen, ALU.subtract))
                link(ve.tensor_tensor(columns[:, :, :, 1], dst, tok_row[:, :].unsqueeze(2).to_broadcast([P, T, E]), ALU.add))

            def place_tokens(l):
                s = L[l]
                dve.wait_ge(pos_ps, l + 1)
                flat = posm.rearrange("p t e -> p (t e)")
                link(ve.scalar_tensor_tensor(out=flat, in0=ps[6][:, 0:T * E], scalar=1.0,
                                             in1=chosen.rearrange("p t e -> p (t e)"), op0=ALU.add, op1=ALU.mult))
                link(ve.tensor_scalar(flat, flat, -1.0, None, ALU.add))
                link(ve.reduce_max(most, ps[6][:, T * E:(T + 1) * E], axis=AX.X))
                ve.tensor_copy(most_i[:, :], most).then_inc(s["table_ok"], 1)
                ve.tensor_copy(counts_i[:, :], ps[6][:, T * E:(T + 1) * E]).then_inc(s["table_ok"], 1)

            dve.wait_ge(consts, 11)
            link(ve.reciprocal(edge, edge))
            for g, w in enumerate(WINDOWS):
                m = ve.tensor_scalar(edge[:, g, :], edge[:, g, :], 1.0 / w, float(w), ALU.max, ALU.mult)
            link(m)

            for l in range(DEPTH):
                s = L[l]
                turn(2 * l)
                if l == 0:
                    for j in range(K):
                        g = j // 2
                        dve.wait_ge(z_sb, j + 1)
                        z = z_pad[:, j % 2, :]
                        a, spare = z, [win_a, win_b]
                        for n in range(g + 1):
                            step, b = 1 << n, spare[n % 2]
                            link(ve.tensor_tensor(b[:, 16:], a[:, 16:], a[:, 16 - step:ZP - step], ALU.add))
                            a = b
                        link(ve.tensor_tensor(a[:, 16:32], a[:, 16:32], edge[:, g, :], ALU.mult))
                        m = ve.scalar_tensor_tensor(out=pooled[:, j, :], in0=a[:, 16:], scalar=1.0 / WINDOWS[g],
                                                    in1=z[:, 16:], op0=ALU.mult, op1=ALU.subtract)
                        m.then_inc(pooled_ok, 1)
                        dve.wait_ge(pooled_ok, j + 1)
                else:
                    for u in range(8):
                        dve.wait_ge(bias_in[u % 2], 16 * (u // 2 + 1))
                        for t in range(T):
                            dve.wait_ge(v_ps, u * T + t + 1)
                            ve.tensor_tensor(v_tok[:, t, u * 256:(u + 1) * 256], ps[t][:, 0:256], v_bias[:, u % 2, :],
                                             ALU.add).then_inc(v_add, 1)
                    for t in range(T):
                        dve.wait_ge(v_sb, 7 * T + t + 1)
                        for h in range(4):
                            link(ve.bn_stats(stats[:, t, h, :], v_tok[:, t, h * 512:(h + 1) * 512]))
                        ve.bn_aggr(mv[:, t, :], stats[:, t, :, :].rearrange("p a b -> p (a b)")).then_inc(v_var, 1)
                    for t in range(T):
                        dve.wait_ge(v_std, t + 1)
                        link(ve.reciprocal(rstd[:, t:t + 1], std[:, t:t + 1]))
                        ve.tensor_scalar(v_tok[:, t, :], v_tok[:, t, :], mv[:, t, 0:1], rstd[:, t:t + 1],
                                         ALU.subtract, ALU.mult).then_inc(v_ok, 1)
                    dve.wait_ge(wsum_ok, 1)
                    for j in range(KS):
                        h = j * HEADS // KS
                        tail = v_bias[:, j % 2, 0:P]
                        link(ve.scalar_tensor_tensor(out=tail, in0=ws_sum[:, h, :], scalar=sgu_cols[:, 2, j:j + 1],
                                                     in1=bs_row[:, h, :], op0=ALU.mult, op1=ALU.add))
                        dve.wait_ge(sp_ps, j + 1)
                        bank = ps[6 + j % 2][:, :].rearrange("p (t n) -> p t n", t=T)
                        link(ve.scalar_tensor_tensor(out=bank, in0=bank, scalar=sgu_cols[:, 1, j:j + 1],
                                                     in1=tail.unsqueeze(1).to_broadcast([P, T, P]),
                                                     op0=ALU.mult, op1=ALU.add))
                        dve.wait_ge(u_sb, j + 1)
                        m = ve.tensor_tensor(gT[:, j, :], gT[:, j, :], ps[6 + j % 2][:, :], ALU.mult)
                        m.then_inc(gated_ok, 1)
                        dve.wait_ge(gated_ok, j + 1)
                for t in range(T):
                    for h in range(2):
                        dve.wait_ge(s["mix_ps"], 2 * t + h + 1)
                        xt = x_tok[:, t, h * HALF:(h + 1) * HALF]
                        m = ve.scalar_tensor_tensor(out=xt, in0=xt, scalar=ALPHA, in1=ps[2 * (t % 2) + h][:, :],
                                                    op0=ALU.mult, op1=ALU.add)
                        m.then_inc(s["mix_res"], 1)
                    dve.wait_ge(s["mix_res"], 2 * t + 2)
                    norm_stats(2 * l, t)
                    if t > 0:
                        norm_apply(2 * l, t - 1)
                norm_apply(2 * l, T - 1)
                turn(2 * l + 1)
                route(l)
                for j in range(J):
                    dve.wait_ge(s["shg_ps"], 2)
                    dve.wait_ge(s["sh_sil_ok"], j + 1)
                    ve.tensor_tensor(sh_hT[:, j, :], sh_sil[:, j, :], ps[2 + j][:, :], ALU.mult).then_inc(s["sh_h_ok"], 1)
                place_tokens(l)
                dve.wait_ge(slots_ok, l + 1)
                dve.wait_ge(s["x1_stored"], 16 * T)
                for t in range(T):
                    for h in range(2):
                        dve.wait_ge(s["shy_ps"], 2 * t + h + 1)
                        xt = x_tok[:, t, h * HALF:(h + 1) * HALF]
                        m = ve.scalar_tensor_tensor(out=xt, in0=xt, scalar=ALPHA, in1=ps[2 * (t % 2) + h][:, :],
                                                    op0=ALU.mult, op1=ALU.add)
                        m.then_inc(s["base_ok"], 1)
                for i in range(-AHEAD, WAYS):
                    onehot_of(l, 0, i + AHEAD)
                    indices(l, 0, i + AHEAD)
                    if i >= -1:
                        product(l, 0, i + 1)
                    if i >= -2:
                        xgt_half(l, 0, i + 2)
                    if i >= 0:
                        y_half(l, 0, i)
                with dve.Fori(1, LAST_BODY) as body:
                    i = body * WAYS
                    for r in range(WAYS):
                        onehot_of(l, i, r + AHEAD)
                        indices(l, i, r + AHEAD)
                        product(l, i, r + 1)
                        xgt_half(l, i, r + 2)
                        y_half(l, i, r)
                for i in range(LAST_BODY * WAYS, E):
                    if i + AHEAD < E:
                        onehot_of(l, 0, i + AHEAD)
                        indices(l, 0, i + AHEAD)
                    if i + 1 < E:
                        product(l, 0, i + 1)
                    if i + 2 < E:
                        xgt_half(l, 0, i + 2)
                    y_half(l, 0, i)
                n_most = dve.value_load(most_i[0:1, 0:1], min_val=0, max_val=S)
                with dve.If(n_most > CAP):
                    wait_scattered(dve, l)
                    dve.wait_ge(ya, E * (l + 1))
                    with dve.Fori(0, E) as e:
                        n_e = dve.value_load(counts_i[0:1, bass.ds(e, 1)], min_val=0, max_val=S)
                        with dve.If(n_e > CAP):
                            for p in range(PASSES - 1):
                                q = e * (PASSES - 1) + p
                                ve.scalar_tensor_tensor(
                                    out=onehot[:, 0, :, :], in0=posm[:, :, bass.ds(e, 1)].to_broadcast([P, T, CAP]),
                                    scalar=-float((p + 1) * CAP),
                                    in1=slot_no.unsqueeze(1).to_broadcast([P, T, CAP]),
                                    op0=ALU.add, op1=ALU.is_equal).then_inc(s["o_onehot"], 1)
                                dve.wait_ge(s["o_idx_ps"], q + 1)
                                ve.tensor_scalar(token_idx[0][0:CAP, :], ps[6][0:CAP, 0:1], float(LATE), None, ALU.add)
                                ve.tensor_scalar(row_idx[0][0:CAP, :], ps[6][0:CAP, 1:2], float(LATE), None, ALU.add)
                                ve.tensor_copy(slots[0:CAP, bass.ds(e * 3, 3)], ps[6][0:CAP, 0:3]).then_inc(s["o_idx"], 1)
                                dve.wait_ge(s["o_t"], q + 1)
                                ve.tensor_copy(xgT[:, 0, 4:8, :],
                                               ps[5][:, 0:4 * CAP].rearrange("p (c n) -> p c n", c=4)).then_inc(s["o_xgt_b"], 1)
                                dve.wait_ge(s["o_silu"], q + 1)
                                ve.tensor_tensor(hT[:, 0, :, :].rearrange("p j n -> p (j n)"), sil[:, 0, :],
                                                 ps[0][:, J * CAP:2 * J * CAP], ALU.mult).then_inc(s["o_hok"], 1)
                                dve.wait_ge(s["o_y"], q + 1)
                                dve.wait_ge(s["o_idx"], q + 1)
                                ve.tensor_scalar(y_sb[0:CAP, 0, HALF:D], ps[3][0:CAP, :],
                                                 slots[0:CAP, bass.ds(e * 3 + 2, 1)], None, ALU.mult).then_inc(s["o_yb"], 1)
                                dve.wait_ge(s["o_scattered"], q + 1)
                                dve.sem_inc(carrier, 1)
                        with dve.Else():
                            dve.sem_inc(s["o_onehot"], PASSES - 1)
                            dve.sem_inc(s["o_idx"], PASSES - 1)
                            dve.sem_inc(s["o_xgt_b"], PASSES - 1)
                            dve.sem_inc(s["o_hok"], PASSES - 1)
                            dve.sem_inc(s["o_yb"], PASSES - 1)
                        dve.nop()
                with dve.Else():
                    dve.nop()
                dve.wait_ge(s["base_ok"], 2 * T)
                for t in range(T):
                    for k in range(TOP // 2):
                        n = t * (TOP // 2) + k
                        g = l * T * (TOP // 2) + n
                        dve.wait_ge(rows_in[n % ROWS], 16 * (g // ROWS + 1))
                        link(ve.tensor_tensor(x_tok[:, t, :], x_tok[:, t, :], rows[n % ROWS][:, 0:D], ALU.add))
                        ve.tensor_tensor(x_tok[:, t, :], x_tok[:, t, :], rows[n % ROWS][:, D:2 * D], ALU.add
                                         ).then_inc(rows_used, 1)
                        dve.wait_ge(rows_used, g + 1)
                    norm_stats(2 * l + 1, t)
                    norm_apply(2 * l + 1, t)

        @block.tensor
        def _(pe):
            te = nc.tensor

            def turn(q):
                for t in range(T):
                    if q > 0:
                        pe.wait_ge(norm_done, (q - 1) * T + t + 1)
                    if t >= 2:
                        pe.wait_ge(xT_a, q * T + t - 1)
                        pe.wait_ge(xT_b, q * T + t - 1)
                    for c in range(K):
                        m = te.transpose(ps[4 + 2 * (t % 2) + c // 4][:, (c % 4) * P:(c % 4 + 1) * P],
                                         x_tok[:, t, bass.ds(c, P, step=K)], ident[:, :])
                    m.then_inc(x_turned, 1)
                pe.wait_ge(xT_a, q * T + T)
                pe.wait_ge(xT_b, q * T + T)

            def mixer_unit(l, m):
                n = MIX_BASE[l] + m
                pe.wait_ge(landed[n % RING], landed_count(n))
                return n % RING

            def token_list(l, i, r):
                g = nth(l, i, r)
                pe.wait_ge(onehot_ok, g + 1)
                wait(pe, idx_ok, g)
                for t in range(T):
                    m = te.matmul(ps[6][0:CAP, 0:3], onehot[:, r % 2, t, :], table[:, t, bass.ds(count(i, r) * 3, 3)],
                                  start=(t == 0), stop=(t == T - 1))
                m.then_inc(idx_ps, 1)

            def turn_rows(l, i, r):
                g, b = nth(l, i, r), r % WAYS
                pe.wait_ge(gathered[b], uses(l, i, r))
                wait(pe, xgt_a, g)
                wait(pe, xgt_b, g)
                for c in range(K):
                    m = te.transpose(ps[4 + c // 4][:, (c % 4) * CAP:(c % 4 + 1) * CAP],
                                     xg[0:CAP, b, bass.ds(c, P, step=K)], ident[0:CAP, 0:CAP])
                m.then_inc(t_ps, 1)

            def gate_up(l, i, r):
                g = nth(l, i, r)
                pe.wait_ge(xgt_a, g + 1)
                pe.wait_ge(xgt_b, g + 1)
                wait(pe, h_ok, g - 1)
                for k in range(2):
                    place, there = expert_unit(l, i, r, k)
                    pe.wait_ge(landed[place], there)
                    w = gate_up_view(place)
                    for j in range(J):
                        for c in range(K):
                            m = te.matmul(ps[r % 2][:, (k * J + j) * CAP:(k * J + j + 1) * CAP],
                                          w[:, c, bass.ds(j, P, step=J)], xgT[:, r % 2, c, :],
                                          start=(c == 0), stop=(c == K - 1))
                m.then_inc(h_ps, 1)

            def down(l, i, r):
                g = nth(l, i, r)
                place, there = expert_unit(l, i, r, 2)
                pe.wait_ge(landed[place], there)
                pe.wait_ge(h_ok, g + 1)
                wait(pe, ya, g)
                wait(pe, yb, g)
                w = down_view(place)
                for h in range(2):
                    for j in range(J):
                        m = te.matmul(ps[2 + h][0:CAP, :], hT[:, r % 2, j, :], w[:, j, h * HALF:(h + 1) * HALF],
                                      start=(j == 0), stop=(j == J - 1))
                m.then_inc(y_ps, 1)

            pe.wait_ge(consts, 11)
            for l in range(DEPTH):
                s = L[l]
                if l == 0:
                    pe.wait_ge(x_in, 16 * T)
                    turn(0)

                    def group_product(g):
                        place = MIX_BASE[0] + 4
                        if g == 0:
                            mixer_unit(0, 4)
                        w = ring[:, place, :].rearrange("p (g k d) -> p g k d", g=4, k=2)
                        pe.wait_ge(pooled_ok, 2 * g + 2)
                        for jd in range(2):
                            if 2 * g + jd >= 2:
                                pe.wait_ge(grp_sb, 2 * g + jd - 1)
                            for k in range(2):
                                m = te.matmul(ps[4 + jd][:, :], w[:, g, k, jd * P:(jd + 1) * P], pooled[:, 2 * g + k, :],
                                              start=(k == 0), stop=(k == 1))
                            m.then_inc(grp_ps, 1)

                    for j in range(K):
                        if j % 2 == 0:
                            place = mixer_unit(0, j // 2)
                        if j >= 4:
                            pe.wait_ge(z_sb, j - 3)
                        w = gate_up_view(place)
                        for c in range(K):
                            m = te.matmul(ps[j % 4][:, :], w[:, c, (j % 2) * P:(j % 2 + 1) * P], xT[:, c, :],
                                          start=(c == 0), stop=(c == K - 1))
                        m.then_inc(z_ps, 1)
                        if j % 2 == 1 and j >= 3:
                            group_product((j - 3) // 2)
                    group_product(3)
                    pe.wait_ge(z_sb, K)
                    pe.wait_ge(grp_sb, K)
                    mid, n_out, first = pool_yT, 4, 5
                else:
                    turn(2)
                    pe.wait_ge(ws_cut, 1)
                    for h in range(HEADS):
                        m = te.transpose(ps[6][:, h * P:(h + 1) * P], ws_raw[:, h, :], ident[:, :])
                    m.then_inc(ws_ps, 1)
                    pe.wait_ge(ws_ok, 1)
                    te.matmul(ps[7][:, :], ones[:, :], wsT[:, :, :].rearrange("p h n -> p (h n)"),
                              start=True, stop=True).then_inc(wsum_ps, 1)
                    for u in range(8):
                        w = gate_up_view(mixer_unit(1, u))
                        for t in range(T):
                            if u >= 1:
                                pe.wait_ge(v_add, (u - 1) * T + t + 1)
                            for c in range(K):
                                m = te.matmul(ps[t][:, 0:256], xT[:, c, t * P:(t + 1) * P], w[:, c, :],
                                              start=(c == 0), stop=(c == K - 1))
                            m.then_inc(v_ps, 1)

                    def spatial(j):
                        h = j * HEADS // KS
                        if j == 0:
                            pe.wait_ge(v_ok, T)
                            pe.wait_ge(wsum_ok, 1)
                        if j >= 2:
                            pe.wait_ge(gated_ok, j - 1)
                        for t in range(T):
                            m = te.matmul(ps[6 + j % 2][:, t * P:(t + 1) * P], v_tok[:, t, j * P:(j + 1) * P],
                                          wsT[:, h, :], start=True, stop=True)
                        m.then_inc(sp_ps, 1)

                    LAG = 4
                    for j in range(KS):
                        if j % 2 == 0:
                            w = gate_up_view(mixer_unit(1, 8 + j // 2))
                        if j >= 2:
                            pe.wait_ge(u_sb, j - 1)
                        for c in range(K):
                            m = te.matmul(ps[4 + j % 2][:, :], w[:, c, (j % 2) * P:(j % 2 + 1) * P], xT[:, c, :],
                                          start=(c == 0), stop=(c == K - 1))
                        m.then_inc(u_ps, 1)
                        if j >= LAG:
                            spatial(j - LAG)
                    for j in range(KS - LAG, KS):
                        spatial(j)
                    pe.wait_ge(gated_ok, KS)
                    mid, n_out, first = gT, 8, 16
                places = [mixer_unit(l, first + u) for u in range(n_out)]
                for t in range(T):
                    for h in range(2):
                        n = 2 * t + h
                        if n >= 4:
                            pe.wait_ge(s["mix_res"], n - 3)
                        for k in range(2 * n_out):
                            w = down_view(places[k // 2])
                            m = te.matmul(ps[2 * (t % 2) + h][:, :], mid[:, k, t * P:(t + 1) * P],
                                          w[:, k % 2, h * HALF:(h + 1) * HALF], start=(k == 0), stop=(k == 2 * n_out - 1))
                        m.then_inc(s["mix_ps"], 1)
                turn(2 * l + 1)
                if l == 0:
                    pe.wait_ge(small, 16 * (5 + DEPTH))
                for t in range(T):
                    for c in range(K):
                        m = te.matmul(ps[6][:, t * E:(t + 1) * E], xT[:, c, t * P:(t + 1) * P], wr[:, l, c, :],
                                      start=(c == 0), stop=(c == K - 1))
                m.then_inc(logit_ps, 1)
                pe.wait_ge(s["mix_res"], 2 * T)
                for k in range(2):
                    w = gate_up_view(mixer_unit(l, first + n_out + k))
                    for j in range(J):
                        for c in range(K):
                            m = te.matmul(ps[2 * k + j][:, :], w[:, c, bass.ds(j, P, step=J)], xT[:, c, :],
                                          start=(c == 0), stop=(c == K - 1))
                    m.then_inc(s["shg_ps"], 1)
                pe.wait_ge(score_ok, l + 1)
                pe.wait_ge(chosen_ok, l + 1)
                for t in range(T):
                    for b in range(t + 1):
                        te.matmul(ps[6][:, t * E:(t + 1) * E], before[:, :] if b == t else ones[:, :], chosen[:, b, :],
                                  start=(b == 0), stop=(b == t))
                for b in range(T):
                    m = te.matmul(ps[6][:, T * E:(T + 1) * E], ones[:, :], chosen[:, b, :], start=(b == 0), stop=(b == T - 1))
                m.then_inc(pos_ps, 1)
                w = down_view(mixer_unit(l, first + n_out + 2))
                pe.wait_ge(s["sh_h_ok"], J)
                for t in range(T):
                    for h in range(2):
                        n = 2 * t + h
                        if n >= 4:
                            pe.wait_ge(s["base_ok"], n - 3)
                        for j in range(J):
                            m = te.matmul(ps[2 * (t % 2) + h][:, :], sh_hT[:, j, t * P:(t + 1) * P],
                                          w[:, j, h * HALF:(h + 1) * HALF], start=(j == 0), stop=(j == J - 1))
                        m.then_inc(s["shy_ps"], 1)
                pe.wait_ge(s["table_ok"], 2)
                pe.wait_ge(s["base_ok"], 2 * T)
                for i in range(-AHEAD, WAYS):
                    if i >= -1:
                        gate_up(l, 0, i + 1)
                    token_list(l, 0, i + AHEAD)
                    if i >= -2:
                        turn_rows(l, 0, i + 2)
                    if i >= 0:
                        down(l, 0, i)
                with pe.Fori(1, LAST_BODY) as body:
                    i = body * WAYS
                    for r in range(WAYS):
                        gate_up(l, i, r + 1)
                        token_list(l, i, r + AHEAD)
                        turn_rows(l, i, r + 2)
                        down(l, i, r)
                for i in range(LAST_BODY * WAYS, E):
                    if i + 1 < E:
                        gate_up(l, 0, i + 1)
                    if i + AHEAD < E:
                        token_list(l, 0, i + AHEAD)
                    if i + 2 < E:
                        turn_rows(l, 0, i + 2)
                    down(l, 0, i)
                n_most = pe.value_load(most_i[0:1, 0:1], min_val=0, max_val=S)
                with pe.If(n_most > CAP):
                    with pe.Fori(0, E) as e:
                        n_e = pe.value_load(counts_i[0:1, bass.ds(e, 1)], min_val=0, max_val=S)
                        with pe.If(n_e > CAP):
                            pe.wait_ge(s["o_w"], e * 48 + 48)
                            for p in range(PASSES - 1):
                                q = e * (PASSES - 1) + p
                                pe.wait_ge(s["o_onehot"], q + 1)
                                for t in range(T):
                                    m = te.matmul(ps[6][0:CAP, 0:3], onehot[:, 0, t, :], table[:, t, bass.ds(e * 3, 3)],
                                                  start=(t == 0), stop=(t == T - 1))
                                m.then_inc(s["o_idx_ps"], 1)
                                pe.wait_ge(s["o_gathered"], q + 1)
                                for c in range(K):
                                    m = te.transpose(ps[4 + c // 4][:, (c % 4) * CAP:(c % 4 + 1) * CAP],
                                                     xg[0:CAP, 0, bass.ds(c, P, step=K)], ident[0:CAP, 0:CAP])
                                m.then_inc(s["o_t"], 1)
                                pe.wait_ge(s["o_xgt_a"], q + 1)
                                pe.wait_ge(s["o_xgt_b"], q + 1)
                                for k in range(2):
                                    w = gate_up_view(k)
                                    for j in range(J):
                                        for c in range(K):
                                            m = te.matmul(ps[0][:, (k * J + j) * CAP:(k * J + j + 1) * CAP],
                                                          w[:, c, bass.ds(j, P, step=J)], xgT[:, 0, c, :],
                                                          start=(c == 0), stop=(c == K - 1))
                                m.then_inc(s["o_h"], 1)
                                pe.wait_ge(s["o_hok"], q + 1)
                                for h in range(2):
                                    for j in range(J):
                                        m = te.matmul(ps[2 + h][0:CAP, :], hT[:, 0, j, :],
                                                      down_view(2)[:, j, h * HALF:(h + 1) * HALF],
                                                      start=(j == 0), stop=(j == J - 1))
                                m.then_inc(s["o_y"], 1)
                                pe.wait_ge(s["o_ya"], q + 1)
                                pe.wait_ge(s["o_yb"], q + 1)
                        with pe.Else():
                            pe.sem_inc(s["o_idx_ps"], PASSES - 1)
                            pe.sem_inc(s["o_t"], PASSES - 1)
                            pe.sem_inc(s["o_h"], PASSES - 1)
                            pe.sem_inc(s["o_y"], PASSES - 1)
                        pe.nop()
                with pe.Else():
                    pe.nop()


_INS = ["x", "pool_w_in", "pool_w_grp", "pool_scale", "pool_w_out", "sgu_w_in", "sgu_b_in", "sgu_ln_g", "sgu_ln_b",
        "sgu_w_s", "sgu_b_s", "sgu_w_out", "ln_mix_g", "ln_mix_b", "moe_w_router", "moe_router_bias", "moe_w_gate",
        "moe_w_up", "moe_w_down", "moe_sh_gate", "moe_sh_up", "moe_sh_down", "ln_ffn_g", "ln_ffn_b"]


def kernel(**inputs):
    import numpy as _np
    import concourse.bacc as _bacc
    from concourse import mybir as _mybir
    from concourse.bass_utils import run_bass_kernel_spmd as _run

    nc = _bacc.Bacc("TRN2", target_bir_lowering=False, num_devices=1)
    arrays, args = {}, []
    for name in _INS:
        a = _np.ascontiguousarray(inputs[name])
        arrays[f"in_{name}_dram"] = a
        args.append(nc.dram_tensor(f"in_{name}_dram", a.shape, _mybir.dt.from_np(a.dtype), kind="ExternalInput").ap())
    args.append(nc.dram_tensor("out_0_dram", tuple(inputs["x"].shape), _mybir.dt.float32, kind="ExternalOutput").ap())
    hybrid_trunk(nc, *args)
    r = _run(nc, [arrays], core_ids=[0])
    return r.results[0]["out_0_dram"]
```

```python
from contextlib import ExitStack

import concourse.bass as bass
from concourse import mybir

ALU = mybir.AluOpType
ACT = mybir.ActivationFunctionType
AX = mybir.AxisListType
F32 = mybir.dt.float32
F32R = mybir.dt.float32r
U32 = mybir.dt.uint32
I32 = mybir.dt.int32

P = 128
BANK = 512
CAP = 112
RING = 12
SIZES = (64, 80, CAP)
AHEAD = 5
ROWS = 4
WAYS = 4
LATE = 4096
COLS = 4
LN_EPS = 1e-5
ROUTED_SCALE = 2.5
WINDOWS = (2, 4, 8, 16)


def count(i, r, div=1, mul=1):
    return i * (mul // div) + mul * (r // div)


def wait(eng, sem, value):
    if isinstance(value, int) and value <= 0:
        return
    eng.wait_ge(sem, value)


def hybrid_trunk(nc, x, pool_w_in, pool_w_grp, pool_scale, pool_w_out, sgu_w_in, sgu_b_in, sgu_ln_g, sgu_ln_b,
                 sgu_w_s, sgu_b_s, sgu_w_out, ln_mix_g, ln_mix_b, moe_w_router, moe_router_bias, moe_w_gate,
                 moe_w_up, moe_w_down, moe_sh_gate, moe_sh_up, moe_sh_down, ln_ffn_g, ln_ffn_b, out):
    _, S, D = x.shape
    DEPTH, E, _, F = moe_w_gate.shape
    T = S // P
    K = D // P
    J = F // P
    TOP = 8
    NG = 8
    EG = E // NG
    TOPG = 4
    SW = sgu_w_in.shape[2] // 2
    KS = SW // P
    HEADS = sgu_w_s.shape[1]
    ALPHA = (2 * DEPTH) ** 0.25
    HALF = D // 2
    SH = S // 2
    PASSES = -(-S // CAP)
    assert D == 1024 and S == 512 and F == 256 and E == 64 and SW == 2048 and RING == 3 * WAYS
    UNIT = 2 * D
    LAG = 4
    LAST_BODY = (E - AHEAD) // WAYS
    RAW = (3, 4, 5, 0, 1, 2)
    RAW_UNITS = (4 + 1 + 4, 8 + 8 + 8)
    GROUP_UNIT = 4
    OUT_UNITS = (4, 8)
    SPLITS = (8, 24)
    raw_at, moe_base, loaded = {}, [], [0] * RING
    for l in range(DEPTH):
        for m in range(RAW_UNITS[l]):
            loaded[RAW[m % len(RAW)]] += 1
            raw_at[l, m] = RAW[m % len(RAW)], 16 * loaded[RAW[m % len(RAW)]]
        moe_base.append(list(loaded))
        for u in range(3 * (E + 1)):
            loaded[u % RING] += 1
    split_units = [(l, m) for l in range(DEPTH) for m in range(RAW_UNITS[l]) if (l, m) != (0, GROUP_UNIT)]
    split_no = {unit: n for n, unit in enumerate(split_units)}

    x1_dram = [nc.dram_tensor(f"mixed_rows_{l}", [S, D], F32, kind="Internal").ap() for l in range(DEPTH)]
    picked_dram = [nc.dram_tensor(f"picked_rows_{l}", [S * TOP, D], F32, kind="Internal").ap() for l in range(DEPTH)]

    with ExitStack() as ctx:
        def sb(name, shape, dt=F32):
            return ctx.enter_context(nc.sbuf_tensor(name, shape, dt))

        def sem(name):
            return ctx.enter_context(nc.semaphore(name))

        ps = [ctx.enter_context(nc.psum_tensor(f"ps{i}", [P, BANK], F32)) for i in range(8)]

        def alias(name, at, shape):
            return nc.alloc_sbuf_tensor_at(name, shape, F32R, offset=at)

        def next_place():
            return -(-nc.sbuf_base // 32) * 32

        ring_at = next_place()
        ring = sb("ring", [P, RING, UNIT])
        x_tok = sb("x_tok", [P, T, D])
        xT_at = next_place()
        xT = sb("xT", [P, K, S])
        ident = sb("ident", [P, P])
        before = sb("before", [P, P])
        ones = sb("ones", [P, P])
        lower = sb("lower", [P, NG, NG])
        tok_id = sb("tok_id", [P, T])
        tok_row = sb("tok_row", [P, T])
        wr = sb("wr", [P, DEPTH, K, E])
        rb = sb("rb", [P, DEPTH, E])
        scale_col = sb("scale_col", [P, K])
        sgu_cols = sb("sgu_cols", [P, 3, KS])
        token_idx = [sb(f"token_idx{i}", [P, 1], U32) for i in range(WAYS)]
        row_idx = [sb(f"row_idx{i}", [P, 1], U32) for i in range(WAYS)]
        eps = sb("eps", [P, 1])
        stats = sb("stats", [P, T, 4, 6])
        mv = sb("mv", [P, T, 2])
        std = sb("std", [P, T])
        rstd = sb("rstd", [P, T])
        counts_i = sb("counts_i", [P, E], I32)
        most_i = sb("most_i", [P, 1], I32)

        WORK = 18432
        work_at = next_place()
        work = sb("work", [P, WORK])

        def area(at, *dims):
            n = 1
            for d in dims:
                n *= d
            assert at + n <= WORK
            v = work[:, at:at + n]
            if len(dims) == 2:
                v = v.rearrange("p (a b) -> p a b", a=dims[0])
            if len(dims) == 3:
                v = v.rearrange("p (a b c) -> p a b c", a=dims[0], b=dims[1])
            return v, at + n

        gain_shift, end = area(0, 2, D)
        ZP = 16 + S
        z_pad, at = area(end, 2, ZP)
        win_a, at = area(at, ZP)
        win_b, at = area(at, ZP)
        pooled, at = area(at, K, S)
        yT_at, at = at, at + 2 * K * S
        edge, at = area(at, len(WINDOWS), 16)
        v_tok, at = area(0, T, SW)
        gT, at = area(at, KS, S)
        v_bias, at = area(at, 2, 256)
        wsT, at = area(at, HEADS, P)
        ws_sum, at = area(at, HEADS, P)
        bs_row, at = area(at, HEADS, P)
        gain_late, _ = area(at - 2 * D, 2, D)
        ws_raw, _ = area(T * SW, HEADS, P)
        xg, at = area(end, WAYS, D)
        xgT, at = area(at, 2, K, CAP)
        sil, at = area(at, 2, J * CAP)
        hT_at = at
        hT, at = area(at, 2, J, CAP)
        hT_low_at, at = at, at + 2 * J * CAP
        y_at = at
        y_sb, at = area(at, WAYS, D)
        onehot_at, at = at, at + 2 * T * CAP
        slot_no, at = area(at, CAP)
        table_at, at = at, at + T * E * COLS
        posm, at = area(at, T, E)
        sh_sil, at = area(at, J, S)
        sh_hT, at = area(at, J, S)
        slots, at = area(at, E * 3)
        assert 2 * WAYS >= 2 * ROWS
        rows = [v[:, 2 * n:2 * n + 2, :].rearrange("p k d -> p (k d)") for v in (xg, y_sb) for n in range(WAYS // 2)]
        end_rows = y_at + WAYS * D
        scores, r_at = area(y_at, T, E)
        biased, r_at = area(r_at, T, E)
        top2, r_at = area(r_at, T * NG, 8)
        gscore, r_at = area(r_at, T, NG)
        g_gt, r_at = area(r_at, T, NG, NG)
        g_eq, r_at = area(r_at, T, NG, NG)
        g_rank, r_at = area(r_at, T, NG)
        g_sel, r_at = area(r_at, T, NG)
        g_pen, r_at = area(r_at, T, NG)
        masked, r_at = area(r_at, T, E)
        top8, r_at = area(r_at, T, 8)
        taken, r_at = area(r_at, T, E)
        chosen, r_at = area(r_at, T, E)
        cum_a, r_at = area(r_at, T, E)
        cum_b, r_at = area(r_at, T, E)
        gsum, r_at = area(r_at, T)
        grec, r_at = area(r_at, T)
        most, r_at = area(r_at, 1)
        assert r_at <= end_rows

        xT_high = alias("xT_high", xT_at, [P, K, S])
        xT_low = alias("xT_low", ring_at + 4 * UNIT * 6, [P, K, S])
        w_high = [alias(f"w_high{i}", ring_at + 4 * UNIT * (8 + 2 * i), [P, UNIT]) for i in range(2)]
        w_low = [alias(f"w_low{i}", ring_at + 4 * UNIT * (9 + 2 * i), [P, UNIT]) for i in range(2)]
        yT_high = alias("yT_high", work_at + 4 * yT_at, [P, K, S])
        yT_low = alias("yT_low", work_at + 4 * (yT_at + K * S), [P, K, S])
        gT_high = alias("gT_high", work_at + 4 * T * SW, [P, KS, S])
        gT_low = alias("gT_low", work_at, [P, T, SW])

        onehot = alias("onehot", work_at + 4 * onehot_at, [P, 2, T, CAP])
        table = alias("table", work_at + 4 * table_at, [P, T, E * COLS])
        hT_high = alias("hT_high", work_at + 4 * hT_at, [P, 2, J, CAP])
        hT_low = alias("hT_low", work_at + 4 * hT_low_at, [P, 2, J, CAP])
        down_high = alias("down_high", xT_at, [P, 2, UNIT])
        down_low = alias("down_low", ring_at, [P, RING, UNIT])

        landed = [sem(f"landed{i}") for i in range(RING)]
        consts = sem("consts")
        const_step = sem("const_step")
        small = sem("small")
        rows_used = sem("rows_used")
        rows_summed = sem("rows_summed")
        gain_in = sem("gain_in")
        dve_step = sem("dve_step")
        out_stored = sem("out_stored")
        carrier = sem("carrier")
        high_ok, low_ok = sem("high_ok"), sem("low_ok")
        out_used = sem("out_used")
        z_ps, z_sb, pooled_ok, grp_ps, grp_hi, grp_sb = map(sem, ("z_ps", "z_sb", "pooled_ok", "grp_ps", "grp_hi", "grp_sb"))
        bias_in = [sem("bias_in0"), sem("bias_in1")]
        v_ps, v_add, v_sb, v_var, v_std, v_ok = map(sem, ("v_ps", "v_add", "v_sb", "v_var", "v_std", "v_ok"))
        ws_in, ws_cut, ws_ps, ws_ok, wsum_ps, wsum_ok = map(sem, ("ws_in", "ws_cut", "ws_ps", "ws_ok", "wsum_ps", "wsum_ok"))
        u_ps, u_sb, sp_ps, gated_ok = map(sem, ("u_ps", "u_sb", "sp_ps", "gated_ok"))

        names = ("mix_ps mix_res "
                 "x1_stored table_ok shg_ps sh_sil_ok sh_h_ok shy_ps base_ok "
                 "o_w o_onehot o_idx_ps o_idx o_gath o_gathered o_t o_xgt_a o_xgt_b o_h o_silu o_hok o_y o_ya o_yb o_scat o_scattered o_done").split()
        L = [{n: sem(f"{n}_{l}") for n in names} for l in range(DEPTH)]
        onehot_ok, idx_ps, idx_ok, t_ps, xgt_a, xgt_b, h_ps, silu_ok, h_ok, y_ps, ya, yb = map(
            sem, ("onehot_ok", "idx_ps", "idx_ok", "t_ps", "xgt_a", "xgt_b", "h_ps", "silu_ok", "h_ok", "y_ps", "ya", "yb"))
        h_step, down_high_ok, down_low_ok = map(sem, ("h_step", "down_high_ok", "down_low_ok"))
        gathered = [sem(f"gathered{i}") for i in range(WAYS)]
        scattered = [sem(f"scattered{i}") for i in range(WAYS)]
        rows_in = [sem(f"rows_in{i}") for i in range(ROWS)]
        logit_ps, score_ok, chosen_ok, pos_ps, slots_ok, zeroed = map(
            sem, ("logit_ps", "score_ok", "chosen_ok", "pos_ps", "slots_ok", "zeroed"))
        norm_var, norm_std, norm_done = map(sem, ("norm_var", "norm_std", "norm_done"))
        x_turned, xT_a, xT_b = map(sem, ("x_turned", "xT_a", "xT_b"))

        def expert_unit(l, i, r, k):
            u = 3 * (r + 1) + k
            place = u % RING
            return place, i * 4 + 16 * (moe_base[l][place] + u // RING + 1)

        def turn_bank(q, t):
            return (2 * (t % 2), 0, 6, 0)[q]

        def v_no(u, t):
            return 2 * t + u if u < 2 else u * T + t

        def gain_of(q):
            return gain_late if q == 2 else gain_shift

        def wait_split_used(eng, n):
            l, m = split_units[n]
            q = m - (RAW_UNITS[l] - OUT_UNITS[l])
            if q >= OUT_UNITS[l] - 2:
                eng.wait_ge(L[l]["mix_ps"], 2 * T)
            elif q >= 0:
                eng.wait_ge(out_used, l * (OUT_UNITS[0] - 2) + q + 1)
            elif l == 0:
                eng.wait_ge(z_ps, 2 * m + 2)
            elif m < 8:
                eng.wait_ge(v_ps, v_no(m, T - 1) + 1)
            else:
                eng.wait_ge(u_ps, 2 * (m - 8) + 2)

        def nth(l, i, r):
            return count(i, r) + l * E

        def uses(l, i, r):
            return count(i, r, WAYS, 16) + 16 + l * 16 * (E // WAYS)

        def wait_scattered(eng, l):
            for b in range(WAYS):
                eng.wait_ge(scattered[b], 16 * (E // WAYS) * (l + 1))

        def gate_up_view(place):
            return ring[:, place, :].rearrange("p (c f) -> p c f", c=K)

        def down_view(place):
            return ring[:, place, :].rearrange("p (j d) -> p j d", j=J)

        block = ctx.enter_context(nc.Block())

        @block.sync
        def _(sp):
            def mixer_sources(l):
                if l == 0:
                    for u in range(4):
                        yield "w", pool_w_in[0][:, u * 256:(u + 1) * 256].rearrange("(p c) f -> p c f", c=K)
                    yield "w", pool_w_grp[0].rearrange("g (k p) d -> p (g k) d", p=P)
                    for u in range(4):
                        yield "r", pool_w_out[0][u * 256:(u + 1) * 256, :].rearrange("(k p) d -> p k d", p=P)
                else:
                    for u in list(range(8, 16)) + list(range(8)):
                        yield "w", sgu_w_in[0][:, u * 256:(u + 1) * 256].rearrange("(p c) f -> p c f", c=K)
                    for u in range(8):
                        yield "r", sgu_w_out[0][u * 256:(u + 1) * 256, :].rearrange("(k p) d -> p k d", p=P)

            def wait_raw_used(l, m):
                if (l, m) == (0, GROUP_UNIT):
                    sp.wait_ge(grp_ps, K)
                else:
                    sp.wait_ge(low_ok, split_no[l, m] + 1)

            def last_raw(l, place):
                return max(m for m in range(RAW_UNITS[l]) if raw_at[l, m][0] == place)

            def load(l, i, r, k, w):
                place, _ = expert_unit(l, 0, r, k)
                src = w[l, bass.ds(count(i, r), 1)].rearrange("o (p c) f -> p (o c f)", p=P)
                sp.dma_start(ring[:, place, :], src).then_inc(landed[place], 16)

            def load_gate_up(l, i, r):
                wait(sp, h_ps, nth(l, i, r) - WAYS + 1)
                load(l, i, r, 0, moe_w_gate)
                load(l, i, r, 1, moe_w_up)

            def load_down(l, i, r):
                wait(sp, y_ps, nth(l, i, r) - WAYS + 1)
                load(l, i, r, 2, moe_w_down)

            def load_rows(l):
                wait_scattered(sp, l)
                sp.wait_ge(L[l]["o_done"], 1)
                picks = picked_dram[l].rearrange("(t p k) d -> t p (k d)", t=T, k=TOP)
                for n in range(T * TOP // 2):
                    if n >= ROWS:
                        used = 2 * (l * T + n // ROWS - 1) + n % ROWS % 2 + 1
                        sp.wait_ge(rows_summed if n % ROWS < 2 else rows_used, used)
                    half = n % (TOP // 2)
                    sp.dma_start(rows[n % ROWS], picks[n // (TOP // 2), :, half * 2 * D:(half + 1) * 2 * D]
                                 ).then_inc(rows_in[n % ROWS], 16)

            EARLY = 3
            for l in range(DEPTH):
                s = L[l]
                for m, (kind, src) in enumerate(mixer_sources(l)):
                    if l > 0 and m == EARLY:
                        load_rows(l - 1)
                    place = raw_at[l, m][0]
                    if m >= len(RAW):
                        wait_raw_used(l, m - len(RAW))
                    elif l > 0:
                        sp.wait_ge(y_ps if place % 3 == 2 else h_ps, l * E - (WAYS - 1 if place >= 3 else 0))
                    dst = ring[:, place, :].rearrange("p (c f) -> p c f", c=K if kind == "w" else 2)
                    sp.dma_start(dst, src).then_inc(landed[place], 16)
                    if l == 0 and m == 0:
                        for t in range(T):
                            sp.dma_start(x_tok[:, t, :], x[0, t * P:(t + 1) * P, :]).then_inc(rows_in[t], 16)
                for k, w in enumerate((moe_sh_gate, moe_sh_up, moe_sh_down)):
                    wait_raw_used(l, last_raw(l, k))
                    sp.dma_start(ring[:, k, :].rearrange("p (c f) -> p c f", c=w.shape[1] // P),
                                 w[l].rearrange("(p c) f -> p c f", p=P)).then_inc(landed[k], 16)
                for r in range(WAYS):
                    for k, w in enumerate((moe_w_gate, moe_w_up, moe_w_down)):
                        place = expert_unit(l, 0, r, k)[0]
                        if r == 0:
                            wait_raw_used(l, last_raw(l, place))
                        elif place < 3:
                            sp.wait_ge(s["shy_ps"] if k == 2 else s["shg_ps"], 2 * T if k == 2 else k + 3)
                        elif place < 8:
                            sp.wait_ge(z_ps if l == 0 else u_ps, K if l == 0 else KS)
                        else:
                            sp.wait_ge(s["mix_ps"], 2 * T)
                        load(l, 0, r, k, w)
                load_gate_up(l, 0, WAYS)
                with sp.Fori(1, E // WAYS - 1) as body:
                    i = body * WAYS
                    for r in range(WAYS):
                        load_down(l, i, r)
                        load_gate_up(l, i, r + 1)
                for r in range(E - WAYS, E):
                    load_down(l, 0, r)
                    if r + 1 < E:
                        load_gate_up(l, 0, r + 1)
                sp.wait_ge(s["table_ok"], 2)
                n_most = sp.value_load(most_i[0:1, 0:1], min_val=0, max_val=S)
                with sp.If(n_most > CAP):
                    sp.wait_ge(y_ps, E * (l + 1))
                    with sp.Fori(0, E) as e:
                        n_e = sp.value_load(counts_i[0:1, bass.ds(e, 1)], min_val=0, max_val=S)
                        with sp.If(n_e > CAP):
                            for k, w in enumerate((moe_w_gate, moe_w_up, moe_w_down)):
                                src = w[l, bass.ds(e, 1)].rearrange("o (p c) f -> p (o c f)", p=P)
                                sp.dma_start(ring[:, k, :], src).then_inc(s["o_w"], 16)
                            sp.wait_ge(s["o_y"], e * (PASSES - 1) + (PASSES - 1))
                            sp.sem_inc(carrier, 1)
                        with sp.Else():
                            sp.sem_inc(s["o_w"], 48)
                            sp.nop()
                        sp.nop()
                with sp.Else():
                    sp.nop()
            load_rows(DEPTH - 1)
            for t in range(T):
                sp.wait_ge(norm_done, (2 * DEPTH - 1) * T + t + 1)
                sp.dma_start(out[0, t * P:(t + 1) * P, :], x_tok[:, t, :]).then_inc(out_stored, 16)
            sp.wait_ge(out_stored, 16 * T)

        @block.gpsimd
        def _(pool):
            gp = nc.gpsimd
            gp.memset(ident[:, :], 0.0).then_inc(const_step, 1)
            gp.memset(before[:, :], 1.0).then_inc(const_step, 1)
            gp.memset(lower[:, :, :], 1.0).then_inc(const_step, 1)
            gp.memset(ones[:, :], 1.0).then_inc(consts, 1)
            gp.memset(eps[:, :], LN_EPS).then_inc(consts, 1)
            gp.memset(z_pad[:, :, 0:16], 0.0).then_inc(consts, 1)
            gp.memset(win_a[:, 0:16], 0.0).then_inc(consts, 1)
            gp.memset(win_b[:, 0:16], 0.0).then_inc(consts, 1)
            pool.wait_ge(const_step, 3)
            gp.affine_select(out=ident[:, :], in_=ident[:, :], compare_op=ALU.not_equal, fill=1.0, base=0,
                             pattern=[[-1, P]], channel_multiplier=1).then_inc(consts, 1)
            gp.affine_select(out=before[:, :], in_=before[:, :], compare_op=ALU.is_gt, fill=0.0, base=0,
                             pattern=[[1, P]], channel_multiplier=-1).then_inc(consts, 1)
            gp.affine_select(out=lower[:, :, :], in_=lower[:, :, :], compare_op=ALU.is_gt, fill=0.0, base=0,
                             pattern=[[1, NG], [-1, NG]], channel_multiplier=0).then_inc(consts, 1)
            gp.iota(tok_id[:, :], pattern=[[P, T]], base=-LATE, channel_multiplier=1,
                    allow_small_or_imprecise_dtypes=True).then_inc(consts, 1)
            gp.iota(tok_row[:, :], pattern=[[P * TOP, T]], base=-LATE, channel_multiplier=TOP,
                    allow_small_or_imprecise_dtypes=True).then_inc(consts, 1)
            gp.iota(edge, pattern=[[0, len(WINDOWS)], [1, 16]], base=1, channel_multiplier=0,
                    allow_small_or_imprecise_dtypes=True).then_inc(consts, 1)

            passed = pool.alloc_register("passed")
            last_token = pool.to_reg(S - 1)
            last_row = pool.to_reg(S * TOP - 1)

            def load_gain_shift(q, g, b):
                pool.dma_start(gain_of(q)[:, 0, :], g.partition_broadcast(P)).then_inc(gain_in, 16)
                pool.dma_start(gain_of(q)[:, 1, :], b.partition_broadcast(P)).then_inc(gain_in, 16)

            def by_size(l, i, r, move, sizes=SIZES, n_e=None):
                if n_e is None:
                    n_e = pool.value_load(counts_i[0:1, bass.ds(count(i, r), 1)], min_val=0, max_val=S)
                if len(sizes) == 1:
                    move(sizes[0])
                    return
                with pool.If(n_e > sizes[0]):
                    by_size(l, i, r, move, sizes[1:], n_e)
                with pool.Else():
                    move(sizes[0])

            def gather(l, i, r):
                g, b = nth(l, i, r), r % WAYS
                pool.wait_ge(idx_ok, g + 1)
                wait(pool, t_ps, g - WAYS + 1)
                pool.sem_inc(carrier, 1)

                def move(n):
                    pool.indirect_dma_start(
                        out=xg[0:n, b, :], out_offset=None, in_=x1_dram[l][:, :],
                        in_offset=bass.IndirectOffsetOnAxis(ap=token_idx[b][0:n, :], axis=0),
                        bounds_check=last_token, oob_is_err=False).then_inc(gathered[b], 16)

                by_size(l, i, r, move)

            def scatter(l, i, r):
                g, b = nth(l, i, r), r % WAYS
                pool.wait_ge(ya, g + 1)
                pool.wait_ge(yb, g + 1)
                pool.sem_inc(carrier, 1)

                def move(n):
                    pool.indirect_dma_start(
                        out=picked_dram[l][:, :],
                        out_offset=bass.IndirectOffsetOnAxis(ap=row_idx[b][0:n, :], axis=0),
                        in_=y_sb[0:n, b, :], in_offset=None,
                        bounds_check=last_row, oob_is_err=False).then_inc(scattered[b], 16)

                by_size(l, i, r, move)

            for l in range(DEPTH):
                s = L[l]
                if l == 0:
                    pool.wait_ge(x_turned, T)
                    load_gain_shift(0, ln_mix_g[0], ln_mix_b[0])
                else:
                    wait_scattered(pool, l - 1)
                    pool.dma_start(ws_raw, sgu_w_s[0].rearrange("h i j -> i h j")).then_inc(ws_in, 16)
                    pool.dma_start(bs_row.rearrange("p h i -> p (h i)"),
                                   sgu_b_s[0].rearrange("h i -> (h i)").partition_broadcast(P)).then_inc(ws_in, 16)
                    for u in range(8):
                        if u >= 2:
                            pool.wait_ge(v_add, v_no(u - 2, T - 1) + 1)
                        pool.dma_start(v_bias[:, u % 2, :], sgu_b_in[0, SW + u * 256:SW + (u + 1) * 256]
                                       .partition_broadcast(P)).then_inc(bias_in[u % 2], 16)
                        if u == 1:
                            pool.wait_ge(ws_in, 32)
                            gp.affine_select(out=ws_raw, in_=ws_raw, compare_op=ALU.is_ge, fill=0.0, base=0,
                                             pattern=[[0, HEADS], [-1, P]], channel_multiplier=1).then_inc(ws_cut, 1)
                    pool.wait_ge(gated_ok, KS)
                    load_gain_shift(2 * l, ln_mix_g[l], ln_mix_b[l])
                for t in range(T):
                    pool.wait_ge(norm_done, 2 * l * T + t + 1)
                    pool.dma_start(x1_dram[l][t * P:(t + 1) * P, :], x_tok[:, t, :]).then_inc(s["x1_stored"], 16)
                load_gain_shift(2 * l + 1, ln_ffn_g[l], ln_ffn_b[l])
                gp.memset(xg[:, :, :], 0.0).then_inc(zeroed, 1)
                gp.iota(slot_no, pattern=[[1, CAP]], base=0, channel_multiplier=0,
                        allow_small_or_imprecise_dtypes=True).then_inc(slots_ok, 1)
                pool.wait_ge(zeroed, l + 1)
                pool.wait_ge(s["x1_stored"], 16 * T)
                pool.wait_ge(s["table_ok"], 2)
                for i in range(-AHEAD, WAYS):
                    gather(l, 0, i + AHEAD)
                    if i >= 0:
                        scatter(l, 0, i)
                with pool.Fori(1, LAST_BODY) as body:
                    i = body * WAYS
                    for r in range(WAYS):
                        gather(l, i, r + AHEAD)
                        scatter(l, i, r)
                for i in range(LAST_BODY * WAYS, E):
                    if i + AHEAD < E:
                        gather(l, 0, i + AHEAD)
                    scatter(l, 0, i)
                n_most = pool.value_load(most_i[0:1, 0:1], min_val=0, max_val=S)
                with pool.If(n_most > CAP):
                    wait_scattered(pool, l)
                    pool.reg_mov(passed, 0)
                    with pool.Fori(0, E) as e:
                        n_e = pool.value_load(counts_i[0:1, bass.ds(e, 1)], min_val=0, max_val=S)
                        with pool.If(n_e > CAP):
                            for p in range(PASSES - 1):
                                q = e * (PASSES - 1) + p
                                pool.wait_ge(s["o_idx"], q + 1)
                                pool.sem_inc(carrier, 1)
                                pool.indirect_dma_start(
                                    out=xg[0:CAP, 0, :], out_offset=None, in_=x1_dram[l][:, :],
                                    in_offset=bass.IndirectOffsetOnAxis(ap=token_idx[0][0:CAP, :], axis=0),
                                    bounds_check=last_token, oob_is_err=False).then_inc(s["o_gath"], 16)
                                pool.reg_add(passed, passed, 16)
                                pool.wait_ge(s["o_gath"], pool.snap(passed))
                                pool.sem_inc(s["o_gathered"], 1)
                                pool.wait_ge(s["o_ya"], q + 1)
                                pool.wait_ge(s["o_yb"], q + 1)
                                pool.sem_inc(carrier, 1)
                                pool.indirect_dma_start(
                                    out=picked_dram[l][:, :],
                                    out_offset=bass.IndirectOffsetOnAxis(ap=row_idx[0][0:CAP, :], axis=0),
                                    in_=y_sb[0:CAP, 0, :], in_offset=None,
                                    bounds_check=last_row, oob_is_err=False).then_inc(s["o_scat"], 16)
                                pool.wait_ge(s["o_scat"], pool.snap(passed))
                                pool.sem_inc(s["o_scattered"], 1)
                        with pool.Else():
                            pool.sem_inc(s["o_gathered"], PASSES - 1)
                            pool.sem_inc(s["o_scattered"], PASSES - 1)
                        pool.nop()
                with pool.Else():
                    pool.nop()
                pool.sem_inc(s["o_done"], 1)

        @block.scalar
        def _(act):
            sc = nc.scalar
            SMALL_ALL = 16 * (5 + DEPTH)

            def turn(q, tiles=range(T)):
                for t in tiles:
                    act.wait_ge(x_turned, q * T + t + 1)
                    for half in range(2):
                        dst = xT_high if q % 2 == 0 else xT
                        m = sc.activation(dst[:, 4 * half:4 * half + 4, t * P:(t + 1) * P],
                                          ps[turn_bank(q, t) + half][:, :].rearrange("p (c n) -> p c n", c=4), ACT.Copy)
                        if q % 2:
                            m.then_inc(xT_b if half else xT_a, 1)
                    if q % 2 == 0:
                        m.then_inc(xT_a, 1)

            def split_high(n):
                place, there = raw_at[split_units[n]]
                act.wait_ge(landed[place], there)
                if n >= 2:
                    wait_split_used(act, n - 2)
                sc.activation(w_high[n % 2][:, :], ring[:, place, :], ACT.Copy).then_inc(high_ok, 1)

            def norm(q, tiles=range(T)):
                for t in tiles:
                    act.wait_ge(norm_var, q * T + t + 1)
                    if q == 0 and t == 0:
                        act.wait_ge(consts, 11)
                    sc.activation(std[:, t:t + 1], mv[:, t, 1:2], ACT.Sqrt, bias=eps[:, 0:1]).then_inc(norm_std, 1)

            def split_down_high(l, i, r):
                g = nth(l, i, r)
                place, there = expert_unit(l, i, r, 2)
                act.wait_ge(landed[place], there)
                wait(act, y_ps, g - 1)
                sc.activation(down_high[:, r % 2, :], ring[:, place, :], ACT.Copy).then_inc(down_high_ok, 1)

            def silu(l, i, r):
                g = nth(l, i, r)
                act.wait_ge(h_ps, g + 1)
                wait(act, h_ok, g - 1)
                sc.activation(sil[:, r % 2, :], ps[r % 2][:, 0:J * CAP], ACT.Silu).then_inc(silu_ok, 1)

            def xgt_half(l, i, r):
                g = nth(l, i, r)
                act.wait_ge(t_ps, g + 1)
                wait(act, h_ps, g - 1)
                sc.activation(xgT[:, r % 2, 0:4, :], ps[4][:, 0:4 * CAP].rearrange("p (c n) -> p c n", c=4),
                              ACT.Copy).then_inc(xgt_a, 1)

            def y_half(l, i, r):
                g, b = nth(l, i, r), r % WAYS
                act.wait_ge(y_ps, g + 1)
                act.wait_ge(idx_ok, g + 1)
                wait(act, scattered[b], uses(l, i, r) - 16)
                act.sem_inc(carrier, 1)
                sc.activation(y_sb[0:CAP, b, 0:HALF], ps[2][0:CAP, :], ACT.Copy,
                              scale=slots[0:CAP, bass.ds(count(i, r) * 3 + 2, 1)]).then_inc(ya, 1)

            for l in range(DEPTH):
                s = L[l]
                if l == 0:
                    split_high(0)
                if l == 0:
                    turn(0)
                    split_high(1)
                    with nc.allow_non_contiguous_dma(reason="per-channel columns, a few hundred numbers"):
                        act.dma_start(scale_col[:, :], pool_scale[0].rearrange("(k p) -> p k", p=P)).then_inc(small, 16)
                        act.dma_start(sgu_cols[:, 0, :], sgu_b_in[0, 0:SW].rearrange("(k p) -> p k", p=P)).then_inc(small, 16)
                        act.dma_start(sgu_cols[:, 1, :], sgu_ln_g[0].rearrange("(k p) -> p k", p=P)).then_inc(small, 16)
                        act.dma_start(sgu_cols[:, 2, :], sgu_ln_b[0].rearrange("(k p) -> p k", p=P)).then_inc(small, 16)
                    act.dma_start(rb[:, :, :].rearrange("p l e -> p (l e)"),
                                  moe_router_bias.rearrange("l e -> (l e)").partition_broadcast(P)).then_inc(small, 16)
                    for layer in range(DEPTH):
                        act.dma_start(wr[:, layer, :, :], moe_w_router[layer].rearrange("(p c) e -> p c e", c=K)).then_inc(small, 16)

                    def y_high(jd):
                        act.wait_ge(grp_ps, jd + 1)
                        sc.activation(yT_high[:, jd, :], ps[4 + jd % 2][:, :], ACT.Copy,
                                      scale=scale_col[:, jd:jd + 1]).then_inc(grp_hi, 1)

                    for j in range(K):
                        act.wait_ge(z_ps, j + 1)
                        if j == 0:
                            act.wait_ge(small, SMALL_ALL)
                        if j >= 2:
                            act.wait_ge(pooled_ok, j - 1)
                        sc.activation(z_pad[:, j % 2, 16:], ps[j % 4][:, :], ACT.Copy).then_inc(z_sb, 1)
                        if j % 2 == 1:
                            split_high(j // 2 + 2)
                            if j >= 3:
                                y_high(j - 3)
                                y_high(j - 2)
                    y_high(K - 2)
                    y_high(K - 1)
                    split_high(6)
                    split_high(7)
                else:
                    act.wait_ge(ws_ps, 1)
                    sc.activation(wsT[:, :, :], ps[4][:, :].rearrange("p (h n) -> p h n", h=HEADS), ACT.Copy).then_inc(ws_ok, 1)
                    split_high(SPLITS[0] + 2)
                    act.wait_ge(wsum_ps, 1)
                    sc.activation(ws_sum[:, :, :], ps[5][:, :].rearrange("p (h n) -> p h n", h=HEADS), ACT.Copy).then_inc(wsum_ok, 1)
                    split_high(SPLITS[0] + 3)

                    def gelu(u, t):
                        act.wait_ge(v_add, v_no(u, t) + 1)
                        blk = v_tok[:, t, u * 256:(u + 1) * 256]
                        sc.activation(blk, blk, ACT.Gelu_apprx_tanh).then_inc(v_sb, 1)

                    for t in range(T):
                        gelu(0, t)
                        gelu(1, t)
                    for u in range(2, 8):
                        for t in range(T):
                            gelu(u, t)
                        split_high(SPLITS[0] + u + 2)
                    for j in range(KS):
                        if j == 1:
                            for t in range(T):
                                act.wait_ge(v_var, t + 1)
                                sc.activation(std[:, t:t + 1], mv[:, t, 1:2], ACT.Sqrt, bias=eps[:, 0:1]).then_inc(v_std, 1)
                        act.wait_ge(u_ps, j + 1)
                        if j == 0:
                            act.wait_ge(ws_ps, 1)
                        sc.activation(gT[:, j, :], ps[4 + j % 2][:, :], ACT.Gelu_apprx_tanh,
                                      bias=sgu_cols[:, 0, j:j + 1]).then_inc(u_sb, 1)
                        if j % 2 == 1:
                            split_high(SPLITS[0] + 8 + j // 2 + 2)
                    for q in range(2, OUT_UNITS[1]):
                        split_high(SPLITS[0] + 16 + q)
                norm(2 * l)
                turn(2 * l + 1)
                act.wait_ge(logit_ps, (l + 1) * T)
                sc.activation(scores.rearrange("p t e -> p (t e)"), ps[2][:, 0:T * E], ACT.Sigmoid).then_inc(score_ok, 1)
                for half in range(2):
                    act.wait_ge(s["shg_ps"], 2 * half + 1)
                    sc.activation(sh_sil[:, :, half * SH:(half + 1) * SH],
                                  ps[4 + 2 * half][:, :].rearrange("p (j n) -> p j n", j=J), ACT.Silu
                                  ).then_inc(s["sh_sil_ok"], 1)
                act.wait_ge(s["shg_ps"], 4)
                for i in range(-2, WAYS):
                    if i >= -1:
                        split_down_high(l, 0, i + 1)
                        silu(l, 0, i + 1)
                    xgt_half(l, 0, i + 2)
                    if i >= 0:
                        y_half(l, 0, i)
                with act.Fori(1, LAST_BODY) as body:
                    i = body * WAYS
                    for r in range(WAYS):
                        split_down_high(l, i, r + 1)
                        silu(l, i, r + 1)
                        xgt_half(l, i, r + 2)
                        y_half(l, i, r)
                for i in range(LAST_BODY * WAYS, E):
                    if i + 1 < E:
                        split_down_high(l, 0, i + 1)
                        silu(l, 0, i + 1)
                    if i + 2 < E:
                        xgt_half(l, 0, i + 2)
                    y_half(l, 0, i)
                n_most = act.value_load(most_i[0:1, 0:1], min_val=0, max_val=S)
                with act.If(n_most > CAP):
                    with act.Fori(0, E) as e:
                        n_e = act.value_load(counts_i[0:1, bass.ds(e, 1)], min_val=0, max_val=S)
                        with act.If(n_e > CAP):
                            for p in range(PASSES - 1):
                                q = e * (PASSES - 1) + p
                                act.wait_ge(s["o_t"], q + 1)
                                sc.activation(xgT[:, 0, 0:4, :], ps[4][:, 0:4 * CAP].rearrange("p (c n) -> p c n", c=4),
                                              ACT.Copy).then_inc(s["o_xgt_a"], 1)
                                act.wait_ge(s["o_h"], q + 1)
                                sc.activation(sil[:, 0, :], ps[0][:, 0:J * CAP], ACT.Silu).then_inc(s["o_silu"], 1)
                                act.wait_ge(s["o_y"], q + 1)
                                act.sem_inc(carrier, 1)
                                sc.activation(y_sb[0:CAP, 0, 0:HALF], ps[2][0:CAP, :], ACT.Copy,
                                              scale=slots[0:CAP, bass.ds(e * 3 + 2, 1)]).then_inc(s["o_ya"], 1)
                                act.wait_ge(s["o_ya"], q + 1)
                                act.sem_inc(carrier, 1)
                        with act.Else():
                            act.sem_inc(s["o_xgt_a"], PASSES - 1)
                            act.sem_inc(s["o_silu"], PASSES - 1)
                            act.sem_inc(s["o_ya"], PASSES - 1)
                        act.nop()
                with act.Else():
                    act.nop()
                if l + 1 < DEPTH:
                    split_high(SPLITS[0])
                    split_high(SPLITS[0] + 1)
                    for t in range(T):
                        norm(2 * l + 1, [t])
                        turn(2 * l + 2, [t])
                else:
                    norm(2 * l + 1)

        @block.vector
        def _(dve):
            ve = nc.vector
            chain = [0]

            def link(ins):
                chain[0] += 1
                ins.then_inc(dve_step, 1)
                dve.wait_ge(dve_step, chain[0])

            def turn(q, tiles=range(T)):
                for t in tiles:
                    banks = [ps[turn_bank(q, t) + half][:, :].rearrange("p (c n) -> p c n", c=4) for half in range(2)]
                    dve.wait_ge(xT_a, q * T + t + 1)
                    for half in range(2):
                        at = (slice(None), slice(4 * half, 4 * half + 4), slice(t * P, (t + 1) * P))
                        m = ve.tensor_tensor(xT_low[at], banks[half], xT_high[at].bitcast(F32), ALU.subtract)
                    m.then_inc(xT_b, 1)

            def split_low(n):
                place, there = raw_at[split_units[n]]
                dve.wait_ge(landed[place], there)
                dve.wait_ge(high_ok, n + 1)
                ve.tensor_tensor(w_low[n % 2][:, :], ring[:, place, :], w_high[n % 2][:, :].bitcast(F32),
                                 ALU.subtract).then_inc(low_ok, 1)

            def norm_stats(q, t):
                for h in range(2):
                    link(ve.bn_stats(stats[:, t, h, :], x_tok[:, t, h * HALF:(h + 1) * HALF]))
                ve.bn_aggr(mv[:, t, :], stats[:, t, 0:2, :].rearrange("p a b -> p (a b)")).then_inc(norm_var, 1)

            def norm_apply(q, t):
                dve.wait_ge(norm_std, q * T + t + 1)
                link(ve.reciprocal(rstd[:, t:t + 1], std[:, t:t + 1]))
                xt = x_tok[:, t, :]
                if t == 0:
                    dve.wait_ge(gain_in, 32 * (q + 1))
                link(ve.scalar_tensor_tensor(out=xt, in0=xt, scalar=mv[:, t, 0:1], in1=gain_of(q)[:, 0, :],
                                             op0=ALU.subtract, op1=ALU.mult))
                ve.scalar_tensor_tensor(out=xt, in0=xt, scalar=rstd[:, t:t + 1], in1=gain_of(q)[:, 1, :],
                                        op0=ALU.mult, op1=ALU.add).then_inc(norm_done, 1)

            def onehot_of(l, i, r):
                g = nth(l, i, r)
                wait(dve, idx_ps, g - 1)
                ve.tensor_tensor(onehot[:, r % 2, :, :], slot_no.unsqueeze(1).to_broadcast([P, T, CAP]),
                                 posm[:, :, bass.ds(count(i, r), 1)].to_broadcast([P, T, CAP]), ALU.is_equal
                                 ).then_inc(onehot_ok, 1)

            def indices(l, i, r):
                g = nth(l, i, r)
                dve.wait_ge(idx_ps, g + 1)
                wait(dve, t_ps, g - WAYS + 1)
                ve.tensor_scalar(token_idx[r % WAYS][0:CAP, :], ps[6][0:CAP, 0:1], float(LATE), None, ALU.add)
                ve.tensor_copy(slots[0:CAP, bass.ds(count(i, r) * 3, 2)], ps[6][0:CAP, 0:2])
                ve.tensor_reduce(slots[0:CAP, bass.ds(count(i, r) * 3 + 2, 1)], ps[6][0:CAP, 2:4], axis=AX.X,
                                 op=ALU.add).then_inc(idx_ok, 1)

            def product(l, i, r):
                g = nth(l, i, r)
                dve.wait_ge(silu_ok, g + 1)
                wait(dve, y_ps, g - 1)
                h = sil[:, r % 2, :]
                high, low = [v[:, r % 2, :, :].rearrange("p j n -> p (j n)") for v in (hT_high, hT_low)]
                ve.tensor_tensor(h, h, ps[r % 2][:, J * CAP:2 * J * CAP], ALU.mult).then_inc(h_step, 1)
                dve.wait_ge(h_step, 2 * g + 1)
                ve.tensor_copy(high, h).then_inc(h_step, 1)
                dve.wait_ge(h_step, 2 * g + 2)
                ve.tensor_tensor(low, h, high.bitcast(F32), ALU.subtract).then_inc(h_ok, 1)

            def split_down_low(l, i, r):
                place, _ = expert_unit(l, 0, r, 2)
                dve.wait_ge(down_high_ok, nth(l, i, r) + 1)
                ve.tensor_tensor(down_low[:, place, :], ring[:, place, :], down_high[:, r % 2, :].bitcast(F32),
                                 ALU.subtract).then_inc(down_low_ok, 1)

            def xgt_half(l, i, r):
                g = nth(l, i, r)
                dve.wait_ge(t_ps, g + 1)
                wait(dve, h_ps, g - 1)
                ve.tensor_copy(xgT[:, r % 2, 4:8, :],
                               ps[5][:, 0:4 * CAP].rearrange("p (c n) -> p c n", c=4)).then_inc(xgt_b, 1)

            def y_half(l, i, r):
                g, e, b = nth(l, i, r), count(i, r), r % WAYS
                dve.wait_ge(idx_ok, g + 1)
                wait(dve, scattered[b], uses(l, i, r) - 16)
                ve.tensor_scalar(row_idx[b][0:CAP, :], slots[0:CAP, bass.ds(e * 3 + 1, 1)], float(LATE), None, ALU.add)
                dve.wait_ge(y_ps, g + 1)
                ve.tensor_scalar(y_sb[0:CAP, b, HALF:D], ps[3][0:CAP, :], slots[0:CAP, bass.ds(e * 3 + 2, 1)], None,
                                 ALU.mult).then_inc(yb, 1)

            def route(l):
                s = L[l]
                dve.wait_ge(score_ok, l + 1)
                link(ve.tensor_tensor(biased, scores, rb[:, l, :].unsqueeze(1).to_broadcast([P, T, E]), ALU.add))
                for t in range(T):
                    for g in range(NG):
                        m = ve.max(top2[:, t * NG + g, :], biased[:, t, g * EG:(g + 1) * EG])
                link(m)
                link(ve.tensor_tensor(gscore.rearrange("p t g -> p (t g)"), top2[:, :, 0], top2[:, :, 1], ALU.add))
                other = gscore.unsqueeze(2).to_broadcast([P, T, NG, NG])
                own = gscore.unsqueeze(3).to_broadcast([P, T, NG, NG])
                ve.tensor_tensor(g_gt, other, own, ALU.is_gt)
                link(ve.tensor_tensor(g_eq, other, own, ALU.is_equal))
                link(ve.tensor_tensor(g_eq, g_eq, lower[:, :, :].unsqueeze(1).to_broadcast([P, T, NG, NG]), ALU.mult))
                link(ve.tensor_tensor(g_gt, g_gt, g_eq, ALU.add))
                link(ve.tensor_reduce(g_rank, g_gt, axis=AX.X, op=ALU.add))
                link(ve.tensor_scalar(g_sel, g_rank, TOPG - 0.5, None, ALU.is_lt))
                link(ve.tensor_scalar(g_pen, g_sel, -1.0, 1e30, ALU.add, ALU.mult))
                by_group = masked.rearrange("p t (g k) -> p t g k", g=NG)
                link(ve.tensor_tensor(by_group, biased.rearrange("p t (g k) -> p t g k", g=NG),
                                      g_sel.unsqueeze(3).to_broadcast([P, T, NG, EG]), ALU.mult))
                link(ve.tensor_tensor(by_group, by_group, g_pen.unsqueeze(3).to_broadcast([P, T, NG, EG]), ALU.add))
                for t in range(T):
                    m = ve.max(top8[:, t, :], masked[:, t, :])
                link(m)
                for t in range(T):
                    m = ve.match_replace(taken[:, t, :], top8[:, t, :], masked[:, t, :], -3e38)
                link(m)
                link(ve.tensor_tensor(chosen, taken, masked, ALU.not_equal))
                link(ve.tensor_tensor(scores, scores, chosen, ALU.mult))
                link(ve.tensor_reduce(gsum, scores, axis=AX.X, op=ALU.add))
                link(ve.reciprocal(grec, gsum))
                link(ve.tensor_scalar(grec, grec, ROUTED_SCALE, None, ALU.mult))
                columns = table[:, :, :].rearrange("p t (e k) -> p t e k", k=COLS)
                link(ve.tensor_tensor(scores, scores, grec.unsqueeze(2).to_broadcast([P, T, E]), ALU.mult))
                link(ve.tensor_copy(columns[:, :, :, 2], scores))
                ve.tensor_tensor(columns[:, :, :, 3], scores, columns[:, :, :, 2].bitcast(F32), ALU.subtract)
                m = ve.tensor_copy(columns[:, :, :, 0], tok_id[:, :].unsqueeze(2).to_broadcast([P, T, E]))
                m.then_inc(chosen_ok, 1)
                src, step = chosen, 1
                spare = [cum_a, cum_b]
                while step < E:
                    dst = spare[0]
                    ve.tensor_copy(dst[:, :, 0:step], src[:, :, 0:step])
                    link(ve.tensor_tensor(dst[:, :, step:], src[:, :, step:], src[:, :, 0:E - step], ALU.add))
                    src, step = dst, 2 * step
                    spare.reverse()
                dst = spare[0]
                link(ve.tensor_tensor(dst, src, chosen, ALU.subtract))
                link(ve.tensor_tensor(columns[:, :, :, 1], dst, tok_row[:, :].unsqueeze(2).to_broadcast([P, T, E]), ALU.add))

            def place_tokens(l):
                s = L[l]
                dve.wait_ge(pos_ps, l + 1)
                flat = posm.rearrange("p t e -> p (t e)")
                link(ve.scalar_tensor_tensor(out=flat, in0=ps[3][:, 0:T * E], scalar=1.0,
                                             in1=chosen.rearrange("p t e -> p (t e)"), op0=ALU.add, op1=ALU.mult))
                link(ve.tensor_scalar(flat, flat, -1.0, None, ALU.add))
                link(ve.reduce_max(most, ps[3][:, T * E:(T + 1) * E], axis=AX.X))
                ve.tensor_copy(most_i[:, :], most).then_inc(s["table_ok"], 1)
                ve.tensor_copy(counts_i[:, :], ps[3][:, T * E:(T + 1) * E]).then_inc(s["table_ok"], 1)

            dve.wait_ge(consts, 11)
            link(ve.reciprocal(edge, edge))
            for g, w in enumerate(WINDOWS):
                m = ve.tensor_scalar(edge[:, g, :], edge[:, g, :], 1.0 / w, float(w), ALU.max, ALU.mult)
            link(m)

            for l in range(DEPTH):
                s = L[l]
                if l == 0:
                    split_low(0)
                    turn(0)
                    split_low(1)

                    def y_low(jd):
                        dve.wait_ge(grp_hi, jd + 1)
                        ve.scalar_tensor_tensor(out=yT_low[:, jd, :], in0=ps[4 + jd % 2][:, :],
                                                scalar=scale_col[:, jd:jd + 1], in1=yT_high[:, jd, :].bitcast(F32),
                                                op0=ALU.mult, op1=ALU.subtract).then_inc(grp_sb, 1)

                    for j in range(K):
                        g = j // 2
                        dve.wait_ge(z_sb, j + 1)
                        z = z_pad[:, j % 2, :]
                        a, spare = z, [win_a, win_b]
                        for n in range(g + 1):
                            step, b = 1 << n, spare[n % 2]
                            link(ve.tensor_tensor(b[:, 16:], a[:, 16:], a[:, 16 - step:ZP - step], ALU.add))
                            a = b
                        link(ve.tensor_tensor(a[:, 16:32], a[:, 16:32], edge[:, g, :], ALU.mult))
                        m = ve.scalar_tensor_tensor(out=pooled[:, j, :], in0=a[:, 16:], scalar=1.0 / WINDOWS[g],
                                                    in1=z[:, 16:], op0=ALU.mult, op1=ALU.subtract)
                        m.then_inc(pooled_ok, 1)
                        dve.wait_ge(pooled_ok, j + 1)
                        if j % 2 == 1:
                            split_low(j // 2 + 2)
                            if j >= 3:
                                y_low(j - 3)
                                y_low(j - 2)
                    y_low(K - 2)
                    y_low(K - 1)
                    split_low(6)
                    split_low(7)
                else:
                    def add_bias(u, t):
                        dve.wait_ge(v_ps, v_no(max(u, 1), t) + 1)
                        ve.tensor_tensor(v_tok[:, t, u * 256:(u + 1) * 256], ps[t][:, u % 2 * 256:(u % 2 + 1) * 256],
                                         v_bias[:, u % 2, :], ALU.add).then_inc(v_add, 1)

                    dve.wait_ge(bias_in[0], 16)
                    dve.wait_ge(bias_in[1], 16)
                    for t in range(T):
                        if t == T - 1:
                            split_low(SPLITS[0] + 2)
                        add_bias(0, t)
                        add_bias(1, t)
                    split_low(SPLITS[0] + 3)
                    for u in range(2, 8):
                        dve.wait_ge(bias_in[u % 2], 16 * (u // 2 + 1))
                        for t in range(T):
                            add_bias(u, t)
                        split_low(SPLITS[0] + u + 2)
                    for t in range(T):
                        dve.wait_ge(v_sb, 7 * T + t + 1)
                        for h in range(4):
                            link(ve.bn_stats(stats[:, t, h, :], v_tok[:, t, h * 512:(h + 1) * 512]))
                        ve.bn_aggr(mv[:, t, :], stats[:, t, :, :].rearrange("p a b -> p (a b)")).then_inc(v_var, 1)
                    split_low(SPLITS[0] + 10)
                    for t in range(T):
                        dve.wait_ge(v_std, t + 1)
                        link(ve.reciprocal(rstd[:, t:t + 1], std[:, t:t + 1]))
                        ve.tensor_scalar(v_tok[:, t, :], v_tok[:, t, :], mv[:, t, 0:1], rstd[:, t:t + 1],
                                         ALU.subtract, ALU.mult).then_inc(v_ok, 1)
                    split_low(SPLITS[0] + 11)
                    dve.wait_ge(wsum_ok, 1)

                    def gate(j):
                        h = j * HEADS // KS
                        tail = v_bias[:, j % 2, 0:P]
                        link(ve.scalar_tensor_tensor(out=tail, in0=ws_sum[:, h, :], scalar=sgu_cols[:, 2, j:j + 1],
                                                     in1=bs_row[:, h, :], op0=ALU.mult, op1=ALU.add))
                        dve.wait_ge(sp_ps, j + 1)
                        flat = ps[6 + j % 2][:, :]
                        bank = flat.rearrange("p (t n) -> p t n", t=T)
                        link(ve.scalar_tensor_tensor(out=bank, in0=bank, scalar=sgu_cols[:, 1, j:j + 1],
                                                     in1=tail.unsqueeze(1).to_broadcast([P, T, P]),
                                                     op0=ALU.mult, op1=ALU.add))
                        dve.wait_ge(u_sb, j + 1)
                        link(ve.tensor_tensor(flat, gT[:, j, :], flat, ALU.mult))
                        link(ve.tensor_copy(gT_high[:, j, :], flat))
                        ve.tensor_tensor(gT_low[:, :, j * P:(j + 1) * P], bank,
                                         gT_high[:, j, :].bitcast(F32).rearrange("p (t n) -> p t n", t=T),
                                         ALU.subtract).then_inc(gated_ok, 1)

                    for w in range(2, 8):
                        gate(2 * w - LAG)
                        gate(2 * w - LAG + 1)
                        split_low(SPLITS[0] + 8 + w + 2)
                    for j in range(KS - LAG, KS):
                        gate(j)
                    for q in range(2, OUT_UNITS[1]):
                        split_low(SPLITS[0] + 16 + q)
                for t in range(T):
                    for h in range(2):
                        dve.wait_ge(s["mix_ps"], 2 * t + h + 1)
                        xt = x_tok[:, t, h * HALF:(h + 1) * HALF]
                        m = ve.scalar_tensor_tensor(out=xt, in0=xt, scalar=ALPHA, in1=ps[2 * t + h][:, :],
                                                    op0=ALU.mult, op1=ALU.add)
                        m.then_inc(s["mix_res"], 1)
                    dve.wait_ge(s["mix_res"], 2 * t + 2)
                    norm_stats(2 * l, t)
                    if t > 0:
                        norm_apply(2 * l, t - 1)
                norm_apply(2 * l, T - 1)
                route(l)
                for half in range(2):
                    if half == 1:
                        place_tokens(l)
                    dve.wait_ge(s["shg_ps"], 2 * half + 2)
                    dve.wait_ge(s["sh_sil_ok"], half + 1)
                    tokens = slice(half * SH, (half + 1) * SH)
                    ve.tensor_tensor(sh_hT[:, :, tokens], sh_sil[:, :, tokens],
                                     ps[5 + 2 * half][:, :].rearrange("p (j n) -> p j n", j=J), ALU.mult
                                     ).then_inc(s["sh_h_ok"], 1)
                dve.wait_ge(slots_ok, l + 1)
                def add_shared():
                    dve.wait_ge(s["x1_stored"], 16 * T)
                    for t in range(T):
                        for h in range(2):
                            dve.wait_ge(s["shy_ps"], 2 * t + h + 1)
                            xt = x_tok[:, t, h * HALF:(h + 1) * HALF]
                            m = ve.scalar_tensor_tensor(out=xt, in0=xt, scalar=ALPHA, in1=ps[2 * (t % 2) + h][:, :],
                                                        op0=ALU.mult, op1=ALU.add)
                            m.then_inc(s["base_ok"], 1)

                for i in range(-AHEAD, WAYS):
                    if i == -2:
                        add_shared()
                    onehot_of(l, 0, i + AHEAD)
                    if i >= -1:
                        split_down_low(l, 0, i + 1)
                    indices(l, 0, i + AHEAD)
                    if i >= -1:
                        product(l, 0, i + 1)
                    if i >= -2:
                        xgt_half(l, 0, i + 2)
                    if i >= 0:
                        y_half(l, 0, i)
                with dve.Fori(1, LAST_BODY) as body:
                    i = body * WAYS
                    for r in range(WAYS):
                        onehot_of(l, i, r + AHEAD)
                        split_down_low(l, i, r + 1)
                        indices(l, i, r + AHEAD)
                        product(l, i, r + 1)
                        xgt_half(l, i, r + 2)
                        y_half(l, i, r)
                for i in range(LAST_BODY * WAYS, E):
                    if i + AHEAD < E:
                        onehot_of(l, 0, i + AHEAD)
                    if i + 1 < E:
                        split_down_low(l, 0, i + 1)
                    if i + AHEAD < E:
                        indices(l, 0, i + AHEAD)
                    if i + 1 < E:
                        product(l, 0, i + 1)
                    if i + 2 < E:
                        xgt_half(l, 0, i + 2)
                    y_half(l, 0, i)
                n_most = dve.value_load(most_i[0:1, 0:1], min_val=0, max_val=S)
                with dve.If(n_most > CAP):
                    wait_scattered(dve, l)
                    dve.wait_ge(ya, E * (l + 1))
                    with dve.Fori(0, E) as e:
                        n_e = dve.value_load(counts_i[0:1, bass.ds(e, 1)], min_val=0, max_val=S)
                        with dve.If(n_e > CAP):
                            for p in range(PASSES - 1):
                                q = e * (PASSES - 1) + p
                                ve.scalar_tensor_tensor(
                                    out=onehot[:, 0, :, :], in0=posm[:, :, bass.ds(e, 1)].to_broadcast([P, T, CAP]),
                                    scalar=-float((p + 1) * CAP),
                                    in1=slot_no.unsqueeze(1).to_broadcast([P, T, CAP]),
                                    op0=ALU.add, op1=ALU.is_equal).then_inc(s["o_onehot"], 1)
                                dve.wait_ge(s["o_idx_ps"], q + 1)
                                ve.tensor_scalar(token_idx[0][0:CAP, :], ps[6][0:CAP, 0:1], float(LATE), None, ALU.add)
                                ve.tensor_scalar(row_idx[0][0:CAP, :], ps[6][0:CAP, 1:2], float(LATE), None, ALU.add)
                                ve.tensor_copy(slots[0:CAP, bass.ds(e * 3, 2)], ps[6][0:CAP, 0:2])
                                ve.tensor_reduce(slots[0:CAP, bass.ds(e * 3 + 2, 1)], ps[6][0:CAP, 2:4], axis=AX.X,
                                                 op=ALU.add).then_inc(s["o_idx"], 1)
                                dve.wait_ge(s["o_t"], q + 1)
                                ve.tensor_copy(xgT[:, 0, 4:8, :],
                                               ps[5][:, 0:4 * CAP].rearrange("p (c n) -> p c n", c=4)).then_inc(s["o_xgt_b"], 1)
                                dve.wait_ge(s["o_silu"], q + 1)
                                ve.tensor_tensor(hT[:, 0, :, :].rearrange("p j n -> p (j n)"), sil[:, 0, :],
                                                 ps[0][:, J * CAP:2 * J * CAP], ALU.mult).then_inc(s["o_hok"], 1)
                                dve.wait_ge(s["o_y"], q + 1)
                                dve.wait_ge(s["o_idx"], q + 1)
                                ve.tensor_scalar(y_sb[0:CAP, 0, HALF:D], ps[3][0:CAP, :],
                                                 slots[0:CAP, bass.ds(e * 3 + 2, 1)], None, ALU.mult).then_inc(s["o_yb"], 1)
                                dve.wait_ge(s["o_scattered"], q + 1)
                                dve.sem_inc(carrier, 1)
                        with dve.Else():
                            dve.sem_inc(s["o_onehot"], PASSES - 1)
                            dve.sem_inc(s["o_idx"], PASSES - 1)
                            dve.sem_inc(s["o_xgt_b"], PASSES - 1)
                            dve.sem_inc(s["o_hok"], PASSES - 1)
                            dve.sem_inc(s["o_yb"], PASSES - 1)
                        dve.nop()
                with dve.Else():
                    dve.nop()
                if l + 1 < DEPTH:
                    split_low(SPLITS[0])
                    split_low(SPLITS[0] + 1)
                dve.wait_ge(s["base_ok"], 2 * T)
                for t in range(T):
                    g = l * T + t
                    for k in range(2, ROWS):
                        dve.wait_ge(rows_in[k], 16 * (g + 2))
                        link(ve.tensor_tensor(x_tok[:, t, :], x_tok[:, t, :], rows[k][:, 0:D], ALU.add))
                        ve.tensor_tensor(x_tok[:, t, :], x_tok[:, t, :], rows[k][:, D:2 * D], ALU.add
                                         ).then_inc(rows_used, 1)
                        dve.wait_ge(rows_used, 2 * g + k - 1)
                        if k == 3 and t > 0 and l + 1 < DEPTH:
                            turn(2 * l + 2, [t - 1])
                    dve.wait_ge(rows_summed, 2 * g + 2)
                    for h in range(2):
                        half = x_tok[:, t, h * HALF:(h + 1) * HALF]
                        m = ve.tensor_tensor(half, half, ps[4 + h][:, :], ALU.add)
                    link(m)
                    norm_stats(2 * l + 1, t)
                    norm_apply(2 * l + 1, t)
                if l + 1 < DEPTH:
                    turn(2 * l + 2, [T - 1])

        @block.tensor
        def _(pe):
            te = nc.tensor

            def turn(q, tiles=range(T), turned=None):
                apart = 2 if q == 0 else 1
                for t in tiles:
                    if q > 0:
                        pe.wait_ge(norm_done, (q - 1) * T + t + 1)
                    else:
                        pe.wait_ge(rows_in[t], 16)
                    if t >= apart:
                        pe.wait_ge(xT_a, q * T + t - apart + 1)
                        pe.wait_ge(xT_b, q * T + t - apart + 1)
                    for c in range(K):
                        m = te.transpose(ps[turn_bank(q, t) + c // 4][:, (c % 4) * P:(c % 4 + 1) * P],
                                         x_tok[:, t, bass.ds(c, P, step=K)], ident[:, :])
                    m.then_inc(x_turned, 1)
                    if turned and t > tiles[0]:
                        turned(t - 1)
                pe.wait_ge(xT_a, q * T + tiles[-1] + 1)
                pe.wait_ge(xT_b, q * T + tiles[-1] + 1)
                if turned:
                    turned(tiles[-1])

            def split_unit(l, m):
                n = split_no[l, m]
                pe.wait_ge(low_ok, n + 1)
                return w_high[n % 2], w_low[n % 2]

            def product3(out, left, right, first, last):
                te.matmul(out, left[0], right[0], start=first, stop=False)
                te.matmul(out, left[0], right[1], start=False, stop=False)
                return te.matmul(out, left[1], right[0], start=False, stop=last)

            def by_column(halves, at):
                return [w[:, :].rearrange("p (c f) -> p c f", c=K)[:, at[0], at[1]] for w in halves]

            def x_part(c, tokens):
                return xT_high[:, c, tokens], xT_low[:, c, tokens]

            def shared_unit(l, k):
                place, there = expert_unit(l, 0, -1, k)
                pe.wait_ge(landed[place], there)
                return place

            def token_list(l, i, r):
                g = nth(l, i, r)
                pe.wait_ge(onehot_ok, g + 1)
                wait(pe, idx_ok, g)
                for t in range(T):
                    m = te.matmul(ps[6][0:CAP, 0:COLS], onehot[:, r % 2, t, :],
                                  table[:, t, bass.ds(count(i, r) * COLS, COLS)],
                                  start=(t == 0), stop=(t == T - 1))
                m.then_inc(idx_ps, 1)

            def turn_rows(l, i, r):
                g, b = nth(l, i, r), r % WAYS
                pe.wait_ge(gathered[b], uses(l, i, r))
                wait(pe, xgt_a, g)
                wait(pe, xgt_b, g)
                for c in range(K):
                    m = te.transpose(ps[4 + c // 4][:, (c % 4) * CAP:(c % 4 + 1) * CAP],
                                     xg[0:CAP, b, bass.ds(c, P, step=K)], ident[0:CAP, 0:CAP])
                m.then_inc(t_ps, 1)

            def gate_up(l, i, r):
                g = nth(l, i, r)
                pe.wait_ge(xgt_a, g + 1)
                pe.wait_ge(xgt_b, g + 1)
                wait(pe, h_ok, g - 1)
                for k in range(2):
                    place, there = expert_unit(l, i, r, k)
                    pe.wait_ge(landed[place], there)
                    w = gate_up_view(place)
                    for j in range(J):
                        for c in range(K):
                            m = te.matmul(ps[r % 2][:, (k * J + j) * CAP:(k * J + j + 1) * CAP],
                                          w[:, c, bass.ds(j, P, step=J)], xgT[:, r % 2, c, :],
                                          start=(c == 0), stop=(c == K - 1))
                m.then_inc(h_ps, 1)

            def down(l, i, r):
                g = nth(l, i, r)
                place, _ = expert_unit(l, 0, r, 2)
                pe.wait_ge(down_low_ok, g + 1)
                pe.wait_ge(h_ok, g + 1)
                wait(pe, ya, g)
                wait(pe, yb, g)
                for h in range(2):
                    for j in range(J):
                        cols = slice(j * D + h * HALF, j * D + (h + 1) * HALF)
                        m = product3(ps[2 + h][0:CAP, :], (hT_high[:, r % 2, j, :], hT_low[:, r % 2, j, :]),
                                     (down_high[:, r % 2, cols], down_low[:, place, cols]), j == 0, j == J - 1)
                m.then_inc(y_ps, 1)

            def sum_rows(l, t):
                g = l * T + t
                if t > 0:
                    pe.wait_ge(norm_var, (2 * l + 1) * T + t)
                for k in range(2):
                    pe.wait_ge(rows_in[k], 16 * (g + 2))
                    for pick in range(2):
                        for h in range(2):
                            m = te.matmul(ps[4 + h][:, :], ident[:, :],
                                          rows[k][:, pick * D + h * HALF:pick * D + (h + 1) * HALF],
                                          start=(k == 0 and pick == 0), stop=(k == 1 and pick == 1))
                    m.then_inc(rows_summed, 1)

            def v_product(u, t):
                w = split_unit(1, u)
                if u >= 2:
                    pe.wait_ge(v_add, v_no(u - 1, t) + 1)
                for c in range(K):
                    m = product3(ps[t][:, u % 2 * 256:(u % 2 + 1) * 256], x_part(c, slice(t * P, (t + 1) * P)),
                                 by_column(w, (c, slice(0, 256))), c == 0, c == K - 1)
                m.then_inc(v_ps, 1)

            pe.wait_ge(consts, 11)
            for l in range(DEPTH):
                s = L[l]
                if l == 0:
                    turn(0)

                    def group_product(g):
                        place, there = raw_at[0, GROUP_UNIT]
                        if g == 0:
                            pe.wait_ge(landed[place], there)
                        w = ring[:, place, :].rearrange("p (g k d) -> p g k d", g=4, k=2)
                        pe.wait_ge(pooled_ok, 2 * g + 2)
                        for jd in range(2):
                            if 2 * g + jd >= 2:
                                pe.wait_ge(grp_sb, 2 * g + jd - 1)
                            for k in range(2):
                                m = te.matmul(ps[4 + jd][:, :], w[:, g, k, jd * P:(jd + 1) * P], pooled[:, 2 * g + k, :],
                                              start=(k == 0), stop=(k == 1))
                            m.then_inc(grp_ps, 1)

                    for j in range(K):
                        if j % 2 == 0:
                            w = split_unit(0, j // 2)
                        if j >= 4:
                            pe.wait_ge(z_sb, j - 3)
                        for c in range(K):
                            m = product3(ps[j % 4][:, :], by_column(w, (c, slice((j % 2) * P, (j % 2 + 1) * P))),
                                         x_part(c, slice(0, S)), c == 0, c == K - 1)
                        m.then_inc(z_ps, 1)
                        if j % 2 == 1 and j >= 3:
                            group_product((j - 3) // 2)
                    group_product(3)
                    pe.wait_ge(z_sb, K)
                else:
                    sum_rows(0, 0)
                    for t in range(T):
                        if t + 1 < T:
                            sum_rows(0, t + 1)
                        turn(2, [t])
                        if t == T - 1:
                            pe.wait_ge(ws_cut, 1)
                            for h in range(HEADS):
                                m = te.transpose(ps[4][:, h * P:(h + 1) * P], ws_raw[:, h, :], ident[:, :])
                            m.then_inc(ws_ps, 1)
                        v_product(0, t)
                        v_product(1, t)
                    pe.wait_ge(ws_ok, 1)
                    te.matmul(ps[5][:, :], ones[:, :], wsT[:, :, :].rearrange("p h n -> p (h n)"),
                              start=True, stop=True).then_inc(wsum_ps, 1)
                    for u in range(2, 8):
                        for t in range(T):
                            v_product(u, t)
                    pe.wait_ge(wsum_ok, 1)

                    def spatial(j):
                        h = j * HEADS // KS
                        if j == 0:
                            pe.wait_ge(v_ok, T)
                            pe.wait_ge(wsum_ok, 1)
                        if j >= 2:
                            pe.wait_ge(gated_ok, j - 1)
                        for t in range(T):
                            m = te.matmul(ps[6 + j % 2][:, t * P:(t + 1) * P], v_tok[:, t, j * P:(j + 1) * P],
                                          wsT[:, h, :], start=True, stop=True)
                        m.then_inc(sp_ps, 1)

                    for j in range(KS):
                        if j % 2 == 0:
                            w = split_unit(1, 8 + j // 2)
                        if j >= 2:
                            pe.wait_ge(u_sb, j - 1)
                        for c in range(K):
                            m = product3(ps[4 + j % 2][:, :], by_column(w, (c, slice((j % 2) * P, (j % 2 + 1) * P))),
                                         x_part(c, slice(0, S)), c == 0, c == K - 1)
                        m.then_inc(u_ps, 1)
                        if j >= LAG:
                            spatial(j - LAG)
                    for j in range(KS - LAG, KS):
                        spatial(j)
                def mixed(k, t):
                    if l == 0:
                        return yT_high[:, k, t * P:(t + 1) * P], yT_low[:, k, t * P:(t + 1) * P]
                    return gT_high[:, k, t * P:(t + 1) * P], gT_low[:, t, k * P:(k + 1) * P]

                def out_product(q, w, t, h):
                    for kk in range(2):
                        k = 2 * q + kk
                        cols = slice(kk * D + h * HALF, kk * D + (h + 1) * HALF)
                        m = product3(ps[2 * t + h][:, :], mixed(k, t), (w[0][:, cols], w[1][:, cols]),
                                     k == 0, k == 2 * OUT_UNITS[l] - 1)
                    return m

                first = RAW_UNITS[l] - OUT_UNITS[l]
                first_two = [(q, split_unit(l, first + q)) for q in range(2)]
                for tiles in ((0, 1), (2, 3)):
                    for q, w in first_two:
                        if tiles[0] == 0:
                            pe.wait_ge(grp_sb if l == 0 else gated_ok, 2 * q + 2)
                        elif q == 0:
                            pe.wait_ge(grp_sb if l == 0 else gated_ok, K if l == 0 else KS)
                        for t in tiles:
                            for h in range(2):
                                m = out_product(q, w, t, h)
                        if tiles[0] == 2 and q < OUT_UNITS[l] - 2:
                            m.then_inc(out_used, 1)
                for q in range(2, OUT_UNITS[l] - 2):
                    w = split_unit(l, first + q)
                    for t in range(T):
                        for h in range(2):
                            m = out_product(q, w, t, h)
                    m.then_inc(out_used, 1)
                q = OUT_UNITS[l] - 2
                before_last = split_unit(l, first + q)
                for t in range(2):
                    for h in range(2):
                        out_product(q, before_last, t, h)
                last = split_unit(l, first + q + 1)
                for t in range(T):
                    for h in range(2):
                        if t >= 2:
                            out_product(q, before_last, t, h)
                        out_product(q + 1, last, t, h).then_inc(s["mix_ps"], 1)
                if l == 0:
                    pe.wait_ge(small, 16 * (5 + DEPTH))

                def router(t):
                    if t == 0:
                        pe.wait_ge(s["mix_res"], 3)
                    for c in range(K):
                        m = te.matmul(ps[2][:, t * E:(t + 1) * E], xT[:, c, t * P:(t + 1) * P], wr[:, l, c, :],
                                      start=(c == 0), stop=(c == K - 1))
                    m.then_inc(logit_ps, 1)

                def shared_gate_up(half, k):
                    pe.wait_ge(s["mix_res"], 6 + 2 * half)
                    w = gate_up_view(shared_unit(l, k))
                    for j in range(J):
                        for c in range(K):
                            m = te.matmul(ps[4 + 2 * half + k][:, j * SH:(j + 1) * SH], w[:, c, bass.ds(j, P, step=J)],
                                          xT[:, c, half * SH:(half + 1) * SH], start=(c == 0), stop=(c == K - 1))
                    m.then_inc(s["shg_ps"], 1)

                turn(2 * l + 1, range(T // 2), router)
                shared_gate_up(0, 0)
                turn(2 * l + 1, range(T // 2, T), router)
                shared_gate_up(0, 1)
                shared_gate_up(1, 0)
                pe.wait_ge(score_ok, l + 1)
                pe.wait_ge(chosen_ok, l + 1)
                for t in range(T):
                    for b in range(t + 1):
                        te.matmul(ps[3][:, t * E:(t + 1) * E], before[:, :] if b == t else ones[:, :], chosen[:, b, :],
                                  start=(b == 0), stop=(b == t))
                for b in range(T):
                    m = te.matmul(ps[3][:, T * E:(T + 1) * E], ones[:, :], chosen[:, b, :], start=(b == 0), stop=(b == T - 1))
                m.then_inc(pos_ps, 1)
                shared_gate_up(1, 1)

                def shared_down():
                    w = down_view(shared_unit(l, 2))
                    pe.wait_ge(s["sh_h_ok"], 2)
                    for t in range(T):
                        for h in range(2):
                            n = 2 * t + h
                            if n >= 4:
                                pe.wait_ge(s["base_ok"], n - 3)
                            for j in range(J):
                                m = te.matmul(ps[2 * (t % 2) + h][:, :], sh_hT[:, j, t * P:(t + 1) * P],
                                              w[:, j, h * HALF:(h + 1) * HALF], start=(j == 0), stop=(j == J - 1))
                            m.then_inc(s["shy_ps"], 1)
                    pe.wait_ge(s["base_ok"], 2 * T)

                pe.wait_ge(s["sh_sil_ok"], 2)
                pe.wait_ge(s["table_ok"], 2)
                for i in range(-AHEAD, WAYS):
                    if i == -2:
                        shared_down()
                    if i >= -1:
                        gate_up(l, 0, i + 1)
                    token_list(l, 0, i + AHEAD)
                    if i >= -2:
                        turn_rows(l, 0, i + 2)
                    if i >= 0:
                        down(l, 0, i)
                with pe.Fori(1, LAST_BODY) as body:
                    i = body * WAYS
                    for r in range(WAYS):
                        gate_up(l, i, r + 1)
                        token_list(l, i, r + AHEAD)
                        turn_rows(l, i, r + 2)
                        down(l, i, r)
                for i in range(LAST_BODY * WAYS, E):
                    if i + 1 < E:
                        gate_up(l, 0, i + 1)
                    if i + AHEAD < E:
                        token_list(l, 0, i + AHEAD)
                    if i + 2 < E:
                        turn_rows(l, 0, i + 2)
                    down(l, 0, i)
                n_most = pe.value_load(most_i[0:1, 0:1], min_val=0, max_val=S)
                with pe.If(n_most > CAP):
                    with pe.Fori(0, E) as e:
                        n_e = pe.value_load(counts_i[0:1, bass.ds(e, 1)], min_val=0, max_val=S)
                        with pe.If(n_e > CAP):
                            pe.wait_ge(s["o_w"], e * 48 + 48)
                            for p in range(PASSES - 1):
                                q = e * (PASSES - 1) + p
                                pe.wait_ge(s["o_onehot"], q + 1)
                                for t in range(T):
                                    m = te.matmul(ps[6][0:CAP, 0:COLS], onehot[:, 0, t, :],
                                                  table[:, t, bass.ds(e * COLS, COLS)],
                                                  start=(t == 0), stop=(t == T - 1))
                                m.then_inc(s["o_idx_ps"], 1)
                                pe.wait_ge(s["o_gathered"], q + 1)
                                for c in range(K):
                                    m = te.transpose(ps[4 + c // 4][:, (c % 4) * CAP:(c % 4 + 1) * CAP],
                                                     xg[0:CAP, 0, bass.ds(c, P, step=K)], ident[0:CAP, 0:CAP])
                                m.then_inc(s["o_t"], 1)
                                pe.wait_ge(s["o_xgt_a"], q + 1)
                                pe.wait_ge(s["o_xgt_b"], q + 1)
                                for k in range(2):
                                    w = gate_up_view(k)
                                    for j in range(J):
                                        for c in range(K):
                                            m = te.matmul(ps[0][:, (k * J + j) * CAP:(k * J + j + 1) * CAP],
                                                          w[:, c, bass.ds(j, P, step=J)], xgT[:, 0, c, :],
                                                          start=(c == 0), stop=(c == K - 1))
                                m.then_inc(s["o_h"], 1)
                                pe.wait_ge(s["o_hok"], q + 1)
                                for h in range(2):
                                    for j in range(J):
                                        m = te.matmul(ps[2 + h][0:CAP, :], hT[:, 0, j, :],
                                                      down_view(2)[:, j, h * HALF:(h + 1) * HALF],
                                                      start=(j == 0), stop=(j == J - 1))
                                m.then_inc(s["o_y"], 1)
                                pe.wait_ge(s["o_ya"], q + 1)
                                pe.wait_ge(s["o_yb"], q + 1)
                        with pe.Else():
                            pe.sem_inc(s["o_idx_ps"], PASSES - 1)
                            pe.sem_inc(s["o_t"], PASSES - 1)
                            pe.sem_inc(s["o_h"], PASSES - 1)
                            pe.sem_inc(s["o_y"], PASSES - 1)
                        pe.nop()
                with pe.Else():
                    pe.nop()
            for t in range(T):
                sum_rows(DEPTH - 1, t)


_INS = ["x", "pool_w_in", "pool_w_grp", "pool_scale", "pool_w_out", "sgu_w_in", "sgu_b_in", "sgu_ln_g", "sgu_ln_b",
        "sgu_w_s", "sgu_b_s", "sgu_w_out", "ln_mix_g", "ln_mix_b", "moe_w_router", "moe_router_bias", "moe_w_gate",
        "moe_w_up", "moe_w_down", "moe_sh_gate", "moe_sh_up", "moe_sh_down", "ln_ffn_g", "ln_ffn_b"]


def kernel(**inputs):
    import numpy as _np
    import concourse.bacc as _bacc
    from concourse import mybir as _mybir
    from concourse.bass_utils import run_bass_kernel_spmd as _run

    nc = _bacc.Bacc("TRN2", target_bir_lowering=False, num_devices=1)
    arrays, args = {}, []
    for name in _INS:
        a = _np.ascontiguousarray(inputs[name])
        arrays[f"in_{name}_dram"] = a
        args.append(nc.dram_tensor(f"in_{name}_dram", a.shape, _mybir.dt.from_np(a.dtype), kind="ExternalInput").ap())
    args.append(nc.dram_tensor("out_0_dram", tuple(inputs["x"].shape), _mybir.dt.float32, kind="ExternalOutput").ap())
    hybrid_trunk(nc, *args)
    r = _run(nc, [arrays], core_ids=[0])
    return r.results[0]["out_0_dram"]
```
